# Optimizing a Trainium2 kernel written in Bass

```python
import math
import jax, jax.numpy as jnp
from jax import lax
import numpy as np

D_MODEL = 2048
BATCH = 1
SEQ = 256
DEPTH = 1

MIX_WIDTH = D_MODEL
DN_WIDTH = MIX_WIDTH // 2
DN_HEAD_DIM = 128
DN_HEADS = DN_WIDTH // DN_HEAD_DIM
POOL_WIDTH = MIX_WIDTH - DN_WIDTH
POOL_WINDOWS = (2, 4, 8, 16)
POOL_GROUPS = len(POOL_WINDOWS)
POOL_GROUP_DIM = POOL_WIDTH // POOL_GROUPS
SHORT_CONV = 4
CHUNK = 64
D_FF = 5632
FFN_CONV = 3
EPS = 1e-6
IN_WIDTH = 4 * DN_WIDTH + 2 * DN_HEADS + POOL_WIDTH

kernel_name = "hybrid_gdn_pool_convffn"

def rms_norm(x, w):
    xf = x.astype(jnp.float32)
    y = xf * lax.rsqrt(jnp.mean(xf * xf, axis=-1, keepdims=True) + EPS)
    return (y * w.astype(jnp.float32)).astype(x.dtype)

def l2norm(x):
    return x * lax.rsqrt(jnp.sum(x * x, axis=-1, keepdims=True) + EPS)

def causal_dwconv(x, w, b=None):
    K = w.shape[0]
    S = x.shape[1]
    xp = jnp.pad(x, ((0, 0), (K - 1, 0), (0, 0)))
    y = w[0] * xp[:, :S]
    for j in range(1, K):
        y = y + w[j] * xp[:, j:j + S]
    if b is not None:
        y = y + b
    return y

def chunk_gated_delta_rule(q, k, v, beta, g):
    B, H, S, dk = q.shape
    dv = v.shape[-1]
    n = S // CHUNK
    q = q * (dk ** -0.5)
    rs = lambda t: t.reshape(B, H, n, CHUNK, *t.shape[3:])
    q, k, v, beta, g = rs(q), rs(k), rs(v), rs(beta), rs(g)
    g = jnp.cumsum(g, axis=-1)
    k_beta = k * beta[..., None]
    v_beta = v * beta[..., None]
    idx = jnp.arange(CHUNK)
    causal = idx[:, None] >= idx[None, :]
    strict = idx[:, None] > idx[None, :]
    decay = jnp.exp(jnp.where(causal, g[..., :, None] - g[..., None, :], -jnp.inf))
    L = jnp.where(strict, jnp.einsum('bhncd,bhnmd->bhncm', k_beta, k) * decay, 0.0)
    eye = jnp.eye(CHUNK, dtype=q.dtype)
    rhs = jnp.concatenate([v_beta, k_beta * jnp.exp(g)[..., None]], axis=-1)
    sol = lax.linalg.triangular_solve(L + eye, rhs, left_side=True, lower=True, unit_diagonal=True)
    value, k_cum = sol[..., :dv], sol[..., dv:]
    qk = jnp.einsum('bhncd,bhnmd->bhncm', q, k) * decay
    q_g = q * jnp.exp(g)[..., None]
    k_tail = k * jnp.exp(g[..., -1:] - g)[..., None]
    g_last = jnp.exp(g[..., -1])
    xs = tuple(jnp.moveaxis(t, 2, 0) for t in (qk, q_g, k_tail, value, k_cum, g_last))

    def step(state, inp):
        qk_c, qg_c, kt_c, v_c, kc_c, gl_c = inp
        v_new = v_c - jnp.einsum('bhcd,bhde->bhce', kc_c, state)
        o = jnp.einsum('bhcd,bhde->bhce', qg_c, state) + jnp.einsum('bhcm,bhme->bhce', qk_c, v_new)
        state = state * gl_c[..., None, None] + jnp.einsum('bhcd,bhce->bhde', kt_c, v_new)
        return state, o

    state0 = jnp.zeros((B, H, dk, dv), dtype=q.dtype)
    _, o = lax.scan(step, state0, xs)
    return jnp.moveaxis(o, 0, 2).reshape(B, H, S, dv)

def multiscale_pool(u, pool_w, pool_scale):
    B, S, _ = u.shape
    uf = u.astype(jnp.float32).reshape(B, S, POOL_GROUPS, POOL_GROUP_DIM)
    csum = jnp.cumsum(uf, axis=1)
    pos = jnp.arange(1, S + 1, dtype=jnp.float32)[None, :, None]
    pooled = []
    for gi, w in enumerate(POOL_WINDOWS):
        c = csum[:, :, gi]
        prev = jnp.pad(c, ((0, 0), (w, 0), (0, 0)))[:, :S]
        pooled.append((c - prev) / jnp.minimum(pos, float(w)) - uf[:, :, gi])
    d = jnp.stack(pooled, axis=2)
    y = jnp.einsum('bsgc,gcd->bsgd', d, pool_w.astype(jnp.float32)).reshape(B, S, POOL_WIDTH)
    return (y * pool_scale.astype(jnp.float32)).astype(u.dtype)

def hybrid_layer(x, norm1_w, w_in, conv_qkv_w, a_log, dt_bias, out_norm_w, pool_w, pool_scale,
                 w_out, norm2_w, w_up, conv_ffn_w, conv_ffn_b, w_down):
    B, S, _ = x.shape
    f32 = jnp.float32
    h = rms_norm(x, norm1_w)
    proj = h @ w_in
    cuts = [3 * DN_WIDTH, 4 * DN_WIDTH, 4 * DN_WIDTH + DN_HEADS, 4 * DN_WIDTH + 2 * DN_HEADS]
    qkv, z, beta_logit, a_logit, u = jnp.split(proj, cuts, axis=-1)
    qkv = jax.nn.silu(causal_dwconv(qkv, conv_qkv_w))
    q, k, v = jnp.split(qkv, 3, axis=-1)
    to_heads = lambda t: t.reshape(B, S, DN_HEADS, DN_HEAD_DIM).transpose(0, 2, 1, 3).astype(f32)
    q = l2norm(to_heads(q))
    k = l2norm(to_heads(k))
    v = to_heads(v)
    beta = jax.nn.sigmoid(beta_logit.astype(f32)).transpose(0, 2, 1)
    g = (-jnp.exp(a_log.astype(f32)) *
         jax.nn.softplus(a_logit.astype(f32) + dt_bias.astype(f32))).transpose(0, 2, 1)
    o = chunk_gated_delta_rule(q, k, v, beta, g).transpose(0, 2, 1, 3)
    o = rms_norm(o, out_norm_w) * jax.nn.silu(z.reshape(B, S, DN_HEADS, DN_HEAD_DIM).astype(f32))
    o_dn = o.reshape(B, S, DN_WIDTH).astype(x.dtype)
    o_pool = multiscale_pool(u, pool_w, pool_scale)
    x = x + jnp.concatenate([o_dn, o_pool], axis=-1) @ w_out
    h = rms_norm(x, norm2_w)
    up = causal_dwconv(h @ w_up, conv_ffn_w, conv_ffn_b)
    gate, val = jnp.split(up, 2, axis=-1)
    x = x + (jax.nn.silu(gate) * val) @ w_down
    return x

def setup_inputs(seed: int = 0) -> dict:
    key = jax.random.key(seed)
    ks = jax.random.split(key, 17)
    nrm = lambda k, shape, s: jax.random.normal(k, shape, dtype=jnp.float32) * s
    L = DEPTH
    dt = jnp.exp(jax.random.uniform(ks[5], (L, DN_HEADS), minval=math.log(1e-3), maxval=math.log(0.1)))
    return {
        "x": nrm(ks[0], (BATCH, SEQ, D_MODEL), 1.0),
        "norm1_w": 1.0 + nrm(ks[1], (L, D_MODEL), 0.02),
        "w_in": nrm(ks[2], (L, D_MODEL, IN_WIDTH), D_MODEL ** -0.5),
        "conv_qkv_w": nrm(ks[3], (L, SHORT_CONV, 3 * DN_WIDTH), SHORT_CONV ** -0.5),
        "a_log": jnp.log(jax.random.uniform(ks[4], (L, DN_HEADS), minval=1.0, maxval=16.0)),
        "dt_bias": dt + jnp.log(-jnp.expm1(-dt)),
        "out_norm_w": 1.0 + nrm(ks[6], (L, DN_HEAD_DIM), 0.02),
        "pool_w": nrm(ks[7], (L, POOL_GROUPS, POOL_GROUP_DIM, POOL_GROUP_DIM), POOL_GROUP_DIM ** -0.5),
        "pool_scale": 1.0 + nrm(ks[8], (L, POOL_WIDTH), 0.02),
        "w_out": nrm(ks[9], (L, MIX_WIDTH, D_MODEL), MIX_WIDTH ** -0.5),
        "norm2_w": 1.0 + nrm(ks[10], (L, D_MODEL), 0.02),
        "w_up": nrm(ks[11], (L, D_MODEL, 2 * D_FF), D_MODEL ** -0.5),
        "conv_ffn_w": nrm(ks[12], (L, FFN_CONV, 2 * D_FF), FFN_CONV ** -0.5),
        "conv_ffn_b": nrm(ks[13], (L, 2 * D_FF), 0.01),
        "w_down": nrm(ks[14], (L, D_FF, D_MODEL), D_FF ** -0.5),
        "final_norm_w": 1.0 + nrm(ks[15], (D_MODEL,), 0.02),
    }

def reference(x, norm1_w, w_in, conv_qkv_w, a_log, dt_bias, out_norm_w, pool_w, pool_scale,
              w_out, norm2_w, w_up, conv_ffn_w, conv_ffn_b, w_down, final_norm_w):
    for l in range(DEPTH):
        x = hybrid_layer(x, norm1_w[l], w_in[l], conv_qkv_w[l], a_log[l], dt_bias[l], out_norm_w[l],
                         pool_w[l], pool_scale[l], w_out[l], norm2_w[l], w_up[l], conv_ffn_w[l],
                         conv_ffn_b[l], w_down[l])
    return rms_norm(x, final_norm_w)


_drawn_inputs = setup_inputs


def setup_inputs(seed=0):
    import zlib

    import numpy as np

    out = dict(_drawn_inputs(seed))
    spreads = {}
    factors = {'norm1_w': 3.317,
     'out_norm_w': 24.589,
     'pool_scale': 20.493,
     'norm2_w': 13.902,
     'conv_ffn_b': 27.463,
     'final_norm_w': 7.525}
    for name, (base, spread) in spreads.items():
        noise = np.random.default_rng([zlib.crc32(name.encode()), seed]).standard_normal(out[name].shape)
        drawn = base * np.exp(spread * noise) if base else spread * noise
        out[name] = __import__('jax').numpy.asarray(drawn.astype(out[name].dtype))
    for name, factor in factors.items():
        out[name] = (out[name] * factor).astype(out[name].dtype)
    return out
```

```python
from contextlib import ExitStack

import concourse.bass as bass
from concourse import mybir

F32 = mybir.dt.float32
F32R = mybir.dt.float32r
ALU = mybir.AluOpType
ACT = mybir.ActivationFunctionType

P = 128
EPS = 1e-6
PAD = 3
LEVELS = (2, 4, 8, 16, 32)
WINDOWS = (2, 4, 8, 16)

C_NM = 0
C_CAUSAL = C_NM + 6 * P
C_STRICT = C_CAUSAL + 64
C_EYE2 = C_STRICT + 64
C_TRI = C_EYE2 + 64
C_HALF = C_TRI + P
C_BLOCK = C_HALF + 64
C_COUNT = C_HALF + 2 * P
C_IDENT = C_COUNT + 64
C_ONES = C_IDENT + P
C_ALL = C_ONES + P


def constants():
    import numpy as np

    c = np.zeros((P, C_ALL), np.float32)
    i = np.arange(P)
    for n, s in enumerate(LEVELS + (1,)):
        row, col = i[:, None] // s, i[None, :] // s
        m = ((row % 2 == 1) & (col == row - 1)).astype(np.float32)
        c[:, C_NM + n * P:C_NM + (n + 1) * P] = -(m.T if s == 1 else m)
    m, t = (i % 64)[:, None], np.arange(64)[None, :]
    c[:, C_CAUSAL:C_CAUSAL + 64] = t >= m
    c[:, C_STRICT:C_STRICT + 64] = t > m
    c[:, C_EYE2:C_EYE2 + 64] = t == m
    same = (i[:, None] // 64) == (i[None, :] // 64)
    c[:, C_TRI:C_TRI + P] = same & (i[:, None] <= i[None, :])
    c[:64, C_HALF:C_HALF + P] = 1.0
    c[64:, C_HALF + P:C_HALF + 2 * P] = 1.0
    for g, w in enumerate(WINDOWS):
        c[:, C_COUNT + 16 * g:C_COUNT + 16 * g + 16] = 1.0 / np.minimum(np.arange(16) + 1.0, w)
    c[:, C_IDENT:C_IDENT + P] = np.eye(P)
    c[:, C_ONES:C_ONES + P] = 1.0
    return c


def hybrid_layer(nc, x, norm1_w, w_in, conv_qkv_w, a_log, dt_bias, out_norm_w, pool_w, pool_scale,
                 w_out, norm2_w, w_up, conv_ffn_w, conv_ffn_b, w_down, final_norm_w, table, out):
    SEQ, D = x.shape[1], x.shape[2]
    HEADS = a_log.shape[1]
    DN = HEADS * P
    FF = w_down.shape[1]
    KD = D // P
    KF = FF // P
    TT = SEQ // P
    PAIRS, CHUNKS = HEADS // 2, SEQ // 64
    J = PAIRS * CHUNKS
    QSCALE = float(P) ** -0.5
    assert (SEQ, D, HEADS, FF) == (256, 2048, 8, 5632)

    OUT_B, UP_B, DOWN_B = 10, 14, 36
    DOWN_U, DOWN_T = 4 * DOWN_B, 4 * DOWN_B
    DOWN_STEPS = KF // 2
    IN_COLS = [512 * i for i in range(6)] + [4 * DN + 2 * HEADS + 512 * i for i in range(2)] \
        + [3 * DN + 512 * i for i in range(2)]

    w_in2, w_out2, w_up2, w_down2 = w_in[0], w_out[0], w_up[0], w_down[0]
    x2, out2 = x[0], out[0]

    ctx = ExitStack()
    phase_a = ExitStack()
    with ctx:
        def sb(name, shape, dt=F32, where=ctx):
            return where.enter_context(nc.sbuf_tensor(name, shape, dt))

        def sem(name):
            return ctx.enter_context(nc.semaphore(name))

        ps = ctx.enter_context(nc.psum_tensor("ps", [P, 8, 512], F32))

        raw = sb("raw", [P, 2, 2048])
        w_hi = sb("w_hi", [P, 2, 2048], F32R)
        w_lo = sb("w_lo", [P, 2, 2048], F32R)
        act = sb("act", [P, KD, 512], F32R)
        xT = sb("xT", [P, KD, SEQ])
        cols = sb("cols", [P, 505])
        ident = sb("ident", [P, P])
        ones = sb("ones", [P, P])
        yb = sb("yb", [P, 4, SEQ])
        ub = sb("ub", [P, 4, PAD + SEQ])
        eps = sb("eps", [P, 1])
        sumsq = sb("sumsq", [P, SEQ])
        rstd = sb("rstd", [P, SEQ])

        cst = sb("cst", [P, C_IDENT], F32, phase_a)
        qkv = sb("qkv", [P, 3, HEADS, SEQ], F32, phase_a)
        zT = sb("zT", [P, HEADS, SEQ], F32, phase_a)
        uT = sb("uT", [P, HEADS, SEQ], F32, phase_a)
        scr = sb("scr", [P, 4, 2048], F32, phase_a)
        dt_s = sb("dt_s", [P, 1024], F32, phase_a)
        qkt = sb("qkt", [P, J, 64], F32, phase_a)
        qg = sb("qg", [P, HEADS, SEQ], F32, phase_a)
        vnew = sb("vnew", [P, PAIRS, 2, P], F32, phase_a)
        gates = sb("gates", [P, 16 * 14 + 16], F32, phase_a)
        sq_acc = sb("sq_acc", [P, 2], F32, phase_a)
        phase_a.close()
        fact = sb("fact", [P, KF, 512], F32R)
        gb = sb("gb", [P, 4, SEQ])

        xtok = scr[:, 0:2, :]
        h32 = scr[:, 0:2, :].rearrange("p a (t n) -> p (a t) n", n=SEQ)
        staged = scr[:, 2, 0:768].rearrange("p (i n) -> p i n", n=P)
        w_log = scr[:, 2, 1024:1280].rearrange("p (k n) -> p k n", n=16)
        lg = scr[0:16, 3, 0:256]
        lgd = scr[0:16, 3, 512:1024].rearrange("p (c d n) -> p c d n", c=CHUNKS, d=2)
        sqx = scr[:, 3, :]
        LT, Tm, TT_, X_ = (scr[:, i, :].rearrange("p (j n) -> p j n", n=P) for i in range(4))
        vb, kg, ktail = LT, Tm, X_
        sq_q = scr[:, 3, :].rearrange("p (h n) -> p h n", n=SEQ)
        sq_k = scr[:, 2, :].rearrange("p (h n) -> p h n", n=SEQ)
        diag_g = scr[:, 1, 0:1024].rearrange("p (j n) -> p j n", n=64)
        diag_b = scr[:, 1, 1024:2048].rearrange("p (j n) -> p j n", n=64)
        bdec = scr[:, 3, 0:1024].rearrange("p (j n) -> p j n", n=64)
        decay = dt_s[:, :].rearrange("p (j n) -> p j n", n=64)
        S = dt_s[:, :].rearrange("p (h n) -> p h n", n=P)
        win = dt_s[:, :].rearrange("p (b k n) -> p b k n", b=2, k=2)
        qT, kT = qkv[:, 0], qkv[:, 1]
        by_problem = qkv[:, :, :, :].rearrange("p k h n -> p k (h n)").rearrange(
            "p k (j c h n) -> p (k j) c h n", j=PAIRS, c=CHUNKS, h=2)
        qg_problem = qg[:, :, :].rearrange("p h n -> p (h n)").rearrange("p (j c h n) -> p j c h n", j=PAIRS, c=CHUNKS, h=2)
        W = qkv[:, 1].rearrange("p h n -> p (h n)").rearrange("p (j h c) -> p j h c", j=J, h=2)
        oT = qkv[:, 2]
        pw = zT[:, :, :].rearrange("p h n -> p (h n)").rearrange("p (g k n) -> p g k n", g=4, k=2)
        rdiag = scr[:, 3, 1024:1280].rearrange("p (a n) -> p a n", n=P)
        sq_o = scr[:, 1, :].rearrange("p (h n) -> p h n", n=SEQ)

        def gcol(i, n=16):
            return gates[:, 16 * i:16 * i + n]

        g_in, g_beta, g_g = gates[:, 0:32], gcol(2), gcol(3)
        g_t1, g_t2, g_sum, g_eg, g_kt, g_nbeg = gcol(4), gcol(5), gcol(6, 64), gcol(10), gcol(11), gcol(12)
        g_cum, g_tot = g_sum[:, 0:16], g_sum[:, 16:32]
        g_last = g_sum[:, 32:64].rearrange("p (h j) -> p h j", h=2)
        al8, dt8 = gates[:, 208:216], gates[:, 216:224]
        g_t3 = gates[:, 224:240]

        N1, N2, NF, PSC, ONW, CB, CW, QW = 0, 16, 32, 48, 56, 57, 145, 409

        def col(n):
            return cols[:, n:n + 1]

        def over(ap, n):
            return ap.unsqueeze(2).to_broadcast([ap.shape[0], ap.shape[1], n])

        def times(ap, n):
            return ap.unsqueeze(1).to_broadcast([ap.shape[0], n, ap.shape[1]])

        def js(p):
            return slice(CHUNKS * p, CHUNKS * p + CHUNKS)

        def hs(p):
            return slice(2 * p, 2 * p + 2)

        def pbank(p, n):
            return ps[:, 4 + p, :].rearrange("p (c n) -> p c n", n=n)

        HALF = (slice(0, 64), slice(64, 128))

        raw_loaded = [sem("raw_loaded0"), sem("raw_loaded1")]
        hi_split, lo_split = sem("hi_split"), sem("lo_split")
        slabs = sem("slabs")
        copied = sem("copied")
        evacuated = sem("evacuated")
        tapped = sem("tapped")
        tap1, tap2 = sem("tap1"), sem("tap2")
        convolved = sem("convolved")
        silu_done = sem("silu_done")
        product = sem("product")
        product_hi, product_lo = sem("product_hi"), sem("product_lo")
        residual = sem("residual")
        squared, summed = sem("squared"), sem("summed")
        normed = sem("normed")
        act_hi, act_lo = sem("act_hi"), sem("act_lo")
        rstd_ready, sums_ready, root_ready = sem("rstd_ready"), sem("sums_ready"), sem("root_ready")
        x_loaded, cst_loaded, par_loaded, pool_w_loaded = sem("x_loaded"), sem("cst_loaded"), sem("par_loaded"), sem("pool_w_loaded")
        x_turned, x_copied_act, x_copied_dve = sem("x_turned"), sem("x_copied_act"), sem("x_copied_dve")
        par_turned, cols_ready = sem("par_turned"), sem("cols_ready")
        x_squared, x_root, x_rstd, x_diag, rstd_rows = sem("x_squared"), sem("x_root"), sem("x_rstd"), sem("x_diag"), sem("rstd_rows")
        filled = sem("filled")
        zeroed = sem("zeroed")
        logits, logits_copied, logits_twice, logits_turned = sem("logits"), sem("logits_copied"), sem("logits_twice"), sem("logits_turned")
        gate_chain, minus_abs, gate_exp, gate_log, log_decay = sem("gate_chain"), sem("minus_abs"), sem("gate_exp"), sem("gate_log"), sem("log_decay")
        decay_sums, decay_summed, decay_exps, gates_ready = sem("decay_sums"), sem("decay_summed"), sem("decay_exps"), sem("gates_ready")
        diag_ready = sem("diag_ready")
        q_sq, k_sq, q_sum, k_sum, q_root, k_root, q_normed, k_normed = (
            sem(n) for n in ("q_sq", "k_sq", "q_sum", "k_sum", "q_root", "k_root", "q_normed", "k_normed"))
        row_g, row_exp, decay_diff, decay_exp, decay_ready, qg_ready = (
            sem(n) for n in ("row_g", "row_exp", "decay_diff", "decay_exp", "decay_ready", "qg_ready"))
        decay_bound = sem("decay_bound")
        row_b, beta_row, beta_decay, kq, lt_ready, qkt_ready = (
            sem(n) for n in ("row_b", "beta_row", "beta_decay", "kq", "lt_ready", "qkt_ready"))
        tt_part, tt_first, t_turned, t_first = sem("tt_part"), sem("tt_first"), sem("t_turned"), sem("t_first")
        lx, lx_copied, tlt, tlt_masked, t_joined, t_back, tt_copied = (
            sem(n) for n in ("lx", "lx_copied", "tlt", "tlt_masked", "t_joined", "t_back", "tt_copied"))
        k_tok, k_scaled, v_tok, v_scaled, w_prod, w_copied = (
            sem(n) for n in ("k_tok", "k_scaled", "v_tok", "v_scaled", "w_prod", "w_copied"))
        v_prod, v_copied, so_prod, s_ready, o_copied = (sem(n) for n in ("v_prod", "v_copied", "so_prod", "s_ready", "o_copied"))
        q_inv, k_inv, o_inv = sem("q_inv"), sem("k_inv"), sem("o_inv")
        o_sq, o_sum, o_root, o_normed, o_gated, o_hi, o_lo = (
            sem(n) for n in ("o_sq", "o_sum", "o_root", "o_normed", "o_gated", "o_hi", "o_lo"))
        pool_chain, pooled, pool_prod, pool_out, pool_hi, pool_lo = (
            sem(n) for n in ("pool_chain", "pooled", "pool_prod", "pool_out", "pool_hi", "pool_lo"))
        y_normed, y_turned, stored = sem("y_normed"), sem("y_turned"), sem("stored")
        y_copied = [sem("y_copied_act"), sem("y_copied_dve")]

        def halves(t, slot, h, k=4):
            n = 1024 // k
            return t[:, slot, :].rearrange("p (k n) -> p k n", k=k)[:, :, n * h:n * h + n]

        block = ctx.enter_context(nc.Block())

        @block.sync
        def _(sp):
            for t in range(TT):
                sp.dma_start(xtok[:, t, :], x2[P * t:P * t + P, :]).then_inc(x_loaded, 16)

            def load(u, slot, src, k, first=False):
                if not first:
                    sp.wait_ge(lo_split, 2 * (u - 1))
                sp.dma_start(raw[:, slot, :].rearrange("p (k n) -> p k n", k=k),
                             src.rearrange("(k p) n -> p k n", p=P)).then_inc(raw_loaded[slot], 16)

            def load_block(b, w, c0, order=(0, 1, 2, 3), first=False):
                for i, r in enumerate(order):
                    load(4 * b + i, i % 2, w[512 * r:512 * r + 512, bass.ds(c0, 512)], 4, first and i < 2)

            load_block(0, w_in2, IN_COLS[0], first=True)
            with sp.Fori(1, 6) as i:
                load_block(i, w_in2, i * 512)
            for b in range(6, 10):
                load_block(b, w_in2, IN_COLS[b])
            load_block(OUT_B, w_out2, 0, (2, 3, 0, 1))
            with sp.Fori(1, 4) as i:
                load_block(OUT_B + i, w_out2, i * 512)
            with sp.Fori(0, 11) as i:
                load_block(UP_B + 2 * i, w_up2, i * 512)
                load_block(UP_B + 1 + 2 * i, w_up2, i * 512 + FF)
            for half in range(2):
                with sp.Fori(0, DOWN_STEPS // 2) as i:
                    for n in range(2):
                        load(DOWN_U + DOWN_STEPS * half + 2 * i + n, n,
                             w_down2[bass.ds(i * 512 + 256 * n, 256), 1024 * half:1024 * half + 1024], 2)
            for n in range(8):
                sp.wait_ge(y_copied[n % 2], n // 2 + 1)
                sp.dma_start(out2[P * (n // 4):P * (n // 4) + P, 512 * (n % 4):512 * (n % 4) + 512],
                             raw[:, n // 4, 512 * (n % 4):512 * (n % 4) + 512]).then_inc(stored, 16)
            sp.wait_ge(stored, 16 * 8)

        @block.gpsimd
        def _(pool):
            pool.memset(eps[:, :], EPS)
            pool.memset(vnew[:, :, :, :], 0.0)
            pool.memset(ub[:, :, 0:PAD], 0.0).then_inc(filled, 1)

            pool.wait_ge(cst_loaded, 48)
            pool.wait_ge(logits, 1)
            pool.wait_ge(act_hi, 4)
            pool.wait_ge(act_lo, 4)
            pool.memset(LT, 0.0).then_inc(zeroed, 1)
            pool.wait_ge(decay_summed, 1)
            pool.tensor_tensor(diag_g, times(cst[:, C_EYE2:C_EYE2 + 64], J), over(g_cum, 64), ALU.mult).then_inc(diag_ready, 1)
            pool.tensor_tensor(diag_b, times(cst[:, C_EYE2:C_EYE2 + 64], J), over(g_beta, 64), ALU.mult).then_inc(diag_ready, 1)
            pool.wait_ge(q_normed, PAIRS)
            pool.wait_ge(row_exp, PAIRS)
            pool.tensor_tensor(qg[:, :, :], qg[:, :, :], qT, ALU.mult).then_inc(qg_ready, 1)

            n = 0
            pool.wait_ge(qkt_ready, PAIRS)
            for g, w in enumerate(WINDOWS):
                u = uT[:, 2 * g:2 * g + 2, :]
                pool.wait_ge(evacuated, 24 + 2 * g + 2)
                src, b, s = u, 0, 1
                while s < w:
                    dst = win[:, b]
                    pool.tensor_tensor(dst[:, :, s:], src[:, :, s:], src[:, :, :SEQ - s], ALU.add)
                    pool.tensor_copy(dst[:, :, 0:s], src[:, :, 0:s]).then_inc(pool_chain, 1)
                    n += 1
                    pool.wait_ge(pool_chain, n)
                    src, b, s = dst, 1 - b, 2 * s
                mean = win[:, b]
                pool.tensor_tensor(mean[:, :, 0:16], src[:, :, 0:16],
                                   times(cst[:, C_COUNT + 16 * g:C_COUNT + 16 * g + 16], 2), ALU.mult)
                pool.tensor_scalar(mean[:, :, 16:], src[:, :, 16:], 1.0 / w, None, ALU.mult).then_inc(pool_chain, 1)
                n += 1
                pool.wait_ge(pool_chain, n)
                pool.tensor_tensor(u, mean, u, ALU.subtract).then_inc(pooled, 1)
                pool.wait_ge(pooled, g + 1)

        @block.scalar
        def _(act_e):
            a = act_e

            def copy(o, i):
                return a.activation(o, i, ACT.Copy)

            a.dma_start(ident[:, :], table[:, C_IDENT:C_IDENT + P]).then_inc(cst_loaded, 16)
            a.dma_start(ones[:, :], table[:, C_ONES:C_ONES + P]).then_inc(cst_loaded, 16)
            a.dma_start(cst[:, :], table[:, 0:C_IDENT]).then_inc(cst_loaded, 16)
            for tile, r, v, k in [(0, N1, norm1_w[0], 16), (0, N2, norm2_w[0], 16), (0, NF, final_norm_w, 16),
                                  (0, PSC, pool_scale[0], 8), (0, ONW, out_norm_w[0], 1), (1, 0, conv_ffn_b[0], 88)]:
                a.dma_start(staged[r:r + k, tile, :], v.rearrange("(t p) -> t p", p=P)).then_inc(par_loaded, 16)
            for t in range(3):
                a.dma_start(staged[0:88, 2 + t, :], conv_ffn_w[0, t, :].rearrange("(t p) -> t p", p=P)).then_inc(par_loaded, 16)
            a.dma_start(staged[0:96, 5, :], conv_qkv_w[0].rearrange("j (t p) -> (j t) p", p=P)).then_inc(par_loaded, 16)
            a.dma_start(w_log, w_in2[:, 4 * DN:4 * DN + 2 * HEADS].rearrange("(k p) n -> p k n", p=P)).then_inc(par_loaded, 16)
            a.dma_start(al8, a_log[0:1, :].to_broadcast([P, 8])).then_inc(par_loaded, 16)
            a.dma_start(dt8, dt_bias[0:1, :].to_broadcast([P, 8])).then_inc(par_loaded, 16)
            a.dma_start(pw, pool_w[0].rearrange("g (k p) n -> p g k n", p=P)).then_inc(pool_w_loaded, 16)

            def hi_half(u, use, slot, h, k=4):
                if h == 0:
                    a.wait_ge(raw_loaded[slot], 16 * (use + 1))
                if isinstance(u, int) and u in (DOWN_U, DOWN_U + 1):
                    a.wait_ge(slabs, 4 * (u - 2) + 4)
                elif not (isinstance(u, int) and u < 2):
                    a.wait_ge(slabs, 4 * (u - 2) + 2 * (h + 1))
                copy(halves(w_hi, slot, h, k), halves(raw, slot, h, k)).then_inc(hi_split, 1)

            def hi(b, i, k=4):
                for h in range(2):
                    hi_half(4 * b + i, 2 * b + i // 2, i % 2, h, k)

            def post_copy(t, slab, free=None, n=4, bank=0, step=1):
                for f in range(n):
                    a.wait_ge(slabs, slab + f // step + 1)
                    if free is not None:
                        a.wait_ge(free[0], free[1] + f)
                    copy(yb[:, f, :], ps[:, bank + f, 256:512]).then_inc(copied, 1)

            def post_tap(t, weight, bias):
                for f in range(4):
                    a.wait_ge(evacuated, t + f + 1)
                    a.activation(yb[:, f, :], ub[:, f, PAD:], ACT.Identity, scale=cols[:, bass.ds(weight + f, 1)],
                                 bias=0.0 if bias is None else cols[:, bass.ds(bias + f, 1)]).then_inc(tapped, 1)

            def post_square(t, n):
                for f in range(4):
                    a.wait_ge(residual, n + f + 1)
                    a.activation(yb[:, f, :], xT[:, bass.ds(t + f, 1), :].rearrange("p a n -> p (a n)"), ACT.Square).then_inc(squared, 1)

            def split_hi(group, g, n):
                a.wait_ge(normed, n + 4 * g + 4)
                copy(act[:, 4 * g:4 * g + 4, 0:SEQ], group).then_inc(act_hi, 1)

            a.wait_ge(x_loaded, 32)
            for t in range(TT):
                if t:
                    a.wait_ge(x_squared, t)
                a.activation(sqx, xtok[:, t, :], ACT.Square, accum_out=sq_acc[:, t:t + 1]).then_inc(x_squared, 1)
            a.wait_ge(x_squared, 2)
            a.wait_ge(filled, 1)
            a.activation(sq_acc[:, :], sq_acc[:, :], ACT.Sqrt, scale=1.0 / D, bias=eps[:, 0:1]).then_inc(x_root, 1)
            for i in range(0, 8, 2):
                a.wait_ge(x_turned, i + 1)
                copy(xT[:, 2 * i:2 * i + 2, :], ps[:, i, :].rearrange("p (t n) -> p t n", n=SEQ)).then_inc(x_copied_act, 1)
            for g in range(4):
                split_hi(h32[:, 4 * g:4 * g + 4, :], g, 0)
            hi(0, 0)
            hi(0, 1)
            a.wait_ge(logits, 1)
            copy(lg, ps[0:16, 4, 0:SEQ]).then_inc(logits_copied, 1)
            a.wait_ge(logits_copied, 1)
            for d in range(2):
                last = copy(lgd[:, :, d, :], lg.rearrange("p (c n) -> p c n", n=64))
            last.then_inc(logits_twice, 1)
            hi(0, 2)
            hi(0, 3)

            def gates_act():
                a.wait_ge(par_loaded, 16 * 13)
                a.activation(al8, al8, ACT.Exp).then_inc(gate_exp, 1)
                a.wait_ge(minus_abs, 1)
                a.activation(g_t1, g_in[:, 0:16], ACT.Exp, scale=-1.0).then_inc(gate_exp, 1)
                a.activation(g_t2, g_t2, ACT.Exp).then_inc(gate_exp, 1)
                a.wait_ge(gate_exp, 3)
                a.activation(g_t2, g_t2, ACT.Ln, bias=1.0).then_inc(gate_log, 1)

            def qkv_silu(pair, f):
                a.activation(by_problem[:, bass.ds(pair, 1), :, f % 2, :].rearrange("p a c n -> p (a c) n"),
                             yb[:, f, :].rearrange("p (c n) -> p c n", n=64), ACT.Silu).then_inc(silu_done, 1)

            def act_qkv_block(i, gates=False):
                hi(i, 0)
                post_copy(4 * i - 4, 16 * i - 4)
                hi(i, 1)
                post_tap(4 * i - 4, QW + 72 + 4 * i - 4, None)
                if gates:
                    gates_act()
                hi(i, 2)
                for f in range(4):
                    a.wait_ge(convolved, 4 * i - 4 + f + 1)
                    qkv_silu(2 * i - 2 + f // 2, f)
                hi(i, 3)

            act_qkv_block(1, gates=True)
            with a.Fori(2, 6) as i:
                act_qkv_block(i)

            post_copy(20, 92)
            a.wait_ge(decay_summed, 1)
            a.activation(g_eg, g_cum, ACT.Exp).then_inc(decay_exps, 1)
            a.activation(g_kt, g_kt, ACT.Exp).then_inc(decay_exps, 1)
            a.activation(g_sum[:, 32:64], g_sum[:, 32:64], ACT.Exp).then_inc(decay_exps, 1)
            post_tap(20, QW + 72 + 20, None)
            for f in range(4):
                a.wait_ge(convolved, 20 + f + 1)
                qkv_silu(10 + f // 2, f)
            a.wait_ge(silu_done, 16)
            for p in range(PAIRS):
                a.activation(sq_q[:, hs(p), :], qT[:, hs(p), :], ACT.Square).then_inc(q_sq, 1)
            for p in range(PAIRS):
                a.activation(sq_k[:, hs(p), :], kT[:, hs(p), :], ACT.Square).then_inc(k_sq, 1)

            def slot_act(s):
                for p in range(PAIRS):
                    if s == 0:
                        a.wait_ge(q_sum, p + 1)
                        a.activation(sq_q[:, hs(p), :], pbank(p, SEQ), ACT.Sqrt, bias=eps[:, 0:1]).then_inc(q_root, 1)
                    elif s == 1:
                        a.wait_ge(row_g, p + 1)
                        a.wait_ge(decay_bound, p + 1)
                        a.activation(qg_problem[:, p].rearrange("p c h n -> p h c n"),
                                     ps[:, 4 + p, :].rearrange("p (h c n) -> p h c n", h=2, n=64), ACT.Exp).then_inc(row_exp, 1)
                        a.activation(decay[:, js(p), :], decay[:, js(p), :], ACT.Exp).then_inc(decay_exp, 1)
                    elif s == 4:
                        a.wait_ge(t_turned, p + 1)
                        copy(Tm[:, js(p), :], pbank(p, P)).then_inc(t_first, 1)
                    elif 5 <= s < 20 and (s - 5) % 3 == 0:
                        n = PAIRS * ((s - 5) // 3) + p
                        a.wait_ge(lx, n + 1)
                        copy(X_[:, js(p), :], pbank(p, P)).then_inc(lx_copied, 1)
                    elif 5 <= s < 20 and (s - 5) % 3 == 2:
                        n = PAIRS * ((s - 5) // 3) + p
                        a.wait_ge(t_back, n + 1)
                        copy(TT_[:, js(p), :], pbank(p, P)).then_inc(tt_copied, 1)
                    elif s == 22:
                        a.wait_ge(w_prod, p + 1)
                        copy(W[:, js(p)].rearrange("p j h c -> p (j h c)"), ps[:, 4 + p, :]).then_inc(w_copied, 1)
                    elif s == 23:
                        for f in range(2):
                            a.wait_ge(pool_prod, p + 1)
                            a.activation(uT[:, 2 * p + f, :], ps[:, 4 + p, SEQ * f:SEQ * f + SEQ], ACT.Identity,
                                         scale=cols[:, PSC + 2 * p + f:PSC + 2 * p + f + 1]).then_inc(pool_out, 1)
                    elif s >= 24 and s % 2 == 0:
                        a.wait_ge(v_prod, PAIRS * ((s - 24) // 2) + p + 1)
                        for h in range(2):
                            last = copy(vnew[HALF[h], p, h, :], ps[HALF[h], 4 + p, 0:P])
                        last.then_inc(v_copied, 1)
                    elif s >= 24:
                        c = (s - 24) // 2
                        a.wait_ge(so_prod, PAIRS * c + p + 1)
                        if c < CHUNKS - 1:
                            a.wait_ge(s_ready, PAIRS * c + p + 1)
                        copy(oT[:, hs(p), 64 * c:64 * c + 64],
                             ps[:, 4 + p, P:2 * P].rearrange("p (h n) -> p h n", h=2)).then_inc(o_copied, 1)
                if s == 0:
                    for p in range(PAIRS):
                        a.wait_ge(k_sum, p + 1)
                        a.activation(sq_k[:, hs(p), :], pbank(p, SEQ), ACT.Sqrt, bias=eps[:, 0:1]).then_inc(k_root, 1)

            def z_silu(n):
                for f in range(4):
                    a.wait_ge(evacuated, 32 + n + f + 1)
                    a.activation(zT[:, n + f, :], ub[:, f, PAD:], ACT.Silu).then_inc(silu_done, 1)

            def late_half(c):
                hi_half(24 + c // 2, 12 + c // 4, (c // 2) % 2, c % 2)

            late_half(0)
            late_half(1)
            for s in range(32):
                if s in (8, 16, 24):
                    post_copy(24 + s // 2 - 4, 92 + 2 * s)
                slot_act(s)
                if s == 25:
                    a.wait_ge(pool_prod, 4)
                    z_silu(0)
                late_half(s + 2)

            post_copy(36, 156)
            a.wait_ge(pool_out, 8)
            for g in range(2):
                copy(act[:, 8 + 4 * g:12 + 4 * g, 0:SEQ], uT[:, 4 * g:4 * g + 4, :]).then_inc(pool_hi, 1)
            for p in range(PAIRS):
                a.wait_ge(o_copied, PAIRS * 3 + p + 1)
                a.activation(sq_o[:, hs(p), :], oT[:, hs(p), :], ACT.Square).then_inc(o_sq, 1)
            hi(10, 1)
            z_silu(4)
            for p in range(PAIRS):
                a.wait_ge(o_sum, p + 1)
                a.activation(sq_o[:, hs(p), :], pbank(p, SEQ), ACT.Sqrt, scale=1.0 / P, bias=eps[:, 0:1]).then_inc(o_root, 1)
            for p in range(PAIRS):
                a.wait_ge(o_gated, p + 1)
                copy(act[:, hs(p), 0:SEQ], oT[:, hs(p), :]).then_inc(o_hi, 1)
            hi(10, 2)
            hi(10, 3)

            def act_out_block(b, i, first=False):
                hi(b, 0)
                post_copy(4 * b - 4, 16 * b - 4, None if first else (summed, 4 * i - 7))
                hi(b, 1)
                hi(b, 2)
                post_square(4 * i - 4, 4 * i - 4)
                hi(b, 3)

            act_out_block(11, 1, first=True)
            with a.Fori(2, 4) as i:
                act_out_block(i + 10, i)
            post_copy(52, 220, (summed, 9))
            post_square(12, 12)

            def root_act(n):
                a.wait_ge(sums_ready, n)
                a.activation(rstd[:, :], ps[:, 4, 0:SEQ], ACT.Sqrt, scale=1.0 / D, bias=eps[:, 0:1]).then_inc(root_ready, 1)

            root_act(1)
            for g in range(4):
                split_hi((yb, gb)[g % 2][:, :, :], g, 16)

            def act_up_block(b, i, prev, first=False):
                hi(b, 0)
                if prev is not None:
                    free = (product_lo, 4 * i - 3) if prev == "gate" and not first else None
                    post_copy(4 * b - 4, 16 * b - 4, free)
                hi(b, 1)
                if prev is not None:
                    t = 4 * i + (44 if prev == "value" else 0)
                    post_tap(4 * b - 4, CW + 176 + t, CB + t)
                hi(b, 2)
                if prev == "gate":
                    for f in range(4):
                        a.wait_ge(convolved, 24 + 8 * i + f + 1)
                        if not first:
                            a.wait_ge(product, 4 * i - 3 + f)
                        a.activation(gb[:, f, :], yb[:, f, :], ACT.Silu).then_inc(silu_done, 1)
                hi(b, 3)
                if prev == "value":
                    product_split_hi(i)

            def product_split_hi(i):
                for f in range(4):
                    a.wait_ge(product, 4 * i + f + 1)
                    copy(fact[:, bass.ds(4 * i + f, 1), 0:SEQ], yb[:, f:f + 1, :]).then_inc(product_hi, 1)

            act_up_block(UP_B, 0, None)
            act_up_block(UP_B + 1, 0, "gate", first=True)
            with a.Fori(0, 10) as i:
                act_up_block(UP_B + 2 + 2 * i, i, "value")
                act_up_block(UP_B + 3 + 2 * i, i + 1, "gate")

            def down_pair(half, i):
                for n in range(2):
                    for h in range(2):
                        hi_half(DOWN_U + DOWN_STEPS * half + 2 * i + n, (DOWN_U + DOWN_STEPS * half) // 2 + i, n, h, 2)

            def down_posts(half, free0):
                t, slab = DOWN_T + 8 * half, 4 * (DOWN_U + DOWN_STEPS * (half + 1)) - 4
                post_copy(t, slab, free0, bank=0, step=2)
                post_square(8 * half, 16 + 8 * half)
                post_copy(t + 4, slab + 2, (summed, 16 + 8 * half + 1), bank=4, step=2)
                post_square(8 * half + 4, 16 + 8 * half + 4)

            def pair_and_posts_0():
                hi_half(DOWN_U, DOWN_U // 2, 0, 0, 2)
                hi_half(DOWN_U, DOWN_U // 2, 0, 1, 2)
                post_copy(4 * DOWN_B - 4, 16 * DOWN_B - 4)
                hi_half(DOWN_U + 1, DOWN_U // 2, 1, 0, 2)
                hi_half(DOWN_U + 1, DOWN_U // 2, 1, 1, 2)
                post_tap(4 * DOWN_B - 4, CW + 176 + 84, CB + 84)
                down_pair(0, 1)
                product_split_hi(10)

            pair_and_posts_0()
            with a.Fori(2, DOWN_STEPS // 2) as i:
                down_pair(0, i)
            down_pair(1, 0)
            down_posts(0, (product_lo, 41))
            with a.Fori(1, DOWN_STEPS // 2) as i:
                down_pair(1, i)
            down_posts(1, (summed, 16 + 5))
            root_act(2)
            for n in range(0, 8, 2):
                a.wait_ge(y_turned, n + 1)
                copy(raw[:, n // 4, 512 * (n % 4):512 * (n % 4) + 512], ps[:, n, :]).then_inc(y_copied[0], 1)

        @block.vector
        def _(v):
            def lo_half(u2, slot, h, k=4):
                v.wait_ge(hi_split, u2 + 1)
                v.tensor_tensor(halves(w_lo, slot, h, k), halves(raw, slot, h, k),
                                halves(w_hi, slot, h, k).bitcast(F32), ALU.subtract).then_inc(lo_split, 1)

            def lo(b, i, k=4):
                for h in range(2):
                    lo_half(8 * b + 2 * i + h, i % 2, h, k)

            def post_add(t, used=None, bank=0):
                for f in range(4):
                    v.wait_ge(copied, t + f + 1)
                    if used is not None:
                        v.wait_ge(used[0], used[1] + f)
                    v.tensor_tensor(ub[:, f, PAD:], ps[:, bank + f, 0:256], yb[:, f, :], ALU.add).then_inc(evacuated, 1)

            def tap(f, back, weight, done, n):
                v.scalar_tensor_tensor(out=yb[:, f, :], in0=ub[:, f, PAD - back:PAD - back + SEQ],
                                       scalar=cols[:, bass.ds(weight + f, 1)], in1=yb[:, f, :],
                                       op0=ALU.mult, op1=ALU.add).then_inc(done, 1)

            def conv_qkv(t):
                for f in range(4):
                    v.wait_ge(tapped, t + f + 1)
                    tap(f, 1, QW + 48 + t, tap1, t)
                for f in range(4):
                    v.wait_ge(tap1, t + f + 1)
                    tap(f, 2, QW + 24 + t, tap2, t)
                for f in range(4):
                    v.wait_ge(tap2, t + f + 1)
                    tap(f, 3, QW + t, convolved, t)

            def conv_ffn(n, t):
                for f in range(4):
                    v.wait_ge(tapped, 24 + n + f + 1)
                    tap(f, 1, CW + 88 + t, tap1, t)
                for f in range(4):
                    v.wait_ge(tap1, 24 + n + f + 1)
                    tap(f, 2, CW + t, convolved, t)

            def post_residual(t, n, evac):
                for f in range(4):
                    v.wait_ge(evacuated, evac + f + 1)
                    x_t = xT[:, bass.ds(t + f, 1), :]
                    v.tensor_tensor(x_t, x_t, ub[:, f:f + 1, PAD:], ALU.add).then_inc(residual, 1)

            def post_sum(n, first=False):
                for f in range(4):
                    v.wait_ge(squared, n + f + 1)
                    if first and f == 0:
                        v.tensor_copy(sumsq[:, :], yb[:, f, :]).then_inc(summed, 1)
                    else:
                        v.wait_ge(summed, n + f)
                        v.tensor_tensor(sumsq[:, :], sumsq[:, :], yb[:, f, :], ALU.add).then_inc(summed, 1)

            def split_lo(group, g, n):
                v.wait_ge(act_hi, n + g + 1)
                v.tensor_tensor(act[:, 4 * g:4 * g + 4, SEQ:], group, act[:, 4 * g:4 * g + 4, 0:SEQ].bitcast(F32),
                                ALU.subtract).then_inc(act_lo, 1)

            for i in range(1, 8, 2):
                v.wait_ge(x_turned, i + 1)
                v.tensor_copy(xT[:, 2 * i:2 * i + 2, :], ps[:, i, :].rearrange("p (t n) -> p t n", n=SEQ)).then_inc(x_copied_dve, 1)
            v.wait_ge(x_root, 1)
            v.reciprocal(sq_acc[:, :], sq_acc[:, :]).then_inc(x_rstd, 1)
            v.wait_ge(x_rstd, 1)
            v.wait_ge(cst_loaded, 48)
            for t in range(TT):
                v.tensor_scalar(rdiag[:, t, :], ident[:, :], sq_acc[:, t:t + 1], None, ALU.mult).then_inc(x_diag, 1)
            v.wait_ge(par_turned, 1)
            v.tensor_copy(cols[:, :], ps[:, 0, 0:505]).then_inc(cols_ready, 1)
            v.wait_ge(cols_ready, 1)
            v.wait_ge(rstd_rows, 1)
            v.wait_ge(x_turned, 8)
            v.wait_ge(x_squared, 2)
            v.wait_ge(x_copied_act, 4)
            v.wait_ge(x_copied_dve, 4)
            for t in range(KD):
                v.scalar_tensor_tensor(out=h32[:, t, :], in0=xT[:, t, :], scalar=cols[:, N1 + t:N1 + t + 1],
                                       in1=ps[:, 1, 0:SEQ], op0=ALU.mult, op1=ALU.mult).then_inc(normed, 1)
            for g in range(4):
                split_lo(h32[:, 4 * g:4 * g + 4, :], g, 0)
            for i in range(4):
                lo(0, i)

            chained = [0]

            def link(ins):
                chained[0] += 1
                ins.then_inc(gate_chain, 1)
                v.wait_ge(gate_chain, chained[0])

            def gates_dve():
                heads = g_in.rearrange("p (k j c) -> p k j c", k=2, c=CHUNKS)
                v.wait_ge(logits_turned, 1)
                for h in range(2):
                    last = v.tensor_copy(heads[HALF[h]], ps[HALF[h], 5, 0:64].rearrange(
                        "p (c k j h) -> p h k j c", c=CHUNKS, k=2, h=2)[:, h])
                link(last)
                v.wait_ge(par_loaded, 16 * 13)
                for h in range(2):
                    bias = dt8[HALF[h]].rearrange("p (j h) -> p h j", h=2)[:, h]
                    last = v.tensor_tensor(heads[HALF[h], 1], heads[HALF[h], 1], over(bias, CHUNKS), ALU.add)
                link(last)
                y = g_in[:, 16:32]
                v.scalar_tensor_tensor(out=g_t2, in0=y, scalar=-1.0, in1=y, op0=ALU.mult, op1=ALU.min).then_inc(minus_abs, 1)
                v.wait_ge(gate_log, 1)
                link(v.tensor_scalar(g_t1, g_t1, 1.0, None, ALU.add))
                link(v.reciprocal(g_beta, g_t1))
                link(v.scalar_tensor_tensor(out=g_t3, in0=y, scalar=0.0, in1=g_t2, op0=ALU.max, op1=ALU.add))
                for h in range(2):
                    ea = al8[HALF[h]].rearrange("p (j h) -> p h j", h=2)[:, h]
                    sp_h = g_t3[HALF[h]].rearrange("p (j c) -> p j c", c=CHUNKS)
                    last = v.scalar_tensor_tensor(out=g_g[HALF[h]].rearrange("p (j c) -> p j c", c=CHUNKS), in0=sp_h, scalar=-1.0,
                                                  in1=over(ea, CHUNKS), op0=ALU.mult, op1=ALU.mult)
                last.then_inc(log_decay, 1)

            def dve_qkv_block(i, gates=False, first=False):
                lo(i, 0)
                post_add(4 * i - 4, None if first else (convolved, 4 * i - 7))
                lo(i, 1)
                conv_qkv(4 * i - 4)
                if gates:
                    gates_dve()
                lo(i, 2)
                lo(i, 3)

            v.wait_ge(filled, 1)
            dve_qkv_block(1, gates=True, first=True)
            with v.Fori(2, 6) as i:
                dve_qkv_block(i)

            post_add(20, (convolved, 17))
            v.wait_ge(decay_sums, 1)
            link(v.tensor_copy(g_sum, ps[:, 5, 64:128]))
            v.tensor_tensor(g_kt, g_tot, g_cum, ALU.subtract).then_inc(decay_summed, 1)
            conv_qkv(20)
            v.wait_ge(decay_exps, 3)
            v.scalar_tensor_tensor(out=g_nbeg, in0=g_beta, scalar=-1.0, in1=g_eg, op0=ALU.mult, op1=ALU.mult).then_inc(gates_ready, 1)

            def slot_dve(s):
                if s == 0:
                    for p in range(PAIRS):
                        v.wait_ge(q_root, p + 1)
                        v.reciprocal(sq_q[:, hs(p), :], sq_q[:, hs(p), :]).then_inc(q_inv, 1)
                    v.wait_ge(silu_done, 24)
                    for p in range(PAIRS):
                        v.wait_ge(q_inv, p + 1)
                        v.scalar_tensor_tensor(out=qT[:, hs(p), :], in0=qT[:, hs(p), :], scalar=QSCALE, in1=sq_q[:, hs(p), :],
                                               op0=ALU.mult, op1=ALU.mult).then_inc(q_normed, 1)
                    for p in range(PAIRS):
                        v.wait_ge(k_root, p + 1)
                        v.reciprocal(sq_k[:, hs(p), :], sq_k[:, hs(p), :]).then_inc(k_inv, 1)
                    for p in range(PAIRS):
                        v.wait_ge(k_inv, p + 1)
                        v.tensor_tensor(kT[:, hs(p), :], kT[:, hs(p), :], sq_k[:, hs(p), :], ALU.mult).then_inc(k_normed, 1)
                if s == 1:
                    for p in range(PAIRS):
                        v.wait_ge(row_g, p + 1)
                        for h in range(2):
                            last = v.tensor_tensor(decay[HALF[h], js(p), :],
                                                   ps[HALF[h], 4 + p, SEQ * h:SEQ * h + SEQ].rearrange("p (j n) -> p j n", n=64),
                                                   over(g_cum[HALF[h], js(p)], 64), ALU.subtract)
                        last.then_inc(decay_diff, 1)
                    for p in range(PAIRS):
                        v.wait_ge(decay_diff, p + 1)
                        v.tensor_scalar(decay[:, js(p), :], decay[:, js(p), :], 0.0, None, ALU.min).then_inc(decay_bound, 1)
                    for p in range(PAIRS):
                        v.wait_ge(decay_exp, p + 1)
                        v.tensor_tensor(decay[:, js(p), :], decay[:, js(p), :], times(cst[:, C_CAUSAL:C_CAUSAL + 64], CHUNKS),
                                        ALU.mult).then_inc(decay_ready, 1)
                if s == 2:
                    for p in range(PAIRS):
                        v.wait_ge(row_b, p + 1)
                        v.wait_ge(decay_ready, p + 1)
                        v.tensor_tensor(bdec[:, js(p), :], ps[:, 4 + p, 0:SEQ].rearrange("p (j n) -> p j n", n=64),
                                        decay[:, js(p), :], ALU.mult).then_inc(beta_row, 1)
                    for p in range(PAIRS):
                        v.wait_ge(beta_row, p + 1)
                        v.tensor_tensor(bdec[:, js(p), :], bdec[:, js(p), :], times(cst[:, C_STRICT:C_STRICT + 64], CHUNKS),
                                        ALU.mult).then_inc(beta_decay, 1)
                if s == 3:
                    v.wait_ge(zeroed, 1)
                    for p in range(PAIRS):
                        v.wait_ge(kq, p + 1)
                        v.wait_ge(beta_decay, p + 1)
                        for h in range(2):
                            last = v.tensor_tensor(LT[HALF[h], js(p), 64 * h:64 * h + 64], pbank(p, P)[HALF[h], :, 64:128],
                                                   bdec[HALF[h], js(p), :], ALU.mult)
                        last.then_inc(lt_ready, 1)
                        v.tensor_tensor(qkt[:, js(p), :], pbank(p, P)[:, :, 0:64], decay[:, js(p), :], ALU.mult).then_inc(qkt_ready, 1)
                    for p in range(PAIRS):
                        v.wait_ge(lt_ready, p + 1)
                        v.tensor_tensor(TT_[:, js(p), :], LT[:, js(p), :], times(cst[:, C_NM + 5 * P:C_NM + 6 * P], CHUNKS),
                                        ALU.mult).then_inc(tt_part, 1)
                    for p in range(PAIRS):
                        v.wait_ge(tt_part, p + 1)
                        v.tensor_tensor(TT_[:, js(p), :], TT_[:, js(p), :], times(ident[:, :], CHUNKS), ALU.add).then_inc(tt_first, 1)
                if 5 <= s < 20 and (s - 5) % 3 == 1:
                    l = (s - 5) // 3
                    for p in range(PAIRS):
                        v.wait_ge(tlt, PAIRS * l + p + 1)
                        v.tensor_tensor(X_[:, js(p), :], pbank(p, P), times(cst[:, C_NM + P * l:C_NM + P * l + P], CHUNKS),
                                        ALU.mult).then_inc(tlt_masked, 1)
                    for p in range(PAIRS):
                        v.wait_ge(tlt_masked, PAIRS * l + p + 1)
                        v.tensor_tensor(Tm[:, js(p), :], Tm[:, js(p), :], X_[:, js(p), :], ALU.add).then_inc(t_joined, 1)
                if s == 20:
                    v.wait_ge(gates_ready, 1)
                    for p in range(PAIRS):
                        v.wait_ge(k_tok, p + 1)
                        v.tensor_tensor(kg[:, js(p), :], pbank(p, P), over(g_nbeg[:, js(p)], P), ALU.mult)
                        v.tensor_tensor(ktail[:, js(p), :], pbank(p, P), over(g_kt[:, js(p)], P), ALU.mult).then_inc(k_scaled, 1)
                if s == 21:
                    for p in range(PAIRS):
                        v.wait_ge(v_tok, p + 1)
                        v.tensor_tensor(vb[:, js(p), :], pbank(p, P), over(g_beta[:, js(p)], P), ALU.mult).then_inc(v_scaled, 1)
                if s >= 25 and s % 2 and s < 31:
                    c = (s - 25) // 2
                    if c == 0:
                        v.wait_ge(pooled, 4)
                    for p in range(PAIRS):
                        v.wait_ge(so_prod, PAIRS * c + p + 1)
                        for h in range(2):
                            new = ps[:, 4 + p, 256 + P * h:256 + P * h + P]
                            j = CHUNKS * p + c
                            if c == 0:
                                last = v.tensor_copy(S[:, 2 * p + h, :], new)
                            else:
                                v.wait_ge(s_ready, PAIRS * c - PAIRS + p + 1)
                                last = v.scalar_tensor_tensor(out=S[:, 2 * p + h, :], in0=S[:, 2 * p + h, :], scalar=g_last[:, h, j:j + 1],
                                                              in1=new, op0=ALU.mult, op1=ALU.add)
                        last.then_inc(s_ready, 1)

            def late_half(c):
                lo_half(48 + c, (c // 2) % 2, c % 2)

            late_half(0)
            late_half(1)
            for s in range(32):
                if s == 8:
                    for f in range(4):
                        v.wait_ge(copied, 24 + f + 1)
                        v.tensor_tensor(uT[:, f, :], ps[:, f, 0:256], yb[:, f, :], ALU.add).then_inc(evacuated, 1)
                if s == 16:
                    for f in range(4):
                        v.wait_ge(copied, 28 + f + 1)
                        v.tensor_tensor(uT[:, 4 + f, :], ps[:, f, 0:256], yb[:, f, :], ALU.add).then_inc(evacuated, 1)
                if s == 24:
                    post_add(32)
                slot_dve(s)
                late_half(s + 2)

            post_add(36, (silu_done, 25))
            for g in range(2):
                v.wait_ge(pool_hi, g + 1)
                v.tensor_tensor(act[:, 8 + 4 * g:12 + 4 * g, SEQ:], uT[:, 4 * g:4 * g + 4, :],
                                act[:, 8 + 4 * g:12 + 4 * g, 0:SEQ].bitcast(F32), ALU.subtract).then_inc(pool_lo, 1)
            lo(10, 1)
            for p in range(PAIRS):
                v.wait_ge(o_root, p + 1)
                v.reciprocal(sq_o[:, hs(p), :], sq_o[:, hs(p), :]).then_inc(o_inv, 1)
            for p in range(PAIRS):
                v.wait_ge(o_inv, p + 1)
                v.wait_ge(o_copied, PAIRS * 3 + p + 1)
                v.scalar_tensor_tensor(out=oT[:, hs(p), :], in0=oT[:, hs(p), :], scalar=cols[:, ONW:ONW + 1], in1=sq_o[:, hs(p), :],
                                       op0=ALU.mult, op1=ALU.mult).then_inc(o_normed, 1)
            v.wait_ge(silu_done, 32)
            for p in range(PAIRS):
                v.wait_ge(o_normed, p + 1)
                v.tensor_tensor(oT[:, hs(p), :], oT[:, hs(p), :], zT[:, hs(p), :], ALU.mult).then_inc(o_gated, 1)
            for p in range(PAIRS):
                v.wait_ge(o_hi, p + 1)
                v.tensor_tensor(act[:, hs(p), SEQ:], oT[:, hs(p), :], act[:, hs(p), 0:SEQ].bitcast(F32), ALU.subtract).then_inc(o_lo, 1)
            lo(10, 2)
            lo(10, 3)

            def dve_out_block(b, i, first=False):
                lo(b, 0)
                post_add(4 * b - 4, (silu_done, 29) if first else (residual, 4 * i - 7))
                lo(b, 1)
                post_residual(4 * i - 4, 4 * i - 4, 4 * b - 4)
                lo(b, 2)
                lo(b, 3)
                post_sum(4 * i - 4, first)

            dve_out_block(11, 1, first=True)
            with v.Fori(2, 4) as i:
                dve_out_block(i + 10, i)
            post_add(52, (residual, 9))
            post_residual(12, 12, 52)
            post_sum(12)

            v.wait_ge(root_ready, 1)
            v.reciprocal(rstd[:, :], rstd[:, :]).then_inc(rstd_ready, 1)
            v.wait_ge(rstd_ready, 1)
            group = (yb, gb)
            for g in range(5):
                if g in (2, 3):
                    v.wait_ge(act_lo, 4 + g - 1)
                if g < 4:
                    for f in range(4):
                        t = 4 * g + f
                        v.scalar_tensor_tensor(out=group[g % 2][:, f, :], in0=xT[:, t, :], scalar=cols[:, N2 + t:N2 + t + 1],
                                               in1=rstd[:, :], op0=ALU.mult, op1=ALU.mult).then_inc(normed, 1)
                if g:
                    split_lo(group[(g - 1) % 2][:, :, :], g - 1, 4)

            def dve_up_block(b, i, prev, first=False):
                lo(b, 0)
                if prev is not None:
                    post_add(4 * b - 4, (residual, 13) if first else (convolved, 24 + 8 * i + (1 if prev == "value" else -3)))
                lo(b, 1)
                if prev is not None:
                    conv_ffn(8 * i + (4 if prev == "value" else 0), 4 * i + (44 if prev == "value" else 0))
                lo(b, 2)
                if prev == "value":
                    products(i)
                lo(b, 3)
                if prev == "value":
                    product_split_lo(i)

            def products(i):
                for f in range(4):
                    v.wait_ge(convolved, 24 + 8 * i + 4 + f + 1)
                    v.wait_ge(silu_done, 32 + 4 * i + f + 1)
                    v.tensor_tensor(yb[:, f, :], yb[:, f, :], gb[:, f, :], ALU.mult).then_inc(product, 1)

            def product_split_lo(i):
                for f in range(4):
                    v.wait_ge(product_hi, 4 * i + f + 1)
                    k = bass.ds(4 * i + f, 1)
                    v.tensor_tensor(fact[:, k, SEQ:], yb[:, f:f + 1, :], fact[:, k, 0:SEQ].bitcast(F32),
                                    ALU.subtract).then_inc(product_lo, 1)

            dve_up_block(UP_B, 0, None)
            dve_up_block(UP_B + 1, 0, "gate", first=True)
            with v.Fori(0, 10) as i:
                dve_up_block(UP_B + 2 + 2 * i, i, "value")
                dve_up_block(UP_B + 3 + 2 * i, i + 1, "gate")

            def down_pair(half, i):
                for n in range(2):
                    for h in range(2):
                        lo_half(2 * (DOWN_U + DOWN_STEPS * half + n) + 4 * i + h, n, h, 2)

            lo_half(2 * DOWN_U, 0, 0, 2)
            lo_half(2 * DOWN_U + 1, 0, 1, 2)
            post_add(4 * DOWN_B - 4, (convolved, 24 + 81))
            lo_half(2 * DOWN_U + 2, 1, 0, 2)
            lo_half(2 * DOWN_U + 3, 1, 1, 2)
            conv_ffn(84, 84)
            products(10)
            down_pair(0, 1)
            product_split_lo(10)
            with v.Fori(2, DOWN_STEPS // 2) as i:
                down_pair(0, i)

            def down_posts(half, used):
                t = DOWN_T + 8 * half
                post_add(t, used, bank=0)
                post_residual(8 * half, 16 + 8 * half, t)
                post_sum(16 + 8 * half, half == 0)
                post_add(t + 4, (residual, 16 + 8 * half + 1), bank=4)
                post_residual(8 * half + 4, 16 + 8 * half + 4, t + 4)
                post_sum(16 + 8 * half + 4)

            down_pair(1, 0)
            down_posts(0, (convolved, 24 + 85))
            with v.Fori(1, DOWN_STEPS // 2) as i:
                down_pair(1, i)
            down_posts(1, (residual, 21))

            v.wait_ge(root_ready, 2)
            v.reciprocal(rstd[:, :], rstd[:, :]).then_inc(rstd_ready, 1)
            v.wait_ge(rstd_ready, 2)
            for t in range(KD):
                v.scalar_tensor_tensor(out=xT[:, t, :], in0=xT[:, t, :], scalar=cols[:, NF + t:NF + t + 1],
                                       in1=rstd[:, :], op0=ALU.mult, op1=ALU.mult).then_inc(y_normed, 1)
            for n in range(1, 8, 2):
                v.wait_ge(y_turned, n + 1)
                v.tensor_copy(raw[:, n // 4, 512 * (n % 4):512 * (n % 4) + 512], ps[:, n, :]).then_inc(y_copied[1], 1)

        @block.tensor
        def _(t_e):
            t = t_e

            def slab(slot, f, k, x, start, stop, bank):
                n_cols = 2048 // k
                wh = w_hi[:, slot, :].rearrange("p (k n) -> p k n", k=k)
                wl = w_lo[:, slot, :].rearrange("p (k n) -> p k n", k=k)
                for n in range(k):
                    c = slice(P * f, P * f + P)
                    t.matmul(ps[:, bank, :], wh[:, n, c], x[n], start=start and n == 0, stop=False)
                    last = t.matmul(ps[:, bank, 0:SEQ], wl[:, n, c], x[n][:, 0:SEQ], start=False, stop=stop and n == k - 1)
                return last

            def unit(b, i, row, parts=(0, 1)):
                for h in parts:
                    t.wait_ge(lo_split, 8 * b + 2 * i + h + 1)
                    for f in (2 * h, 2 * h + 1):
                        if i == 0 and not (isinstance(b, int) and b == 0):
                            t.wait_ge(evacuated, 4 * b + f - 3)
                        slab(i % 2, f, 4, [act[:, row + n, :] for n in range(4)], i == 0, i == 3, f).then_inc(slabs, 1)

            t.wait_ge(cst_loaded, 48)
            t.wait_ge(x_loaded, 32)
            for i in range(8):
                for n in range(4):
                    last = t.transpose(ps[:, i, P * n:P * n + P], xtok[:, n % 2, P * (2 * i + n // 2):P * (2 * i + n // 2) + P], ident[:, :])
                last.then_inc(x_turned, 1)
            t.wait_ge(par_loaded, 16 * 13)
            t.wait_ge(x_copied_act, 1)
            at = 0
            for tile, rows in enumerate((57, 88, 88, 88, 88, 96)):
                last = t.transpose(ps[:, 0, at:at + rows], staged[0:rows, tile, :], ident[0:rows, 0:rows])
                at += rows
            last.then_inc(par_turned, 1)
            t.wait_ge(x_copied_dve, 1)
            for n in range(TT):
                t.wait_ge(x_diag, n + 1)
                last = t.matmul(ps[:, 1, P * n:P * n + P], ones[:, :], rdiag[:, n, :], start=True, stop=True)
            last.then_inc(rstd_rows, 1)
            t.wait_ge(normed, KD)
            t.wait_ge(x_copied_act, 3)
            for k in range(KD):
                last = t.matmul(ps[0:16, 4, 0:SEQ], w_log[:, k, :], h32[:, k, :], start=k == 0, stop=k == KD - 1)
            last.then_inc(logits, 1)
            t.wait_ge(cols_ready, 1)
            t.wait_ge(x_copied_act, 4)
            t.wait_ge(x_copied_dve, 4)
            for i in range(4):
                t.wait_ge(act_lo, i + 1)
                unit(0, i, 4 * i)
            t.wait_ge(logits_twice, 1)
            for c in range(CHUNKS):
                last = t.matmul(ps[:, 5, 16 * c:16 * c + 16], lgd[:, c].rearrange("p d n -> p (d n)"), ident[0:16, 0:16],
                                start=True, stop=True)
            last.then_inc(logits_turned, 1)
            with t.Fori(1, 6) as b:
                for i in range(4):
                    unit(b, i, 4 * i)

            t.wait_ge(log_decay, 1)
            t.matmul(ps[:, 5, 64:80], cst[:, C_TRI:C_TRI + P], g_g, start=True, stop=True)
            t.matmul(ps[:, 5, 80:96], cst[:, C_BLOCK:C_BLOCK + P], g_g, start=True, stop=True)
            for h in range(2):
                last = t.matmul(ps[:, 5, 96 + 16 * h:112 + 16 * h], cst[:, C_HALF + P * h:C_HALF + P * h + P], g_g, start=True, stop=True)
            last.then_inc(decay_sums, 1)

            def slot_pe(s):
                for p in range(PAIRS):
                    bank = 4 + p
                    if s == 0:
                        t.wait_ge(q_sq, p + 1)
                        t.wait_ge(decay_summed, 1)
                        t.matmul(ps[:, bank, :], ones[:, :], sq_q[:, hs(p), :].rearrange("p h n -> p (h n)"),
                                 start=True, stop=True).then_inc(q_sum, 1)
                    elif s == 1:
                        t.wait_ge(diag_ready, 1)
                        t.wait_ge(k_root, p + 1)
                        for h in range(2):
                            last = t.matmul(ps[:, bank, SEQ * h:SEQ * h + SEQ], cst[:, C_HALF + P * h:C_HALF + P * h + P],
                                            diag_g[:, js(p), :].rearrange("p j n -> p (j n)"), start=True, stop=True)
                        last.then_inc(row_g, 1)
                    elif s == 2:
                        t.wait_ge(diag_ready, 2)
                        t.wait_ge(row_exp, p + 1)
                        t.matmul(ps[:, bank, 0:SEQ], cst[:, C_BLOCK:C_BLOCK + P], diag_b[:, js(p), :].rearrange("p j n -> p (j n)"),
                                 start=True, stop=True).then_inc(row_b, 1)
                    elif s == 3:
                        t.wait_ge(q_normed, p + 1)
                        t.wait_ge(k_normed, p + 1)
                        t.wait_ge(beta_row, p + 1)
                        for c in range(CHUNKS):
                            for h in range(2):
                                last = t.matmul(ps[HALF[h], bank, P * c:P * c + P].rearrange("p (a n) -> p a n", a=2),
                                                by_problem[:, PAIRS + p, c, h, :], by_problem[:, p:PAIRS + p + 1:PAIRS, c, h, :],
                                                start=True, stop=True)
                        last.then_inc(kq, 1)
                    elif s == 4:
                        t.wait_ge(tt_first, p + 1)
                        t.wait_ge(qkt_ready, p + 1)
                        for c in range(CHUNKS):
                            last = t.transpose(ps[:, bank, P * c:P * c + P], TT_[:, CHUNKS * p + c, :], ident[:, :])
                        last.then_inc(t_turned, 1)
                    elif 5 <= s < 20:
                        l, k = divmod(s - 5, 3)
                        n = PAIRS * l + p
                        if k == 0:
                            t.wait_ge(t_first, p + 1)
                            if l:
                                t.wait_ge(tt_copied, n - PAIRS + 1)
                        if k == 1:
                            t.wait_ge(lx_copied, n + 1)
                        if k == 2:
                            t.wait_ge(t_joined, n + 1)
                        for c in range(CHUNKS):
                            j = CHUNKS * p + c
                            o = ps[:, bank, P * c:P * c + P]
                            if k == 0:
                                last = t.matmul(o, LT[:, j, :], Tm[:, j, :], start=True, stop=True)
                            elif k == 1:
                                last = t.matmul(o, TT_[:, j, :], X_[:, j, :], start=True, stop=True)
                            else:
                                last = t.transpose(o, Tm[:, j, :], ident[:, :])
                        last.then_inc((lx, tlt, t_back)[k], 1)
                    elif s in (20, 21):
                        if s == 20:
                            t.wait_ge(tt_copied, PAIRS * 4 + p + 1)
                        else:
                            t.wait_ge(k_scaled, p + 1)
                        for c in range(CHUNKS):
                            tokens = by_problem[:, (PAIRS if s == 20 else 2 * PAIRS) + p, c]
                            last = t.transpose(ps[:, bank, P * c:P * c + P], tokens.rearrange("p h n -> p (h n)"), ident[:, :])
                        last.then_inc(k_tok if s == 20 else v_tok, 1)
                    elif s == 22:
                        t.wait_ge(v_scaled, p + 1)
                        for c in range(CHUNKS):
                            last = t.matmul(ps[:, bank, P * c:P * c + P], kg[:, CHUNKS * p + c, :], TT_[:, CHUNKS * p + c, :],
                                            start=True, stop=True)
                        last.then_inc(w_prod, 1)
                    elif s == 23:
                        t.wait_ge(pooled, p + 1)
                        t.wait_ge(pool_w_loaded, 16)
                        t.wait_ge(w_copied, p + 1)
                        for f in range(2):
                            for k in range(2):
                                last = t.matmul(ps[:, bank, SEQ * f:SEQ * f + SEQ], pw[:, p, k, P * f:P * f + P], uT[:, 2 * p + k, :],
                                                start=k == 0, stop=k == 1)
                        last.then_inc(pool_prod, 1)
                    elif s % 2 == 0:
                        c = (s - 24) // 2
                        j = CHUNKS * p + c
                        if c == 0:
                            t.wait_ge(pool_out, 2 * p + 2)
                        else:
                            t.wait_ge(o_copied, PAIRS * (c - 1) + p + 1)
                        last = t.matmul(ps[:, bank, 0:P], TT_[:, j, :], vb[:, j, :], start=True, stop=c == 0)
                        if c:
                            t.wait_ge(s_ready, PAIRS * (c - 1) + p + 1)
                            for h in range(2):
                                last = t.matmul(ps[HALF[h], bank, 0:P], W[:, j, h, :], S[:, 2 * p + h, :], start=False, stop=True)
                        last.then_inc(v_prod, 1)
                    else:
                        c = (s - 25) // 2
                        j = CHUNKS * p + c
                        t.wait_ge(qg_ready, 1)
                        t.wait_ge(v_copied, PAIRS * c + p + 1)
                        for h in range(2):
                            o = ps[:, bank, P + 64 * h:P + 64 * h + 64]
                            if c:
                                t.matmul(o, S[:, 2 * p + h, :], qg_problem[:, p, c, h, :], start=True, stop=False)
                            last = t.matmul(o, vnew[:, p, h, :], qkt[:, j, :], start=c == 0, stop=True)
                        if c < CHUNKS - 1:
                            last = t.matmul(ps[:, bank, 256:512], ktail[:, j, :], vnew[:, p, :, :].rearrange("p h n -> p (h n)"),
                                            start=True, stop=True)
                        last.then_inc(so_prod, 1)
                if s == 0:
                    for p in range(PAIRS):
                        t.wait_ge(k_sq, p + 1)
                        t.wait_ge(q_root, p + 1)
                        t.matmul(ps[:, 4 + p, :], ones[:, :], sq_k[:, hs(p), :].rearrange("p h n -> p (h n)"),
                                 start=True, stop=True).then_inc(k_sum, 1)

            for s in range(32):
                slot_pe(s)
                u = s // 2
                unit(6 + u // 4, u % 4, 4 * (u % 4), (s % 2,))

            t.wait_ge(pool_lo, 2)
            unit(10, 0, 8)
            for p in range(PAIRS):
                t.wait_ge(o_sq, p + 1)
                t.matmul(ps[:, 4 + p, :], ones[:, :], sq_o[:, hs(p), :].rearrange("p h n -> p (h n)"),
                         start=True, stop=True).then_inc(o_sum, 1)
            unit(10, 1, 12)
            t.wait_ge(o_lo, 2)
            unit(10, 2, 0)
            t.wait_ge(o_lo, 4)
            unit(10, 3, 4)
            with t.Fori(OUT_B + 1, OUT_B + 4) as b:
                for i in range(4):
                    unit(b, i, 4 * i)

            def sums(n):
                t.wait_ge(summed, 16 * n)
                t.wait_ge(o_root, PAIRS)
                t.matmul(ps[:, 4, 0:SEQ], ones[:, :], sumsq[:, :], start=True, stop=True).then_inc(sums_ready, 1)

            sums(1)
            for i in range(4):
                t.wait_ge(act_lo, 4 + i + 1)
                unit(UP_B, i, 4 * i)
            with t.Fori(UP_B + 1, UP_B + 22) as b:
                for i in range(4):
                    unit(b, i, 4 * i)

            def down_unit(half, i, n, start=False, stop=False):
                u2 = 2 * (DOWN_U + DOWN_STEPS * half + n) + 4 * i
                for h in range(2):
                    t.wait_ge(lo_split, u2 + h + 1)
                    for f in range(4 * h, 4 * h + 4):
                        if start:
                            if half == 0 and f < 4:
                                t.wait_ge(evacuated, DOWN_T - 4 + f + 1)
                            if half == 0 and f == 4:
                                t.wait_ge(root_ready, 1)
                            if half == 1:
                                t.wait_ge(evacuated, DOWN_T + f + 1)
                        x = [fact[:, bass.ds(4 * i + 2 * n + k, 1), :].rearrange("p a n -> p (a n)") for k in range(2)]
                        last = slab(n, f, 2, x, start, stop, f)
                        if f % 2:
                            last.then_inc(slabs, 1)

            for half in range(2):
                down_unit(half, 0, 0, start=True)
                down_unit(half, 0, 1)
                with t.Fori(1, DOWN_STEPS // 2 - 1) as i:
                    down_unit(half, i, 0)
                    down_unit(half, i, 1)
                if half == 0:
                    t.wait_ge(product_lo, KF)
                down_unit(half, DOWN_STEPS // 2 - 1, 0)
                down_unit(half, DOWN_STEPS // 2 - 1, 1, stop=True)
            t.wait_ge(evacuated, DOWN_T + 16)
            sums(2)
            for n in range(8):
                for k in range(4):
                    f = 4 * (n % 4) + k
                    t.wait_ge(y_normed, f + 1)
                    last = t.transpose(ps[:, n, P * k:P * k + P], xT[:, f, P * (n // 4):P * (n // 4) + P], ident[:, :])
                last.then_inc(y_turned, 1)


_INS = ["x", "norm1_w", "w_in", "conv_qkv_w", "a_log", "dt_bias", "out_norm_w", "pool_w", "pool_scale",
        "w_out", "norm2_w", "w_up", "conv_ffn_w", "conv_ffn_b", "w_down", "final_norm_w"]


def kernel(**inputs):
    import numpy as np
    import concourse.bacc as bacc
    from concourse.bass_utils import run_bass_kernel_spmd

    nc = bacc.Bacc("TRN2", target_bir_lowering=False, num_devices=1)
    arrays, args = {}, []
    for name in _INS:
        arrays[f"in_{name}"] = np.ascontiguousarray(inputs[name])
    arrays["in_table"] = constants()
    for name, a in arrays.items():
        args.append(nc.dram_tensor(name, a.shape, mybir.dt.from_np(a.dtype), kind="ExternalInput").ap())
    shape = arrays["in_x"].shape
    args.append(nc.dram_tensor("out_y", shape, F32, kind="ExternalOutput").ap())
    hybrid_layer(nc, *args)
    r = run_bass_kernel_spmd(nc, [arrays], core_ids=[0])
    return r.results[0]["out_y"]
```

```python
from contextlib import ExitStack

import concourse.bass as bass
from concourse import mybir

F32 = mybir.dt.float32
F32R = mybir.dt.float32r
ALU = mybir.AluOpType
ACT = mybir.ActivationFunctionType

P = 128
EPS = 1e-6
PAD = 3
LEVELS = (2, 4, 8, 16, 32)
WINDOWS = (2, 4, 8, 16)

C_NM = 0
C_CAUSAL = C_NM + 6 * P
C_EYE2 = C_CAUSAL + 64
C_TRI = C_EYE2 + 64
C_HALF = C_TRI + P
C_BLOCK = C_HALF + 64
C_COUNT = C_HALF + 2 * P
C_IDENT = C_COUNT + 64
C_ONES = C_IDENT + P
C_ALL = C_ONES + P


def constants():
    import numpy as np

    c = np.zeros((P, C_ALL), np.float32)
    i = np.arange(P)
    for n, s in enumerate(LEVELS + (1,)):
        row, col = i[:, None] // s, i[None, :] // s
        m = ((row % 2 == 1) & (col == row - 1)).astype(np.float32)
        c[:, C_NM + n * P:C_NM + (n + 1) * P] = -m.T
    m, t = (i % 64)[:, None], np.arange(64)[None, :]
    c[:, C_CAUSAL:C_CAUSAL + 64] = t >= m
    c[:, C_EYE2:C_EYE2 + 64] = t == m
    same = (i[:, None] // 64) == (i[None, :] // 64)
    c[:, C_TRI:C_TRI + P] = same & (i[:, None] <= i[None, :])
    c[:64, C_HALF:C_HALF + P] = 1.0
    c[64:, C_HALF + P:C_HALF + 2 * P] = 1.0
    for g, w in enumerate(WINDOWS):
        c[:, C_COUNT + 16 * g:C_COUNT + 16 * g + 16] = 1.0 / np.minimum(np.arange(16) + 1.0, w)
    c[:, C_IDENT:C_IDENT + P] = np.eye(P)
    c[:, C_ONES:C_ONES + P] = 1.0
    return c


def hybrid_layer(nc, x, norm1_w, w_in, conv_qkv_w, a_log, dt_bias, out_norm_w, pool_w, pool_scale,
                 w_out, norm2_w, w_up, conv_ffn_w, conv_ffn_b, w_down, final_norm_w, table, out):
    SEQ, D = x.shape[1], x.shape[2]
    HEADS = a_log.shape[1]
    DN = HEADS * P
    FF = w_down.shape[1]
    KD = D // P
    KF = FF // P
    TT = SEQ // P
    PAIRS, CHUNKS = HEADS // 2, SEQ // 64
    J = PAIRS * CHUNKS
    QSCALE = float(P) ** -0.5
    assert (SEQ, D, HEADS, FF) == (256, 2048, 8, 5632)

    OUT_B, UP_B, DOWN_B = 10, 14, 36
    DOWN_U, DOWN_T = 4 * DOWN_B, 4 * DOWN_B
    DOWN_STEPS = KF // 2
    IN_COLS = [512 * i for i in range(6)] + [4 * DN + 2 * HEADS + 512 * i for i in range(2)] \
        + [3 * DN + 512 * i for i in range(2)]

    w_in2, w_out2, w_up2, w_down2 = w_in[0], w_out[0], w_up[0], w_down[0]
    x2, out2 = x[0], out[0]

    ctx = ExitStack()
    phase_a = ExitStack()
    with ctx:
        def sb(name, shape, dt=F32, where=ctx):
            return where.enter_context(nc.sbuf_tensor(name, shape, dt))

        def sem(name):
            return ctx.enter_context(nc.semaphore(name))

        ps = ctx.enter_context(nc.psum_tensor("ps", [P, 8, 512], F32))

        raw = sb("raw", [P, 2, 2048])
        w_hi = sb("w_hi", [P, 2, 2048], F32R)
        w_lo = sb("w_lo", [P, 2, 2048], F32R)
        act = sb("act", [P, KD, 512], F32R)
        xT = sb("xT", [P, KD, SEQ])
        cols = sb("cols", [P, 505])
        ident = sb("ident", [P, P])
        ones = sb("ones", [P, P])
        yb = sb("yb", [P, 4, SEQ])
        ub = sb("ub", [P, 4, PAD + SEQ])
        eps = sb("eps", [P, 1])
        sumsq = sb("sumsq", [P, SEQ])
        rstd = sb("rstd", [P, SEQ])

        cst = sb("cst", [P, C_IDENT], F32, phase_a)
        qkv = sb("qkv", [P, 3, HEADS, SEQ], F32, phase_a)
        zT = sb("zT", [P, HEADS, SEQ], F32, phase_a)
        uT = sb("uT", [P, HEADS, SEQ], F32, phase_a)
        scr = sb("scr", [P, 4, 2048], F32, phase_a)
        dt_s = sb("dt_s", [P, 1024], F32, phase_a)
        qkt = sb("qkt", [P, J, 64], F32, phase_a)
        masked = sb("masked", [P, J, P], F32, phase_a)
        vnew = sb("vnew", [P, PAIRS, 2, P], F32, phase_a)
        gates = sb("gates", [P, 16 * 14 + 16], F32, phase_a)
        sq_acc = sb("sq_acc", [P, 2], F32, phase_a)
        phase_a.close()
        fact = sb("fact", [P, KF, 512], F32R)
        gb = sb("gb", [P, 4, SEQ])

        xtok = scr[:, 0:2, :]
        h32 = scr[:, 0:2, :].rearrange("p a (t n) -> p (a t) n", n=SEQ)
        staged = scr[:, 2, 0:768].rearrange("p (i n) -> p i n", n=P)
        w_log = scr[:, 2, 1024:1280].rearrange("p (k n) -> p k n", n=16)
        lg = scr[0:16, 3, 0:256]
        lgd = scr[0:16, 3, 512:1024].rearrange("p (c d n) -> p c d n", c=CHUNKS, d=2)
        sqx = scr[:, 3, :]
        LT, Tm, TT_, X_ = (scr[:, i, :].rearrange("p (j n) -> p j n", n=P) for i in range(4))
        vb, kg, ktail = LT, Tm, X_
        sq_q, sq_k = scr[:, 3, :], scr[:, 2, :]
        diag_g = scr[:, 1, 0:1024].rearrange("p (j n) -> p j n", n=64)
        diag_b = scr[:, 1, 1024:2048].rearrange("p (j n) -> p j n", n=64)
        bdec = scr[:, 3, 0:1024].rearrange("p (j n) -> p j n", n=64)
        decay = dt_s[:, :].rearrange("p (j n) -> p j n", n=64)
        S = dt_s[:, :].rearrange("p (h n) -> p h n", n=P)
        diag_q, diag_eq = masked[:, 0:8].rearrange("p a n -> p (a n)").rearrange("p (j n) -> p j n", n=64), \
            masked[:, 8:16].rearrange("p a n -> p (a n)").rearrange("p (j n) -> p j n", n=64)
        win = masked[:, 0:8].rearrange("p a n -> p (a n)").rearrange("p (b k n) -> p b k n", b=2, k=2)
        qT, kT = qkv[:, 0], qkv[:, 1]
        by_problem = qkv[:, :, :, :].rearrange("p k h n -> p k (h n)").rearrange(
            "p k (j c h n) -> p (k j) c h n", j=PAIRS, c=CHUNKS, h=2)
        W = qkv[:, 1].rearrange("p h n -> p (h n)").rearrange("p (j h c) -> p j h c", j=J, h=2)
        oT = qkv[:, 2]
        pw = zT[:, :, :].rearrange("p h n -> p (h n)").rearrange("p (g k n) -> p g k n", g=4, k=2)
        rdiag = scr[:, 3, 1024:1280].rearrange("p (a n) -> p a n", n=P)
        sq_o = scr[:, 1, :].rearrange("p (h n) -> p h n", n=SEQ)
        diag_o = scr[:, 3, :].rearrange("p (i n) -> p i n", n=P)

        def gcol(i, n=16):
            return gates[:, 16 * i:16 * i + n]

        g_in, g_beta, g_g = gates[:, 0:32], gcol(2), gcol(3)
        g_t1, g_t2, g_sum, g_eg, g_kt, g_nbeg = gcol(4), gcol(5), gcol(6, 64), gcol(10), gcol(11), gcol(12)
        g_cum, g_tot = g_sum[:, 0:16], g_sum[:, 16:32]
        g_last = g_sum[:, 32:64].rearrange("p (h j) -> p h j", h=2)
        al8, dt8 = gates[:, 208:216], gates[:, 216:224]
        g_t3 = gates[:, 224:240]
        g_norm = sumsq[:, 0:32]
        g_rq, g_rk, g_qs, g_brk, g_eq, g_ro = (sumsq[:, 16 * i:16 * i + 16] for i in range(6))

        N1, N2, NF, PSC, ONW, CB, CW, QW = 0, 16, 32, 48, 56, 57, 145, 409

        def col(n):
            return cols[:, n:n + 1]

        def over(ap, n):
            return ap.unsqueeze(2).to_broadcast([ap.shape[0], ap.shape[1], n])

        def times(ap, n):
            return ap.unsqueeze(1).to_broadcast([ap.shape[0], n, ap.shape[1]])

        def js(p):
            return slice(CHUNKS * p, CHUNKS * p + CHUNKS)

        def hs(p):
            return slice(2 * p, 2 * p + 2)

        def pbank(p, n):
            return ps[:, 4 + p, :].rearrange("p (c n) -> p c n", n=n)

        HALF = (slice(0, 64), slice(64, 128))

        raw_loaded = [sem("raw_loaded0"), sem("raw_loaded1")]
        hi_split, lo_split = sem("hi_split"), sem("lo_split")
        slabs = sem("slabs")
        copied = sem("copied")
        evacuated = sem("evacuated")
        tapped = sem("tapped")
        tap1, tap2 = sem("tap1"), sem("tap2")
        convolved = sem("convolved")
        silu_done = sem("silu_done")
        product = sem("product")
        product_hi, product_lo = sem("product_hi"), sem("product_lo")
        residual = sem("residual")
        squared, summed = sem("squared"), sem("summed")
        normed = sem("normed")
        act_hi, act_lo = sem("act_hi"), sem("act_lo")
        rstd_ready, sums_ready, root_ready = sem("rstd_ready"), sem("sums_ready"), sem("root_ready")
        x_loaded, cst_loaded, par_loaded, pool_w_loaded = sem("x_loaded"), sem("cst_loaded"), sem("par_loaded"), sem("pool_w_loaded")
        x_turned, x_copied_act, x_copied_dve = sem("x_turned"), sem("x_copied_act"), sem("x_copied_dve")
        par_turned, cols_ready = sem("par_turned"), sem("cols_ready")
        x_squared, x_root, x_rstd, x_diag, rstd_rows = sem("x_squared"), sem("x_root"), sem("x_rstd"), sem("x_diag"), sem("rstd_rows")
        filled = sem("filled")
        zeroed = sem("zeroed")
        logits, logits_copied, logits_twice, logits_turned = sem("logits"), sem("logits_copied"), sem("logits_twice"), sem("logits_turned")
        gate_chain, minus_abs, gate_exp, gate_log, log_decay = sem("gate_chain"), sem("minus_abs"), sem("gate_exp"), sem("gate_log"), sem("log_decay")
        decay_sums, decay_summed, decay_exps, gates_ready = sem("decay_sums"), sem("decay_summed"), sem("decay_exps"), sem("gates_ready")
        diag_ready = sem("diag_ready")
        qk_sq, qk_sum, qk_root, qk_inv, norm_cols = (sem(n) for n in ("qk_sq", "qk_sum", "qk_root", "qk_inv", "norm_cols"))
        decay_rows, decay_diff, decay_bound, decay_exp, decay_ready, beta_decay, q_row, q_decay = (
            sem(n) for n in ("decay_rows", "decay_diff", "decay_bound", "decay_exp", "decay_ready", "beta_decay", "q_row", "q_decay"))
        kq, lt_ready, qkt_ready, qg_rows, qg_ready = (sem(n) for n in ("kq", "lt_ready", "qkt_ready", "qg_rows", "qg_ready"))
        tt_part, tt_first, t_turned, t_first = sem("tt_part"), sem("tt_first"), sem("t_turned"), sem("t_first")
        l_masked, lx, lx_copied, tlt, t_joined, t_back, tt_copied = (
            sem(n) for n in ("l_masked", "lx", "lx_copied", "tlt", "t_joined", "t_back", "tt_copied"))
        k_tok, k_scaled, v_tok, v_scaled, w_prod, w_copied = (
            sem(n) for n in ("k_tok", "k_scaled", "v_tok", "v_scaled", "w_prod", "w_copied"))
        v_prod, v_copied, so_prod, s_ready, o_copied = (sem(n) for n in ("v_prod", "v_copied", "so_prod", "s_ready", "o_copied"))
        o_sq, o_sum, o_root, o_inv, o_diag, o_row, o_normed, o_gated, o_hi, o_lo = (
            sem(n) for n in ("o_sq", "o_sum", "o_root", "o_inv", "o_diag", "o_row", "o_normed", "o_gated", "o_hi", "o_lo"))
        pool_chain, pooled, pool_prod, pool_out, pool_hi, pool_lo = (
            sem(n) for n in ("pool_chain", "pooled", "pool_prod", "pool_out", "pool_hi", "pool_lo"))
        y_normed, y_turned, stored = sem("y_normed"), sem("y_turned"), sem("stored")
        y_copied = [sem("y_copied_act"), sem("y_copied_dve")]

        def halves(t, slot, h, k=4):
            n = 1024 // k
            return t[:, slot, :].rearrange("p (k n) -> p k n", k=k)[:, :, n * h:n * h + n]

        SCHEDULE = {4: ("decay_rows", 0), 7: ("q_row", 0), 9: ("kq", 0), 12: ("qg_rows", 0), 13: ("first", 0)}
        for l in range(len(LEVELS)):
            SCHEDULE[15 + 3 * l], SCHEDULE[16 + 3 * l] = ("lx", l), ("join", l)
            if l < len(LEVELS) - 1:
                SCHEDULE[17 + 3 * l] = ("turn", l)
        SCHEDULE.update({30: ("k_tok", 0), 31: ("v_tok", 0), 33: ("w", 0)})
        for c in range(CHUNKS):
            SCHEDULE[35 + 3 * c], SCHEDULE[36 + 3 * c] = ("values", c), ("outputs", c)
        SCHEDULE.update({48: ("mixer", 0), 50: ("o_sums", 0), 53: ("mix_split", 0), 55: ("o_rows", 0), 57: ("mix_split", 1)})
        QUARTERS = 64

        block = ctx.enter_context(nc.Block())

        @block.sync
        def _(sp):
            for t in range(TT):
                sp.dma_start(xtok[:, t, :], x2[P * t:P * t + P, :]).then_inc(x_loaded, 16)

            def load(u, slot, src, k, first=False):
                if not first:
                    sp.wait_ge(lo_split, 2 * (u - 1))
                sp.dma_start(raw[:, slot, :].rearrange("p (k n) -> p k n", k=k),
                             src.rearrange("(k p) n -> p k n", p=P)).then_inc(raw_loaded[slot], 16)

            def load_block(b, w, c0, order=(0, 1, 2, 3), first=False):
                for i, r in enumerate(order):
                    load(4 * b + i, i % 2, w[512 * r:512 * r + 512, bass.ds(c0, 512)], 4, first and i < 2)

            load_block(0, w_in2, IN_COLS[0], first=True)
            with sp.Fori(1, 6) as i:
                load_block(i, w_in2, i * 512)
            for b in range(6, 10):
                load_block(b, w_in2, IN_COLS[b])
            for i in range(4):
                load_block(OUT_B + i, w_out2, 512 * i, (2, 3, 0, 1))
            with sp.Fori(0, 11) as i:
                load_block(UP_B + 2 * i, w_up2, i * 512)
                load_block(UP_B + 1 + 2 * i, w_up2, i * 512 + FF)
            for half in range(2):
                with sp.Fori(0, DOWN_STEPS // 2) as i:
                    for n in range(2):
                        load(DOWN_U + DOWN_STEPS * half + 2 * i + n, n,
                             w_down2[bass.ds(i * 512 + 256 * n, 256), 1024 * half:1024 * half + 1024], 2)
            for n in range(8):
                sp.wait_ge(y_copied[n % 2], n // 2 + 1)
                sp.dma_start(out2[P * (n // 4):P * (n // 4) + P, 512 * (n % 4):512 * (n % 4) + 512],
                             raw[:, n // 4, 512 * (n % 4):512 * (n % 4) + 512]).then_inc(stored, 16)
            sp.wait_ge(stored, 16 * 8)

        @block.gpsimd
        def _(pool):
            pool.memset(eps[:, :], EPS)
            pool.memset(vnew[:, :, :, :], 0.0)
            pool.memset(ub[:, :, 0:PAD], 0.0).then_inc(filled, 1)

            pool.wait_ge(cst_loaded, 48)
            pool.wait_ge(logits, 1)
            pool.wait_ge(act_hi, 4)
            pool.wait_ge(act_lo, 4)
            pool.memset(LT, 0.0).then_inc(zeroed, 1)
            pool.wait_ge(decay_summed, 1)
            pool.tensor_tensor(diag_g, times(cst[:, C_EYE2:C_EYE2 + 64], J), over(g_cum, 64), ALU.mult).then_inc(diag_ready, 1)
            pool.wait_ge(norm_cols, 1)
            pool.wait_ge(qk_sum, 1)
            pool.tensor_tensor(diag_b, times(cst[:, C_EYE2:C_EYE2 + 64], J), over(g_brk, 64), ALU.mult).then_inc(diag_ready, 1)
            pool.tensor_tensor(qkt[:, :, :], times(cst[:, C_CAUSAL:C_CAUSAL + 64], J), over(g_rk, 64), ALU.mult).then_inc(diag_ready, 1)
            pool.wait_ge(norm_cols, 2)
            pool.tensor_tensor(diag_q, times(cst[:, C_EYE2:C_EYE2 + 64], J), over(g_qs, 64), ALU.mult).then_inc(diag_ready, 1)
            pool.wait_ge(norm_cols, 3)
            pool.tensor_tensor(diag_eq, times(cst[:, C_EYE2:C_EYE2 + 64], J), over(g_eq, 64), ALU.mult).then_inc(diag_ready, 1)
            pool.wait_ge(qg_rows, PAIRS)
            for l in range(len(LEVELS)):
                for p in range(PAIRS):
                    if l == 0:
                        pool.wait_ge(lt_ready, p + 1)
                    else:
                        pool.wait_ge(lx, PAIRS * (l - 1) + p + 1)
                    pool.tensor_tensor(masked[:, js(p), :], LT[:, js(p), :], times(cst[:, C_NM + P * l:C_NM + P * l + P], CHUNKS),
                                       ALU.mult).then_inc(l_masked, 1)

            n = 0
            pool.wait_ge(lx, PAIRS * len(LEVELS))
            for g, w in enumerate(WINDOWS):
                u = uT[:, 2 * g:2 * g + 2, :]
                pool.wait_ge(evacuated, 24 + 2 * g + 2)
                src, b, s = u, 0, 1
                while s < w:
                    dst = win[:, b]
                    pool.tensor_tensor(dst[:, :, s:], src[:, :, s:], src[:, :, :SEQ - s], ALU.add)
                    pool.tensor_copy(dst[:, :, 0:s], src[:, :, 0:s]).then_inc(pool_chain, 1)
                    n += 1
                    pool.wait_ge(pool_chain, n)
                    src, b, s = dst, 1 - b, 2 * s
                mean = win[:, b]
                pool.tensor_tensor(mean[:, :, 0:16], src[:, :, 0:16],
                                   times(cst[:, C_COUNT + 16 * g:C_COUNT + 16 * g + 16], 2), ALU.mult)
                pool.tensor_scalar(mean[:, :, 16:], src[:, :, 16:], 1.0 / w, None, ALU.mult).then_inc(pool_chain, 1)
                n += 1
                pool.wait_ge(pool_chain, n)
                pool.tensor_tensor(u, mean, u, ALU.subtract).then_inc(pooled, 1)
                pool.wait_ge(pooled, g + 1)

        @block.scalar
        def _(act_e):
            a = act_e

            def copy(o, i):
                return a.activation(o, i, ACT.Copy)

            a.dma_start(ident[:, :], table[:, C_IDENT:C_IDENT + P]).then_inc(cst_loaded, 16)
            a.dma_start(ones[:, :], table[:, C_ONES:C_ONES + P]).then_inc(cst_loaded, 16)
            a.dma_start(cst[:, :], table[:, 0:C_IDENT]).then_inc(cst_loaded, 16)
            for tile, r, v, k in [(0, N1, norm1_w[0], 16), (0, N2, norm2_w[0], 16), (0, NF, final_norm_w, 16),
                                  (0, PSC, pool_scale[0], 8), (0, ONW, out_norm_w[0], 1), (1, 0, conv_ffn_b[0], 88)]:
                a.dma_start(staged[r:r + k, tile, :], v.rearrange("(t p) -> t p", p=P)).then_inc(par_loaded, 16)
            for t in range(3):
                a.dma_start(staged[0:88, 2 + t, :], conv_ffn_w[0, t, :].rearrange("(t p) -> t p", p=P)).then_inc(par_loaded, 16)
            a.dma_start(staged[0:96, 5, :], conv_qkv_w[0].rearrange("j (t p) -> (j t) p", p=P)).then_inc(par_loaded, 16)
            a.dma_start(w_log, w_in2[:, 4 * DN:4 * DN + 2 * HEADS].rearrange("(k p) n -> p k n", p=P)).then_inc(par_loaded, 16)
            a.dma_start(al8, a_log[0:1, :].to_broadcast([P, 8])).then_inc(par_loaded, 16)
            a.dma_start(dt8, dt_bias[0:1, :].to_broadcast([P, 8])).then_inc(par_loaded, 16)
            a.dma_start(pw, pool_w[0].rearrange("g (k p) n -> p g k n", p=P)).then_inc(pool_w_loaded, 16)

            def hi_half(u, use, slot, h, k=4):
                if h == 0:
                    a.wait_ge(raw_loaded[slot], 16 * (use + 1))
                if isinstance(u, int) and u in (DOWN_U, DOWN_U + 1):
                    a.wait_ge(slabs, 4 * (u - 2) + 4)
                elif not (isinstance(u, int) and u < 2):
                    a.wait_ge(slabs, 4 * (u - 2) + 2 * (h + 1))
                copy(halves(w_hi, slot, h, k), halves(raw, slot, h, k)).then_inc(hi_split, 1)

            def hi(b, i, k=4):
                for h in range(2):
                    hi_half(4 * b + i, 2 * b + i // 2, i % 2, h, k)

            def post_copy(t, slab, free=None, n=4, bank=0, step=1):
                for f in range(n):
                    a.wait_ge(slabs, slab + f // step + 1)
                    if free is not None:
                        a.wait_ge(free[0], free[1] + f)
                    copy(yb[:, f, :], ps[:, bank + f, 256:512]).then_inc(copied, 1)

            def post_tap(t, weight, bias):
                for f in range(4):
                    a.wait_ge(evacuated, t + f + 1)
                    a.activation(yb[:, f, :], ub[:, f, PAD:], ACT.Identity, scale=cols[:, bass.ds(weight + f, 1)],
                                 bias=0.0 if bias is None else cols[:, bass.ds(bias + f, 1)]).then_inc(tapped, 1)

            def post_square(t, n):
                for f in range(4):
                    a.wait_ge(residual, n + f + 1)
                    a.activation(yb[:, f, :], xT[:, bass.ds(t + f, 1), :].rearrange("p a n -> p (a n)"), ACT.Square).then_inc(squared, 1)

            def split_hi(group, g, n):
                a.wait_ge(normed, n + 4 * g + 4)
                copy(act[:, 4 * g:4 * g + 4, 0:SEQ], group).then_inc(act_hi, 1)

            a.wait_ge(x_loaded, 32)
            for t in range(TT):
                if t:
                    a.wait_ge(x_squared, t)
                a.activation(sqx, xtok[:, t, :], ACT.Square, accum_out=sq_acc[:, t:t + 1]).then_inc(x_squared, 1)
            a.wait_ge(x_squared, 2)
            a.wait_ge(filled, 1)
            a.activation(sq_acc[:, :], sq_acc[:, :], ACT.Sqrt, scale=1.0 / D, bias=eps[:, 0:1]).then_inc(x_root, 1)
            for i in range(0, 8, 2):
                a.wait_ge(x_turned, i + 1)
                copy(xT[:, 2 * i:2 * i + 2, :], ps[:, i, :].rearrange("p (t n) -> p t n", n=SEQ)).then_inc(x_copied_act, 1)
            for g in range(4):
                split_hi(h32[:, 4 * g:4 * g + 4, :], g, 0)
            hi(0, 0)
            hi(0, 1)
            a.wait_ge(logits, 1)
            copy(lg, ps[0:16, 4, 0:SEQ]).then_inc(logits_copied, 1)
            a.wait_ge(logits_copied, 1)
            for d in range(2):
                last = copy(lgd[:, :, d, :], lg.rearrange("p (c n) -> p c n", n=64))
            last.then_inc(logits_twice, 1)
            hi(0, 2)
            hi(0, 3)

            def gates_act():
                a.wait_ge(par_loaded, 16 * 13)
                a.activation(al8, al8, ACT.Exp).then_inc(gate_exp, 1)
                a.wait_ge(minus_abs, 1)
                a.activation(g_t1, g_in[:, 0:16], ACT.Exp, scale=-1.0).then_inc(gate_exp, 1)
                a.activation(g_t2, g_t2, ACT.Exp).then_inc(gate_exp, 1)
                a.wait_ge(gate_exp, 3)
                a.activation(g_t2, g_t2, ACT.Ln, bias=1.0).then_inc(gate_log, 1)

            def qkv_silu(pair, f):
                a.activation(by_problem[:, bass.ds(pair, 1), :, f % 2, :].rearrange("p a c n -> p (a c) n"),
                             yb[:, f, :].rearrange("p (c n) -> p c n", n=64), ACT.Silu).then_inc(silu_done, 1)

            def act_qkv_block(i, gates=False, norms=False):
                hi(i, 0)
                post_copy(4 * i - 4, 16 * i - 4)
                hi(i, 1)
                post_tap(4 * i - 4, QW + 72 + 4 * i - 4, None)
                if gates:
                    gates_act()
                hi(i, 2)
                for f in range(4):
                    a.wait_ge(convolved, 4 * i - 4 + f + 1)
                    qkv_silu(2 * i - 2 + f // 2, f)
                hi(i, 3)
                if norms:
                    a.wait_ge(silu_done, 16)
                    for d, k in ((sq_q, 0), (sq_k, 1)):
                        a.activation(d, qkv[:, k].rearrange("p h n -> p (h n)"), ACT.Square).then_inc(qk_sq, 1)
                    a.wait_ge(decay_summed, 1)
                    a.activation(g_eg, g_cum, ACT.Exp).then_inc(decay_exps, 1)
                    a.activation(g_kt, g_kt, ACT.Exp).then_inc(decay_exps, 1)
                    a.activation(g_sum[:, 32:64], g_sum[:, 32:64], ACT.Exp).then_inc(decay_exps, 1)

            act_qkv_block(1, gates=True)
            with a.Fori(2, 5) as i:
                act_qkv_block(i)
            act_qkv_block(5, norms=True)

            post_copy(20, 92)
            a.wait_ge(qk_sum, 1)
            a.activation(g_norm, ps[:, 5, 128:160], ACT.Sqrt, bias=eps[:, 0:1]).then_inc(qk_root, 1)

            def act_step(step, k):
                for p in range(PAIRS):
                    n = PAIRS * k + p
                    if step == "decay_rows":
                        a.wait_ge(decay_bound, p + 1)
                        a.activation(decay[:, js(p), :], decay[:, js(p), :], ACT.Exp).then_inc(decay_exp, 1)
                    elif step == "first":
                        a.wait_ge(t_turned, p + 1)
                        copy(Tm[:, js(p), :], pbank(p, P)).then_inc(t_first, 1)
                    elif step == "lx":
                        a.wait_ge(lx, n + 1)
                        copy(X_[:, js(p), :], pbank(p, P)).then_inc(lx_copied, 1)
                    elif step == "turn":
                        a.wait_ge(t_back, n + 1)
                        copy(TT_[:, js(p), :], pbank(p, P)).then_inc(tt_copied, 1)
                    elif step == "w":
                        a.wait_ge(w_prod, p + 1)
                        copy(W[:, js(p)].rearrange("p j h c -> p (j h c)"), ps[:, 4 + p, :]).then_inc(w_copied, 1)
                    elif step == "values":
                        a.wait_ge(v_prod, n + 1)
                        for h in range(2):
                            last = copy(vnew[HALF[h], p, h, :], ps[HALF[h], 4 + p, 0:P])
                        last.then_inc(v_copied, 1)
                    elif step == "outputs":
                        a.wait_ge(so_prod, n + 1)
                        if k < CHUNKS - 1:
                            a.wait_ge(s_ready, n + 1)
                        copy(oT[:, hs(p), 64 * k:64 * k + 64],
                             ps[:, 4 + p, P:2 * P].rearrange("p (h n) -> p h n", h=2)).then_inc(o_copied, 1)
                    elif step == "mixer":
                        for f in range(2):
                            a.wait_ge(pool_prod, p + 1)
                            a.activation(uT[:, 2 * p + f, :], ps[:, 4 + p, SEQ * f:SEQ * f + SEQ], ACT.Identity,
                                         scale=cols[:, PSC + 2 * p + f:PSC + 2 * p + f + 1]).then_inc(pool_out, 1)
                if step == "outputs" and k == CHUNKS - 1:
                    for p in range(PAIRS):
                        a.wait_ge(o_copied, PAIRS * k + p + 1)
                        a.activation(sq_o[:, hs(p), :], oT[:, hs(p), :], ACT.Square).then_inc(o_sq, 1)
                elif step == "o_sums":
                    a.wait_ge(o_sum, 1)
                    a.activation(g_ro, ps[:, 4, 0:16], ACT.Sqrt, scale=1.0 / P, bias=eps[:, 0:1]).then_inc(o_root, 1)
                    z_silu(0)
                elif step == "mix_split":
                    a.wait_ge(pool_out, 4 * k + 4)
                    a.wait_ge(slabs, 4 * 36 + 4 * (k + 1))
                    copy(act[:, 4 * k:4 * k + 4, 0:SEQ], uT[:, 4 * k:4 * k + 4, :]).then_inc(pool_hi, 1)

            def z_silu(n):
                for f in range(4):
                    a.wait_ge(evacuated, 32 + n + f + 1)
                    a.activation(zT[:, n + f, :], ub[:, f, PAD:], ACT.Silu).then_inc(silu_done, 1)

            def late_half(c):
                hi_half(24 + c // 2, 12 + c // 4, (c // 2) % 2, c % 2)

            late_half(0)
            late_half(1)
            post_tap(20, QW + 72 + 20, None)
            for f in range(4):
                a.wait_ge(convolved, 20 + f + 1)
                qkv_silu(10 + f // 2, f)
            for q in range(QUARTERS):
                if q in (16, 32, 48):
                    post_copy(20 + q // 4, 92 + q)
                if q in SCHEDULE:
                    act_step(*SCHEDULE[q])
                if q % 2:
                    late_half(q // 2 + 2)

            def heads_hi(p):
                a.wait_ge(o_gated, p + 1)
                a.wait_ge(slabs, 4 * 38 + 4 * (p // 2 + 1))
                copy(act[:, 8 + 2 * p:10 + 2 * p, 0:SEQ], oT[:, hs(p), :]).then_inc(o_hi, 1)

            post_copy(36, 156)
            hi(10, 1)
            z_silu(4)
            heads_hi(0)
            heads_hi(1)
            hi(10, 2)
            heads_hi(2)
            heads_hi(3)
            hi(10, 3)

            def act_out_block(b, i, first=False):
                hi(b, 0)
                post_copy(4 * b - 4, 16 * b - 4, None if first else (summed, 4 * i - 7))
                hi(b, 1)
                hi(b, 2)
                post_square(4 * i - 4, 4 * i - 4)
                hi(b, 3)

            act_out_block(11, 1, first=True)
            with a.Fori(2, 4) as i:
                act_out_block(i + 10, i)
            post_copy(52, 220, (summed, 9))
            post_square(12, 12)

            def root_act(n):
                a.wait_ge(sums_ready, n)
                a.activation(rstd[:, :], ps[:, 4, 0:SEQ], ACT.Sqrt, scale=1.0 / D, bias=eps[:, 0:1]).then_inc(root_ready, 1)

            root_act(1)
            for g in range(4):
                split_hi((yb, gb)[g % 2][:, :, :], g, 16)

            def act_up_block(b, i, prev, first=False):
                hi(b, 0)
                if prev is not None:
                    free = (product_lo, 4 * i - 3) if prev == "gate" and not first else None
                    post_copy(4 * b - 4, 16 * b - 4, free)
                hi(b, 1)
                if prev is not None:
                    t = 4 * i + (44 if prev == "value" else 0)
                    post_tap(4 * b - 4, CW + 176 + t, CB + t)
                hi(b, 2)
                if prev == "gate":
                    for f in range(4):
                        a.wait_ge(convolved, 24 + 8 * i + f + 1)
                        if not first:
                            a.wait_ge(product, 4 * i - 3 + f)
                        a.activation(gb[:, f, :], yb[:, f, :], ACT.Silu).then_inc(silu_done, 1)
                hi(b, 3)
                if prev == "value":
                    product_split_hi(i)

            def product_split_hi(i):
                for f in range(4):
                    a.wait_ge(product, 4 * i + f + 1)
                    copy(fact[:, bass.ds(4 * i + f, 1), 0:SEQ], yb[:, f:f + 1, :]).then_inc(product_hi, 1)

            act_up_block(UP_B, 0, None)
            act_up_block(UP_B + 1, 0, "gate", first=True)
            with a.Fori(0, 10) as i:
                act_up_block(UP_B + 2 + 2 * i, i, "value")
                act_up_block(UP_B + 3 + 2 * i, i + 1, "gate")

            def down_pair(half, i):
                for n in range(2):
                    for h in range(2):
                        hi_half(DOWN_U + DOWN_STEPS * half + 2 * i + n, (DOWN_U + DOWN_STEPS * half) // 2 + i, n, h, 2)

            def down_posts(half, free0):
                t, slab = DOWN_T + 8 * half, 4 * (DOWN_U + DOWN_STEPS * (half + 1)) - 4
                post_copy(t, slab, free0, bank=0, step=2)
                post_square(8 * half, 16 + 8 * half)
                post_copy(t + 4, slab + 2, (summed, 16 + 8 * half + 1), bank=4, step=2)
                post_square(8 * half + 4, 16 + 8 * half + 4)

            def pair_and_posts_0():
                hi_half(DOWN_U, DOWN_U // 2, 0, 0, 2)
                hi_half(DOWN_U, DOWN_U // 2, 0, 1, 2)
                post_copy(4 * DOWN_B - 4, 16 * DOWN_B - 4)
                hi_half(DOWN_U + 1, DOWN_U // 2, 1, 0, 2)
                hi_half(DOWN_U + 1, DOWN_U // 2, 1, 1, 2)
                post_tap(4 * DOWN_B - 4, CW + 176 + 84, CB + 84)
                down_pair(0, 1)
                product_split_hi(10)

            pair_and_posts_0()
            with a.Fori(2, DOWN_STEPS // 2) as i:
                down_pair(0, i)
            down_pair(1, 0)
            down_posts(0, (product_lo, 41))
            with a.Fori(1, DOWN_STEPS // 2) as i:
                down_pair(1, i)
            down_posts(1, (summed, 16 + 5))
            root_act(2)
            for n in range(0, 8, 2):
                a.wait_ge(y_turned, n + 1)
                copy(raw[:, n // 4, 512 * (n % 4):512 * (n % 4) + 512], ps[:, n, :]).then_inc(y_copied[0], 1)

        @block.vector
        def _(v):
            def lo_half(u2, slot, h, k=4):
                v.wait_ge(hi_split, u2 + 1)
                v.tensor_tensor(halves(w_lo, slot, h, k), halves(raw, slot, h, k),
                                halves(w_hi, slot, h, k).bitcast(F32), ALU.subtract).then_inc(lo_split, 1)

            def lo(b, i, k=4):
                for h in range(2):
                    lo_half(8 * b + 2 * i + h, i % 2, h, k)

            def post_add(t, used=None, bank=0):
                for f in range(4):
                    v.wait_ge(copied, t + f + 1)
                    if used is not None:
                        v.wait_ge(used[0], used[1] + f)
                    v.tensor_tensor(ub[:, f, PAD:], ps[:, bank + f, 0:256], yb[:, f, :], ALU.add).then_inc(evacuated, 1)

            def tap(f, back, weight, done, n):
                v.scalar_tensor_tensor(out=yb[:, f, :], in0=ub[:, f, PAD - back:PAD - back + SEQ],
                                       scalar=cols[:, bass.ds(weight + f, 1)], in1=yb[:, f, :],
                                       op0=ALU.mult, op1=ALU.add).then_inc(done, 1)

            def conv_qkv(t):
                for f in range(4):
                    v.wait_ge(tapped, t + f + 1)
                    tap(f, 1, QW + 48 + t, tap1, t)
                for f in range(4):
                    v.wait_ge(tap1, t + f + 1)
                    tap(f, 2, QW + 24 + t, tap2, t)
                for f in range(4):
                    v.wait_ge(tap2, t + f + 1)
                    tap(f, 3, QW + t, convolved, t)

            def conv_ffn(n, t):
                for f in range(4):
                    v.wait_ge(tapped, 24 + n + f + 1)
                    tap(f, 1, CW + 88 + t, tap1, t)
                for f in range(4):
                    v.wait_ge(tap1, 24 + n + f + 1)
                    tap(f, 2, CW + t, convolved, t)

            def post_residual(t, n, evac):
                for f in range(4):
                    v.wait_ge(evacuated, evac + f + 1)
                    x_t = xT[:, bass.ds(t + f, 1), :]
                    v.tensor_tensor(x_t, x_t, ub[:, f:f + 1, PAD:], ALU.add).then_inc(residual, 1)

            def post_sum(n, first=False):
                for f in range(4):
                    v.wait_ge(squared, n + f + 1)
                    if first and f == 0:
                        v.tensor_copy(sumsq[:, :], yb[:, f, :]).then_inc(summed, 1)
                    else:
                        v.wait_ge(summed, n + f)
                        v.tensor_tensor(sumsq[:, :], sumsq[:, :], yb[:, f, :], ALU.add).then_inc(summed, 1)

            def split_lo(group, g, n):
                v.wait_ge(act_hi, n + g + 1)
                v.tensor_tensor(act[:, 4 * g:4 * g + 4, SEQ:], group, act[:, 4 * g:4 * g + 4, 0:SEQ].bitcast(F32),
                                ALU.subtract).then_inc(act_lo, 1)

            for i in range(1, 8, 2):
                v.wait_ge(x_turned, i + 1)
                v.tensor_copy(xT[:, 2 * i:2 * i + 2, :], ps[:, i, :].rearrange("p (t n) -> p t n", n=SEQ)).then_inc(x_copied_dve, 1)
            v.wait_ge(x_root, 1)
            v.reciprocal(sq_acc[:, :], sq_acc[:, :]).then_inc(x_rstd, 1)
            v.wait_ge(x_rstd, 1)
            v.wait_ge(cst_loaded, 48)
            for t in range(TT):
                v.tensor_scalar(rdiag[:, t, :], ident[:, :], sq_acc[:, t:t + 1], None, ALU.mult).then_inc(x_diag, 1)
            v.wait_ge(par_turned, 1)
            v.tensor_copy(cols[:, :], ps[:, 0, 0:505]).then_inc(cols_ready, 1)
            v.wait_ge(cols_ready, 1)
            v.wait_ge(rstd_rows, 1)
            v.wait_ge(x_turned, 8)
            v.wait_ge(x_squared, 2)
            v.wait_ge(x_copied_act, 4)
            v.wait_ge(x_copied_dve, 4)
            for t in range(KD):
                v.scalar_tensor_tensor(out=h32[:, t, :], in0=xT[:, t, :], scalar=cols[:, N1 + t:N1 + t + 1],
                                       in1=ps[:, 1, 0:SEQ], op0=ALU.mult, op1=ALU.mult).then_inc(normed, 1)
            for g in range(4):
                split_lo(h32[:, 4 * g:4 * g + 4, :], g, 0)
            for i in range(4):
                lo(0, i)

            chained = [0]

            def link(ins):
                chained[0] += 1
                ins.then_inc(gate_chain, 1)
                v.wait_ge(gate_chain, chained[0])

            def gates_dve():
                heads = g_in.rearrange("p (k j c) -> p k j c", k=2, c=CHUNKS)
                v.wait_ge(logits_turned, 1)
                for h in range(2):
                    last = v.tensor_copy(heads[HALF[h]], ps[HALF[h], 5, 0:64].rearrange(
                        "p (c k j h) -> p h k j c", c=CHUNKS, k=2, h=2)[:, h])
                link(last)
                v.wait_ge(par_loaded, 16 * 13)
                for h in range(2):
                    bias = dt8[HALF[h]].rearrange("p (j h) -> p h j", h=2)[:, h]
                    last = v.tensor_tensor(heads[HALF[h], 1], heads[HALF[h], 1], over(bias, CHUNKS), ALU.add)
                link(last)
                y = g_in[:, 16:32]
                v.scalar_tensor_tensor(out=g_t2, in0=y, scalar=-1.0, in1=y, op0=ALU.mult, op1=ALU.min).then_inc(minus_abs, 1)
                v.wait_ge(gate_log, 1)
                link(v.tensor_scalar(g_t1, g_t1, 1.0, None, ALU.add))
                link(v.reciprocal(g_beta, g_t1))
                link(v.scalar_tensor_tensor(out=g_t3, in0=y, scalar=0.0, in1=g_t2, op0=ALU.max, op1=ALU.add))
                for h in range(2):
                    ea = al8[HALF[h]].rearrange("p (j h) -> p h j", h=2)[:, h]
                    sp_h = g_t3[HALF[h]].rearrange("p (j c) -> p j c", c=CHUNKS)
                    last = v.scalar_tensor_tensor(out=g_g[HALF[h]].rearrange("p (j c) -> p j c", c=CHUNKS), in0=sp_h, scalar=-1.0,
                                                  in1=over(ea, CHUNKS), op0=ALU.mult, op1=ALU.mult)
                last.then_inc(log_decay, 1)

            def dve_qkv_block(i, gates=False, first=False, sums=False):
                lo(i, 0)
                post_add(4 * i - 4, None if first else (convolved, 4 * i - 7))
                lo(i, 1)
                conv_qkv(4 * i - 4)
                if gates:
                    gates_dve()
                lo(i, 2)
                if sums:
                    v.wait_ge(decay_sums, 1)
                    link(v.tensor_copy(g_sum, ps[:, 5, 64:128]))
                    v.tensor_tensor(g_kt, g_tot, g_cum, ALU.subtract).then_inc(decay_summed, 1)
                lo(i, 3)

            v.wait_ge(filled, 1)
            dve_qkv_block(1, gates=True, first=True)
            with v.Fori(2, 5) as i:
                dve_qkv_block(i)
            dve_qkv_block(5, sums=True)

            post_add(20, (convolved, 17))
            v.wait_ge(qk_root, 1)
            v.reciprocal(g_norm, g_norm).then_inc(qk_inv, 1)
            v.wait_ge(qk_inv, 1)
            v.tensor_tensor(g_brk, g_beta, g_rk, ALU.mult).then_inc(norm_cols, 1)
            v.tensor_scalar(g_qs, g_rq, QSCALE, None, ALU.mult).then_inc(norm_cols, 1)
            v.wait_ge(norm_cols, 2)
            v.wait_ge(decay_exps, 3)
            v.tensor_tensor(g_eq, g_eg, g_qs, ALU.mult).then_inc(norm_cols, 1)
            v.scalar_tensor_tensor(out=g_nbeg, in0=g_brk, scalar=-1.0, in1=g_eg, op0=ALU.mult, op1=ALU.mult)
            v.tensor_tensor(g_kt, g_kt, g_rk, ALU.mult).then_inc(gates_ready, 1)

            def dve_step(step, k):
                if step == "decay_rows":
                    for p in range(PAIRS):
                        v.wait_ge(decay_rows, p + 1)
                        v.tensor_tensor(decay[:, js(p), :], ps[:, 4 + p, 0:SEQ].rearrange("p (j n) -> p j n", n=64),
                                        over(g_cum[:, js(p)], 64), ALU.subtract).then_inc(decay_diff, 1)
                    for p in range(PAIRS):
                        v.wait_ge(decay_diff, p + 1)
                        v.tensor_scalar(decay[:, js(p), :], decay[:, js(p), :], 0.0, None, ALU.min).then_inc(decay_bound, 1)
                    v.wait_ge(diag_ready, 3)
                    for p in range(PAIRS):
                        v.wait_ge(decay_exp, p + 1)
                        v.tensor_tensor(decay[:, js(p), :], decay[:, js(p), :], qkt[:, js(p), :], ALU.mult).then_inc(decay_ready, 1)
                    for p in range(PAIRS):
                        v.wait_ge(decay_ready, p + 1)
                        v.tensor_tensor(bdec[:, js(p), :], ps[:, 4 + p, SEQ:].rearrange("p (j n) -> p j n", n=64),
                                        decay[:, js(p), :], ALU.mult).then_inc(beta_decay, 1)
                if step == "q_row":
                    for p in range(PAIRS):
                        v.wait_ge(q_row, p + 1)
                        v.tensor_tensor(qkt[:, js(p), :], ps[:, 4 + p, 0:SEQ].rearrange("p (j n) -> p j n", n=64),
                                        decay[:, js(p), :], ALU.mult).then_inc(q_decay, 1)
                if step == "kq":
                    v.wait_ge(zeroed, 1)
                    for p in range(PAIRS):
                        v.wait_ge(kq, p + 1)
                        v.wait_ge(beta_decay, p + 1)
                        for h in range(2):
                            last = v.tensor_tensor(LT[HALF[h], js(p), 64 * h:64 * h + 64], pbank(p, P)[HALF[h], :, 64:128],
                                                   bdec[HALF[h], js(p), :], ALU.mult)
                        last.then_inc(lt_ready, 1)
                        v.wait_ge(q_decay, p + 1)
                        v.tensor_tensor(qkt[:, js(p), :], pbank(p, P)[:, :, 0:64], qkt[:, js(p), :], ALU.mult).then_inc(qkt_ready, 1)
                    for p in range(PAIRS):
                        v.wait_ge(lt_ready, p + 1)
                        v.tensor_tensor(TT_[:, js(p), :], LT[:, js(p), :], times(cst[:, C_NM + 5 * P:C_NM + 6 * P], CHUNKS),
                                        ALU.mult).then_inc(tt_part, 1)
                    for p in range(PAIRS):
                        v.wait_ge(tt_part, p + 1)
                        v.tensor_tensor(TT_[:, js(p), :], TT_[:, js(p), :], times(ident[:, :], CHUNKS), ALU.add).then_inc(tt_first, 1)
                if step == "qg_rows":
                    for p in range(PAIRS):
                        v.wait_ge(qg_rows, p + 1)
                        q = by_problem[:, p]
                        for h in range(2):
                            last = v.tensor_tensor(q[:, :, h, :], ps[:, 4 + p, SEQ * h:SEQ * h + SEQ].rearrange("p (c n) -> p c n", n=64),
                                                   q[:, :, h, :], ALU.mult)
                        last.then_inc(qg_ready, 1)
                if step == "join":
                    for p in range(PAIRS):
                        v.wait_ge(tlt, PAIRS * k + p + 1)
                        t_ = (Tm, TT_)[k == len(LEVELS) - 1][:, js(p), :]
                        v.tensor_tensor(t_, t_, pbank(p, P), ALU.add).then_inc(t_joined, 1)
                if step == "k_tok":
                    v.wait_ge(gates_ready, 1)
                    for p in range(PAIRS):
                        v.wait_ge(k_tok, p + 1)
                        v.tensor_tensor(kg[:, js(p), :], pbank(p, P), over(g_nbeg[:, js(p)], P), ALU.mult)
                        v.tensor_tensor(ktail[:, js(p), :], pbank(p, P), over(g_kt[:, js(p)], P), ALU.mult).then_inc(k_scaled, 1)
                if step == "v_tok":
                    for p in range(PAIRS):
                        v.wait_ge(v_tok, p + 1)
                        v.tensor_tensor(vb[:, js(p), :], pbank(p, P), over(g_beta[:, js(p)], P), ALU.mult).then_inc(v_scaled, 1)
                if step == "outputs" and k < CHUNKS - 1:
                    for p in range(PAIRS):
                        v.wait_ge(so_prod, PAIRS * k + p + 1)
                        for h in range(2):
                            new = ps[:, 4 + p, 256 + P * h:256 + P * h + P]
                            j = CHUNKS * p + k
                            if k == 0:
                                last = v.tensor_copy(S[:, 2 * p + h, :], new)
                            else:
                                v.wait_ge(s_ready, PAIRS * k - PAIRS + p + 1)
                                last = v.scalar_tensor_tensor(out=S[:, 2 * p + h, :], in0=S[:, 2 * p + h, :], scalar=g_last[:, h, j:j + 1],
                                                              in1=new, op0=ALU.mult, op1=ALU.add)
                        last.then_inc(s_ready, 1)
                if step == "mix_split":
                    v.wait_ge(pool_hi, k + 1)
                    v.tensor_tensor(act[:, 4 * k:4 * k + 4, SEQ:], uT[:, 4 * k:4 * k + 4, :],
                                    act[:, 4 * k:4 * k + 4, 0:SEQ].bitcast(F32), ALU.subtract).then_inc(pool_lo, 1)
                if step == "o_sums":
                    v.wait_ge(o_root, 1)
                    v.reciprocal(g_ro, g_ro).then_inc(o_inv, 1)
                    v.wait_ge(o_inv, 1)
                    for p in range(PAIRS):
                        v.tensor_tensor(diag_o[:, 4 * p:4 * p + 4, :], times(ident[:, :], 4), over(g_ro[:, 4 * p:4 * p + 4], P),
                                        ALU.mult).then_inc(o_diag, 1)
                if step == "o_rows":
                    for p in range(PAIRS):
                        v.wait_ge(o_row, p + 1)
                        v.tensor_tensor(oT[:, hs(p), :], oT[:, hs(p), :], pbank(p, SEQ), ALU.mult).then_inc(o_normed, 1)
                    gate_heads(0)

            def gate_heads(g):
                v.wait_ge(silu_done, 28 + 4 * g)
                for p in (2 * g, 2 * g + 1):
                    v.wait_ge(o_normed, p + 1)
                    v.scalar_tensor_tensor(out=oT[:, hs(p), :], in0=oT[:, hs(p), :], scalar=cols[:, ONW:ONW + 1], in1=zT[:, hs(p), :],
                                           op0=ALU.mult, op1=ALU.mult).then_inc(o_gated, 1)

            def late_half(c):
                lo_half(48 + c, (c // 2) % 2, c % 2)

            late_half(0)
            late_half(1)
            conv_qkv(20)
            for q in range(QUARTERS):
                if q in (16, 32):
                    for f in range(4):
                        t = 20 + q // 4 + f
                        v.wait_ge(copied, t + 1)
                        v.tensor_tensor(uT[:, t - 24, :], ps[:, f, 0:256], yb[:, f, :], ALU.add).then_inc(evacuated, 1)
                if q == 48:
                    post_add(32)
                if q in SCHEDULE:
                    dve_step(*SCHEDULE[q])
                if q % 2:
                    late_half(q // 2 + 2)

            def heads_lo(p):
                v.wait_ge(o_hi, p + 1)
                v.tensor_tensor(act[:, 8 + 2 * p:10 + 2 * p, SEQ:], oT[:, hs(p), :], act[:, 8 + 2 * p:10 + 2 * p, 0:SEQ].bitcast(F32),
                                ALU.subtract).then_inc(o_lo, 1)

            post_add(36, (silu_done, 25))
            lo(10, 1)
            heads_lo(0)
            heads_lo(1)
            gate_heads(1)
            lo(10, 2)
            heads_lo(2)
            heads_lo(3)
            lo(10, 3)

            def dve_out_block(b, i, first=False):
                lo(b, 0)
                post_add(4 * b - 4, (silu_done, 29) if first else (residual, 4 * i - 7))
                lo(b, 1)
                post_residual(4 * i - 4, 4 * i - 4, 4 * b - 4)
                lo(b, 2)
                lo(b, 3)
                post_sum(4 * i - 4, first)

            dve_out_block(11, 1, first=True)
            with v.Fori(2, 4) as i:
                dve_out_block(i + 10, i)
            post_add(52, (residual, 9))
            post_residual(12, 12, 52)
            post_sum(12)

            v.wait_ge(root_ready, 1)
            v.reciprocal(rstd[:, :], rstd[:, :]).then_inc(rstd_ready, 1)
            v.wait_ge(rstd_ready, 1)
            group = (yb, gb)
            for g in range(5):
                if g in (2, 3):
                    v.wait_ge(act_lo, 4 + g - 1)
                if g < 4:
                    for f in range(4):
                        t = 4 * g + f
                        v.scalar_tensor_tensor(out=group[g % 2][:, f, :], in0=xT[:, t, :], scalar=cols[:, N2 + t:N2 + t + 1],
                                               in1=rstd[:, :], op0=ALU.mult, op1=ALU.mult).then_inc(normed, 1)
                if g:
                    split_lo(group[(g - 1) % 2][:, :, :], g - 1, 4)

            def dve_up_block(b, i, prev, first=False):
                lo(b, 0)
                if prev is not None:
                    post_add(4 * b - 4, (residual, 13) if first else (convolved, 24 + 8 * i + (1 if prev == "value" else -3)))
                lo(b, 1)
                if prev is not None:
                    conv_ffn(8 * i + (4 if prev == "value" else 0), 4 * i + (44 if prev == "value" else 0))
                lo(b, 2)
                if prev == "value":
                    products(i)
                lo(b, 3)
                if prev == "value":
                    product_split_lo(i)

            def products(i):
                for f in range(4):
                    v.wait_ge(convolved, 24 + 8 * i + 4 + f + 1)
                    v.wait_ge(silu_done, 32 + 4 * i + f + 1)
                    v.tensor_tensor(yb[:, f, :], yb[:, f, :], gb[:, f, :], ALU.mult).then_inc(product, 1)

            def product_split_lo(i):
                for f in range(4):
                    v.wait_ge(product_hi, 4 * i + f + 1)
                    k = bass.ds(4 * i + f, 1)
                    v.tensor_tensor(fact[:, k, SEQ:], yb[:, f:f + 1, :], fact[:, k, 0:SEQ].bitcast(F32),
                                    ALU.subtract).then_inc(product_lo, 1)

            dve_up_block(UP_B, 0, None)
            dve_up_block(UP_B + 1, 0, "gate", first=True)
            with v.Fori(0, 10) as i:
                dve_up_block(UP_B + 2 + 2 * i, i, "value")
                dve_up_block(UP_B + 3 + 2 * i, i + 1, "gate")

            def down_pair(half, i):
                for n in range(2):
                    for h in range(2):
                        lo_half(2 * (DOWN_U + DOWN_STEPS * half + n) + 4 * i + h, n, h, 2)

            lo_half(2 * DOWN_U, 0, 0, 2)
            lo_half(2 * DOWN_U + 1, 0, 1, 2)
            post_add(4 * DOWN_B - 4, (convolved, 24 + 81))
            lo_half(2 * DOWN_U + 2, 1, 0, 2)
            lo_half(2 * DOWN_U + 3, 1, 1, 2)
            conv_ffn(84, 84)
            products(10)
            down_pair(0, 1)
            product_split_lo(10)
            with v.Fori(2, DOWN_STEPS // 2) as i:
                down_pair(0, i)

            def down_posts(half, used):
                t = DOWN_T + 8 * half
                post_add(t, used, bank=0)
                post_residual(8 * half, 16 + 8 * half, t)
                post_sum(16 + 8 * half, half == 0)
                post_add(t + 4, (residual, 16 + 8 * half + 1), bank=4)
                post_residual(8 * half + 4, 16 + 8 * half + 4, t + 4)
                post_sum(16 + 8 * half + 4)

            down_pair(1, 0)
            down_posts(0, (convolved, 24 + 85))
            with v.Fori(1, DOWN_STEPS // 2) as i:
                down_pair(1, i)
            down_posts(1, (residual, 21))

            v.wait_ge(root_ready, 2)
            v.reciprocal(rstd[:, :], rstd[:, :]).then_inc(rstd_ready, 1)
            v.wait_ge(rstd_ready, 2)
            for t in range(KD):
                v.scalar_tensor_tensor(out=xT[:, t, :], in0=xT[:, t, :], scalar=cols[:, NF + t:NF + t + 1],
                                       in1=rstd[:, :], op0=ALU.mult, op1=ALU.mult).then_inc(y_normed, 1)
            for n in range(1, 8, 2):
                v.wait_ge(y_turned, n + 1)
                v.tensor_copy(raw[:, n // 4, 512 * (n % 4):512 * (n % 4) + 512], ps[:, n, :]).then_inc(y_copied[1], 1)

        @block.tensor
        def _(t_e):
            t = t_e

            def slab(slot, f, k, x, start, stop, bank):
                n_cols = 2048 // k
                wh = w_hi[:, slot, :].rearrange("p (k n) -> p k n", k=k)
                wl = w_lo[:, slot, :].rearrange("p (k n) -> p k n", k=k)
                for n in range(k):
                    c = slice(P * f, P * f + P)
                    t.matmul(ps[:, bank, :], wh[:, n, c], x[n], start=start and n == 0, stop=False)
                    last = t.matmul(ps[:, bank, 0:SEQ], wl[:, n, c], x[n][:, 0:SEQ], start=False, stop=stop and n == k - 1)
                return last

            def quarter(b, i, f):
                if f % 2 == 0:
                    t.wait_ge(lo_split, 8 * b + 2 * i + f // 2 + 1)
                if i == 0 and not (isinstance(b, int) and b == 0):
                    t.wait_ge(evacuated, 4 * b + f - 3)
                slab(i % 2, f, 4, [act[:, 4 * i + n, :] for n in range(4)], i == 0, i == 3, f).then_inc(slabs, 1)

            def unit(b, i):
                for f in range(4):
                    quarter(b, i, f)

            t.wait_ge(cst_loaded, 48)
            t.wait_ge(x_loaded, 32)
            for i in range(8):
                for n in range(4):
                    last = t.transpose(ps[:, i, P * n:P * n + P], xtok[:, n % 2, P * (2 * i + n // 2):P * (2 * i + n // 2) + P], ident[:, :])
                last.then_inc(x_turned, 1)
            t.wait_ge(par_loaded, 16 * 13)
            t.wait_ge(x_copied_act, 1)
            at = 0
            for tile, rows in enumerate((57, 88, 88, 88, 88, 96)):
                last = t.transpose(ps[:, 0, at:at + rows], staged[0:rows, tile, :], ident[0:rows, 0:rows])
                at += rows
            last.then_inc(par_turned, 1)
            t.wait_ge(x_copied_dve, 1)
            for n in range(TT):
                t.wait_ge(x_diag, n + 1)
                last = t.matmul(ps[:, 1, P * n:P * n + P], ones[:, :], rdiag[:, n, :], start=True, stop=True)
            last.then_inc(rstd_rows, 1)
            t.wait_ge(normed, KD)
            t.wait_ge(x_copied_act, 3)
            for k in range(KD):
                last = t.matmul(ps[0:16, 4, 0:SEQ], w_log[:, k, :], h32[:, k, :], start=k == 0, stop=k == KD - 1)
            last.then_inc(logits, 1)
            t.wait_ge(cols_ready, 1)
            t.wait_ge(x_copied_act, 4)
            t.wait_ge(x_copied_dve, 4)
            for i in range(4):
                t.wait_ge(act_lo, i + 1)
                unit(0, i)
            t.wait_ge(logits_twice, 1)
            for c in range(CHUNKS):
                last = t.matmul(ps[:, 5, 16 * c:16 * c + 16], lgd[:, c].rearrange("p d n -> p (d n)"), ident[0:16, 0:16],
                                start=True, stop=True)
            last.then_inc(logits_turned, 1)
            with t.Fori(1, 5) as b:
                for i in range(4):
                    unit(b, i)

            t.wait_ge(log_decay, 1)
            t.matmul(ps[:, 5, 64:80], cst[:, C_TRI:C_TRI + P], g_g, start=True, stop=True)
            t.matmul(ps[:, 5, 80:96], cst[:, C_BLOCK:C_BLOCK + P], g_g, start=True, stop=True)
            for h in range(2):
                last = t.matmul(ps[:, 5, 96 + 16 * h:112 + 16 * h], cst[:, C_HALF + P * h:C_HALF + P * h + P], g_g, start=True, stop=True)
            last.then_inc(decay_sums, 1)
            for i in range(4):
                unit(5, i)
            for k, sq in enumerate((sq_q, sq_k)):
                t.wait_ge(qk_sq, k + 1)
                for j in range(J):
                    last = t.matmul(ps[:, 5, 128 + 16 * k + j:129 + 16 * k + j], sq[:, P * j:P * j + P], ones[:, 0:1], start=True, stop=True)
            last.then_inc(qk_sum, 1)

            def broadcast(out, lhsT, diag, p):
                return t.matmul(out, lhsT, diag[:, js(p), :].rearrange("p j n -> p (j n)"), start=True, stop=True)

            def pe_step(step, k):
                for p in range(PAIRS):
                    bank = 4 + p
                    n = PAIRS * k + p
                    if step == "decay_rows":
                        t.wait_ge(diag_ready, 2)
                        t.wait_ge(gates_ready, 1)
                        broadcast(ps[:, bank, 0:SEQ], cst[:, C_BLOCK:C_BLOCK + P], diag_g, p)
                        broadcast(ps[:, bank, SEQ:], cst[:, C_BLOCK:C_BLOCK + P], diag_b, p).then_inc(decay_rows, 1)
                    elif step == "q_row":
                        t.wait_ge(diag_ready, 4)
                        t.wait_ge(beta_decay, p + 1)
                        broadcast(ps[:, bank, 0:SEQ], cst[:, C_BLOCK:C_BLOCK + P], diag_q, p).then_inc(q_row, 1)
                    elif step == "kq":
                        t.wait_ge(silu_done, 16)
                        t.wait_ge(q_decay, p + 1)
                        for c in range(CHUNKS):
                            for h in range(2):
                                last = t.matmul(ps[HALF[h], bank, P * c:P * c + P].rearrange("p (a n) -> p a n", a=2),
                                                by_problem[:, PAIRS + p, c, h, :], by_problem[:, p:PAIRS + p + 1:PAIRS, c, h, :],
                                                start=True, stop=True)
                        last.then_inc(kq, 1)
                    elif step == "qg_rows":
                        t.wait_ge(diag_ready, 5)
                        t.wait_ge(qkt_ready, p + 1)
                        for h in range(2):
                            last = broadcast(ps[:, bank, SEQ * h:SEQ * h + SEQ], cst[:, C_HALF + P * h:C_HALF + P * h + P], diag_eq, p)
                        last.then_inc(qg_rows, 1)
                    elif step == "first":
                        t.wait_ge(tt_first, p + 1)
                        t.wait_ge(qg_ready, p + 1)
                        for c in range(CHUNKS):
                            last = t.transpose(ps[:, bank, P * c:P * c + P], TT_[:, CHUNKS * p + c, :], ident[:, :])
                        last.then_inc(t_turned, 1)
                    elif step in ("lx", "join", "turn"):
                        if step == "lx":
                            t.wait_ge(l_masked, n + 1)
                            t.wait_ge(tt_copied if k else t_first, n - PAIRS + 1 if k else p + 1)
                        elif step == "join":
                            t.wait_ge(lx_copied, n + 1)
                        else:
                            t.wait_ge(t_joined, n + 1)
                        for c in range(CHUNKS):
                            j = CHUNKS * p + c
                            o = ps[:, bank, P * c:P * c + P]
                            if step == "lx":
                                last = t.matmul(o, masked[:, j, :], Tm[:, j, :], start=True, stop=True)
                            elif step == "turn":
                                last = t.transpose(o, Tm[:, j, :], ident[:, :])
                            elif k < len(LEVELS) - 1:
                                last = t.matmul(o, TT_[:, j, :], X_[:, j, :], start=True, stop=True)
                            else:
                                last = t.matmul(o, X_[:, j, :], TT_[:, j, :], start=True, stop=True)
                        last.then_inc({"lx": lx, "join": tlt, "turn": t_back}[step], 1)
                    elif step in ("k_tok", "v_tok"):
                        if step == "k_tok":
                            t.wait_ge(t_joined, PAIRS * (len(LEVELS) - 1) + p + 1)
                        else:
                            t.wait_ge(k_scaled, p + 1)
                            t.wait_ge(silu_done, 24)
                        for c in range(CHUNKS):
                            tokens = by_problem[:, (PAIRS if step == "k_tok" else 2 * PAIRS) + p, c]
                            last = t.transpose(ps[:, bank, P * c:P * c + P], tokens.rearrange("p h n -> p (h n)"), ident[:, :])
                        last.then_inc(k_tok if step == "k_tok" else v_tok, 1)
                    elif step == "w":
                        t.wait_ge(v_scaled, p + 1)
                        for c in range(CHUNKS):
                            last = t.matmul(ps[:, bank, P * c:P * c + P], kg[:, CHUNKS * p + c, :], TT_[:, CHUNKS * p + c, :],
                                            start=True, stop=True)
                        last.then_inc(w_prod, 1)
                    elif step == "values":
                        j = CHUNKS * p + k
                        t.wait_ge(o_copied if k else w_copied, n - PAIRS + 1 if k else p + 1)
                        last = t.matmul(ps[:, bank, 0:P], TT_[:, j, :], vb[:, j, :], start=True, stop=k == 0)
                        if k:
                            t.wait_ge(s_ready, n - PAIRS + 1)
                            for h in range(2):
                                last = t.matmul(ps[HALF[h], bank, 0:P], W[:, j, h, :], S[:, 2 * p + h, :], start=False, stop=True)
                        last.then_inc(v_prod, 1)
                    elif step == "outputs":
                        j = CHUNKS * p + k
                        t.wait_ge(v_copied, n + 1)
                        for h in range(2):
                            o = ps[:, bank, P + 64 * h:P + 64 * h + 64]
                            if k:
                                t.matmul(o, S[:, 2 * p + h, :], by_problem[:, p, k, h, :], start=True, stop=False)
                            last = t.matmul(o, vnew[:, p, h, :], qkt[:, j, :], start=k == 0, stop=True)
                        if k < CHUNKS - 1:
                            last = t.matmul(ps[:, bank, 256:512], ktail[:, j, :], vnew[:, p, :, :].rearrange("p h n -> p (h n)"),
                                            start=True, stop=True)
                        last.then_inc(so_prod, 1)
                    elif step == "mixer":
                        t.wait_ge(pooled, p + 1)
                        t.wait_ge(pool_w_loaded, 16)
                        t.wait_ge(o_copied, PAIRS * (CHUNKS - 1) + p + 1)
                        for f in range(2):
                            for c in range(2):
                                last = t.matmul(ps[:, bank, SEQ * f:SEQ * f + SEQ], pw[:, p, c, P * f:P * f + P], uT[:, 2 * p + c, :],
                                                start=c == 0, stop=c == 1)
                        last.then_inc(pool_prod, 1)
                    elif step == "o_sums":
                        if p == 0:
                            t.wait_ge(pool_out, 2)
                        t.wait_ge(o_sq, p + 1)
                        for c in range(2 * TT):
                            last = t.matmul(ps[:, 4, 4 * p + c:4 * p + c + 1], sq_o[:, 2 * p + c // TT, P * (c % TT):P * (c % TT) + P],
                                            ones[:, 0:1], start=True, stop=True)
                        if p == PAIRS - 1:
                            last.then_inc(o_sum, 1)
                    elif step == "o_rows":
                        t.wait_ge(o_diag, p + 1)
                        t.wait_ge(pool_out, 2 * p + 2)
                        t.matmul(ps[:, bank, :], ones[:, :], diag_o[:, 4 * p:4 * p + 4, :].rearrange("p i n -> p (i n)"),
                                 start=True, stop=True).then_inc(o_row, 1)

            for q in range(QUARTERS):
                if q in SCHEDULE:
                    pe_step(*SCHEDULE[q])
                quarter(6 + q // 16, q // 4 % 4, q % 4)

            for i, (ready, n) in enumerate(((pool_lo, 1), (pool_lo, 2), (o_lo, 2), (o_lo, 4))):
                t.wait_ge(ready, n)
                unit(OUT_B, i)
            with t.Fori(OUT_B + 1, OUT_B + 4) as b:
                for i in range(4):
                    unit(b, i)

            def sums(n):
                t.wait_ge(summed, 16 * n)
                t.wait_ge(o_normed, PAIRS)
                t.matmul(ps[:, 4, 0:SEQ], ones[:, :], sumsq[:, :], start=True, stop=True).then_inc(sums_ready, 1)

            sums(1)
            for i in range(4):
                t.wait_ge(act_lo, 4 + i + 1)
                unit(UP_B, i)
            with t.Fori(UP_B + 1, UP_B + 22) as b:
                for i in range(4):
                    unit(b, i)

            def down_unit(half, i, n, start=False, stop=False):
                u2 = 2 * (DOWN_U + DOWN_STEPS * half + n) + 4 * i
                for h in range(2):
                    t.wait_ge(lo_split, u2 + h + 1)
                    for f in range(4 * h, 4 * h + 4):
                        if start:
                            if half == 0 and f < 4:
                                t.wait_ge(evacuated, DOWN_T - 4 + f + 1)
                            if half == 0 and f == 4:
                                t.wait_ge(root_ready, 1)
                            if half == 1:
                                t.wait_ge(evacuated, DOWN_T + f + 1)
                        x = [fact[:, bass.ds(4 * i + 2 * n + k, 1), :].rearrange("p a n -> p (a n)") for k in range(2)]
                        last = slab(n, f, 2, x, start, stop, f)
                        if f % 2:
                            last.then_inc(slabs, 1)

            for half in range(2):
                down_unit(half, 0, 0, start=True)
                down_unit(half, 0, 1)
                with t.Fori(1, DOWN_STEPS // 2 - 1) as i:
                    down_unit(half, i, 0)
                    down_unit(half, i, 1)
                if half == 0:
                    t.wait_ge(product_lo, KF)
                down_unit(half, DOWN_STEPS // 2 - 1, 0)
                down_unit(half, DOWN_STEPS // 2 - 1, 1, stop=True)
            t.wait_ge(evacuated, DOWN_T + 16)
            sums(2)
            for n in range(8):
                for k in range(4):
                    f = 4 * (n % 4) + k
                    t.wait_ge(y_normed, f + 1)
                    last = t.transpose(ps[:, n, P * k:P * k + P], xT[:, f, P * (n // 4):P * (n // 4) + P], ident[:, :])
                last.then_inc(y_turned, 1)


_INS = ["x", "norm1_w", "w_in", "conv_qkv_w", "a_log", "dt_bias", "out_norm_w", "pool_w", "pool_scale",
        "w_out", "norm2_w", "w_up", "conv_ffn_w", "conv_ffn_b", "w_down", "final_norm_w"]


def kernel(**inputs):
    import numpy as np
    import concourse.bacc as bacc
    from concourse.bass_utils import run_bass_kernel_spmd

    nc = bacc.Bacc("TRN2", target_bir_lowering=False, num_devices=1)
    arrays, args = {}, []
    for name in _INS:
        arrays[f"in_{name}"] = np.ascontiguousarray(inputs[name])
    arrays["in_table"] = constants()
    for name, a in arrays.items():
        args.append(nc.dram_tensor(name, a.shape, mybir.dt.from_np(a.dtype), kind="ExternalInput").ap())
    shape = arrays["in_x"].shape
    args.append(nc.dram_tensor("out_y", shape, F32, kind="ExternalOutput").ap())
    hybrid_layer(nc, *args)
    r = run_bass_kernel_spmd(nc, [arrays], core_ids=[0])
    return r.results[0]["out_y"]
```

```python
from contextlib import ExitStack

import concourse.bass as bass
from concourse import mybir

F32 = mybir.dt.float32
F32R = mybir.dt.float32r
ALU = mybir.AluOpType
ACT = mybir.ActivationFunctionType

P = 128
EPS = 1e-6
PAD = 3
LEVELS = (2, 4, 8, 16, 32)
WINDOWS = (2, 4, 8, 16)

C_NM = 0
C_CAUSAL = C_NM + 6 * P
C_EYE2 = C_CAUSAL + 64
C_TRI = C_EYE2 + 64
C_HALF = C_TRI + P
C_BLOCK = C_HALF + 64
C_COUNT = C_HALF + 2 * P
C_IDENT = C_COUNT + 64
C_ONES = C_IDENT + P
C_ALL = C_ONES + P


def constants():
    import numpy as np

    c = np.zeros((P, C_ALL), np.float32)
    i = np.arange(P)
    for n, s in enumerate(LEVELS + (1,)):
        row, col = i[:, None] // s, i[None, :] // s
        m = ((row % 2 == 1) & (col == row - 1)).astype(np.float32)
        c[:, C_NM + n * P:C_NM + (n + 1) * P] = -m.T
    m, t = (i % 64)[:, None], np.arange(64)[None, :]
    c[:, C_CAUSAL:C_CAUSAL + 64] = t >= m
    c[:, C_EYE2:C_EYE2 + 64] = t == m
    same = (i[:, None] // 64) == (i[None, :] // 64)
    c[:, C_TRI:C_TRI + P] = same & (i[:, None] <= i[None, :])
    c[:64, C_HALF:C_HALF + P] = 1.0
    c[64:, C_HALF + P:C_HALF + 2 * P] = 1.0
    for g, w in enumerate(WINDOWS):
        c[:, C_COUNT + 16 * g:C_COUNT + 16 * g + 16] = 1.0 / np.minimum(np.arange(16) + 1.0, w)
    c[:, C_IDENT:C_IDENT + P] = np.eye(P)
    c[:, C_ONES:C_ONES + P] = 1.0
    return c


def hybrid_layer(nc, x, norm1_w, w_in, conv_qkv_w, a_log, dt_bias, out_norm_w, pool_w, pool_scale,
                 w_out, norm2_w, w_up, conv_ffn_w, conv_ffn_b, w_down, final_norm_w, table, out):
    SEQ, D = x.shape[1], x.shape[2]
    HEADS = a_log.shape[1]
    DN = HEADS * P
    FF = w_down.shape[1]
    KD = D // P
    KF = FF // P
    TT = SEQ // P
    PAIRS, CHUNKS = HEADS // 2, SEQ // 64
    J = PAIRS * CHUNKS
    QSCALE = float(P) ** -0.5
    assert (SEQ, D, HEADS, FF) == (256, 2048, 8, 5632)

    OUT_B, UP_B, DOWN_B = 10, 14, 36
    DOWN_U, DOWN_T = 4 * DOWN_B, 4 * DOWN_B
    DOWN_STEPS = KF // 4
    PASSES = KD // 4
    IN_COLS = [512 * i for i in range(6)] + [4 * DN + 2 * HEADS + 512 * i for i in range(2)] \
        + [3 * DN + 512 * i for i in range(2)]

    w_in2, w_out2, w_up2, w_down2 = w_in[0], w_out[0], w_up[0], w_down[0]
    x2, out2 = x[0], out[0]

    ctx = ExitStack()
    phase_a = ExitStack()
    with ctx:
        def sb(name, shape, dt=F32, where=ctx):
            return where.enter_context(nc.sbuf_tensor(name, shape, dt))

        def sem(name):
            return ctx.enter_context(nc.semaphore(name))

        ps = ctx.enter_context(nc.psum_tensor("ps", [P, 8, 512], F32))

        raw = sb("raw", [P, 2, 2048])
        w_hi = sb("w_hi", [P, 2, 2048], F32R)
        w_lo = sb("w_lo", [P, 2, 2048], F32R)
        act = sb("act", [P, KD, 512], F32R)
        xT = sb("xT", [P, KD, SEQ])
        cols = sb("cols", [P, 505])
        ident = sb("ident", [P, P])
        ones = sb("ones", [P, P])
        yb = sb("yb", [P, 4, SEQ])
        ub = sb("ub", [P, 4, PAD + SEQ])
        eps = sb("eps", [P, 1])
        sumsq = sb("sumsq", [P, SEQ])
        rstd = sb("rstd", [P, SEQ])
        y_rstd = sb("y_rstd", [P, TT])

        cst = sb("cst", [P, C_IDENT], F32, phase_a)
        qkv = sb("qkv", [P, 3, HEADS, SEQ], F32, phase_a)
        zT = sb("zT", [P, HEADS, SEQ], F32, phase_a)
        uT = sb("uT", [P, HEADS, SEQ], F32, phase_a)
        scr = sb("scr", [P, 4, 2048], F32, phase_a)
        dt_s = sb("dt_s", [P, 1024], F32, phase_a)
        qkt = sb("qkt", [P, J, 64], F32, phase_a)
        masked = sb("masked", [P, J, P], F32, phase_a)
        vnew = sb("vnew", [P, PAIRS, 2, P], F32, phase_a)
        gates = sb("gates", [P, 16 * 14 + 16], F32, phase_a)
        sq_acc = sb("sq_acc", [P, 2], F32, phase_a)
        phase_a.close()
        fact = sb("fact", [P, KF, 512], F32R)
        gb = sb("gb", [P, 4, SEQ])

        xtok = scr[:, 0:2, :]
        h32 = scr[:, 0:2, :].rearrange("p a (t n) -> p (a t) n", n=SEQ)
        staged = scr[:, 2, 0:768].rearrange("p (i n) -> p i n", n=P)
        w_log = scr[:, 2, 1024:1280].rearrange("p (k n) -> p k n", n=16)
        lg = scr[0:16, 3, 0:256]
        lgd = scr[0:16, 3, 512:1024].rearrange("p (c d n) -> p c d n", c=CHUNKS, d=2)
        sqx = scr[:, 3, :]
        LT, Tm, TT_, X_ = (scr[:, i, :].rearrange("p (j n) -> p j n", n=P) for i in range(4))
        vb, kg, ktail = LT, Tm, X_
        sq_q, sq_k = scr[:, 3, :], scr[:, 2, :]
        diag_g = scr[:, 1, 0:1024].rearrange("p (j n) -> p j n", n=64)
        diag_b = scr[:, 1, 1024:2048].rearrange("p (j n) -> p j n", n=64)
        bdec = scr[:, 3, 0:1024].rearrange("p (j n) -> p j n", n=64)
        decay = dt_s[:, :].rearrange("p (j n) -> p j n", n=64)
        S = dt_s[:, :].rearrange("p (h n) -> p h n", n=P)
        diag_q, diag_eq = masked[:, 0:8].rearrange("p a n -> p (a n)").rearrange("p (j n) -> p j n", n=64), \
            masked[:, 8:16].rearrange("p a n -> p (a n)").rearrange("p (j n) -> p j n", n=64)
        win = masked[:, 0:8].rearrange("p a n -> p (a n)").rearrange("p (b k n) -> p b k n", b=2, k=2)
        by_problem = qkv[:, :, :, :].rearrange("p k h n -> p k (h n)").rearrange(
            "p k (j c h n) -> p (k j) c h n", j=PAIRS, c=CHUNKS, h=2)
        W = qkv[:, 1].rearrange("p h n -> p (h n)").rearrange("p (j h c) -> p j h c", j=J, h=2)
        oT = qkv[:, 2]
        pw = zT[:, :, :].rearrange("p h n -> p (h n)").rearrange("p (g k n) -> p g k n", g=4, k=2)
        rdiag = scr[:, 3, 1024:1280].rearrange("p (a n) -> p a n", n=P)
        sq_o = scr[:, 1, :].rearrange("p (c n) -> p c n", n=P)
        diag_o = scr[:, 3, :].rearrange("p (i n) -> p i n", n=P)

        def gcol(i, n=16):
            return gates[:, 16 * i:16 * i + n]

        g_in, g_beta, g_g = gates[:, 0:32], gcol(2), gcol(3)
        g_t1, g_t2, g_sum, g_eg, g_kt, g_nbeg = gcol(4), gcol(5), gcol(6, 64), gcol(10), gcol(11), gcol(12)
        g_cum, g_tot = g_sum[:, 0:16], g_sum[:, 16:32]
        g_last = g_sum[:, 32:64].rearrange("p (h j) -> p h j", h=2)
        al8, dt8 = gates[:, 208:216], gates[:, 216:224]
        g_t3 = gates[:, 224:240]
        g_norm = sumsq[:, 0:32]
        g_rq, g_rk, g_qs, g_brk, g_eq, g_ro = (sumsq[:, 16 * i:16 * i + 16] for i in range(6))

        N1, N2, NF, PSC, ONW, CB, CW, QW = 0, 16, 32, 48, 56, 57, 145, 409

        def over(ap, n):
            return ap.unsqueeze(2).to_broadcast([ap.shape[0], ap.shape[1], n])

        def times(ap, n):
            return ap.unsqueeze(1).to_broadcast([ap.shape[0], n, ap.shape[1]])

        def js(p):
            return slice(CHUNKS * p, CHUNKS * p + CHUNKS)

        def hs(p):
            return slice(2 * p, 2 * p + 2)

        def pbank(p, n):
            return ps[:, 4 + p, :].rearrange("p (c n) -> p c n", n=n)

        HALF = (slice(0, 64), slice(64, 128))

        raw_loaded = [sem("raw_loaded0"), sem("raw_loaded1")]
        hi_split, lo_split = sem("hi_split"), sem("lo_split")
        slabs = sem("slabs")
        copied = sem("copied")
        evacuated = sem("evacuated")
        tapped = sem("tapped")
        tap1, tap2 = sem("tap1"), sem("tap2")
        convolved = sem("convolved")
        silu_done = sem("silu_done")
        product = sem("product")
        product_hi, product_lo = sem("product_hi"), sem("product_lo")
        residual = sem("residual")
        squared, summed = sem("squared"), sem("summed")
        normed = sem("normed")
        act_hi, act_lo = sem("act_hi"), sem("act_lo")
        rstd_ready, sums_ready, root_ready = sem("rstd_ready"), sem("sums_ready"), sem("root_ready")
        x_loaded = [sem("x_loaded0"), sem("x_loaded1")]
        ident_loaded, ones_loaded, cst_loaded = sem("ident_loaded"), sem("ones_loaded"), sem("cst_loaded")
        norms_loaded = sem("norms_loaded")
        par_loaded = sem("par_loaded")
        pool_w_loaded = sem("pool_w_loaded")
        x_turned = sem("x_turned")
        x_copied_act, x_copied_dve = sem("x_copied_act"), sem("x_copied_dve")
        par_turned, cols_ready = sem("par_turned"), sem("cols_ready")
        x_squared, x_root = sem("x_squared"), sem("x_root")
        x_rstd, x_diag = sem("x_rstd"), sem("x_diag")
        rstd_rows = sem("rstd_rows")
        filled = sem("filled")
        zeroed = sem("zeroed")
        logits, logits_turned = sem("logits"), sem("logits_turned")
        logits_copied, logits_twice = sem("logits_copied"), sem("logits_twice")
        gate_chain = sem("gate_chain")
        minus_abs = sem("minus_abs")
        gate_exp, gate_log = sem("gate_exp"), sem("gate_log")
        log_decay = sem("log_decay")
        decay_sums, decay_summed = sem("decay_sums"), sem("decay_summed")
        decay_exps = sem("decay_exps")
        diag_ready = sem("diag_ready")
        qk_turned = sem("qk_turned")
        qk_sq, qk_root = sem("qk_sq"), sem("qk_root")
        qk_inv, norm_cols = sem("qk_inv"), sem("norm_cols")
        gates_ready = sem("gates_ready")
        decay_rows, q_row, qg_rows = sem("decay_rows"), sem("q_row"), sem("qg_rows")
        decay_diff, decay_bound = sem("decay_diff"), sem("decay_bound")
        decay_exp = sem("decay_exp")
        decay_ready, beta_decay, q_decay = sem("decay_ready"), sem("beta_decay"), sem("q_decay")
        kq = sem("kq")
        lt_ready, qkt_ready, qg_ready = sem("lt_ready"), sem("qkt_ready"), sem("qg_ready")
        tt_part, tt_first = sem("tt_part"), sem("tt_first")
        t_turned, t_first = sem("t_turned"), sem("t_first")
        l_masked = sem("l_masked")
        lx, lx_copied = sem("lx"), sem("lx_copied")
        tlt, t_joined = sem("tlt"), sem("t_joined")
        t_back, tt_copied = sem("t_back"), sem("tt_copied")
        k_tok, v_tok = sem("k_tok"), sem("v_tok")
        k_scaled, v_scaled = sem("k_scaled"), sem("v_scaled")
        k_decayed = sem("k_decayed")
        w_prod, w_copied = sem("w_prod"), sem("w_copied")
        v_prod, v_copied = sem("v_prod"), sem("v_copied")
        so_prod, s_ready, o_copied = sem("so_prod"), sem("s_ready"), sem("o_copied")
        o_turned, o_sq, o_root = sem("o_turned"), sem("o_sq"), sem("o_root")
        o_inv, o_diag, o_row = sem("o_inv"), sem("o_diag"), sem("o_row")
        o_normed, o_gated = sem("o_normed"), sem("o_gated")
        o_hi, o_lo = sem("o_hi"), sem("o_lo")
        pool_chain, pooled = sem("pool_chain"), sem("pooled")
        pool_prod, pool_out = sem("pool_prod"), sem("pool_out")
        pool_hi, pool_lo = sem("pool_hi"), sem("pool_lo")
        scaled = sem("scaled")
        y_weighted = sem("y_weighted")
        y_turned = sem("y_turned")
        y_kept = [sem("y_kept_act"), sem("y_kept_dve")]
        y_scaled = [sem("y_scaled_act"), sem("y_scaled_dve")]
        stored = sem("stored")

        def halves(t, slot, h):
            return t[:, slot, :].rearrange("p (k n) -> p k n", k=4)[:, :, 256 * h:256 * h + 256]

        SCHEDULE = {4: ("decay_rows", 0), 9: ("q_row", 0), 11: ("kq", 0), 13: ("qg_rows", 0), 14: ("first", 0)}
        for l in range(len(LEVELS)):
            SCHEDULE[16 + 3 * l], SCHEDULE[17 + 3 * l] = ("lx", l), ("join", l)
            if l < len(LEVELS) - 1:
                SCHEDULE[18 + 3 * l] = ("turn", l)
        SCHEDULE.update({32: ("k_tok", 0), 34: ("v_tok", 0), 36: ("w", 0)})
        for c, q in enumerate((38, 41, 44, 48)):
            SCHEDULE[q], SCHEDULE[q + 2] = ("values", c), ("outputs", c)
        SCHEDULE.update({52: ("mixer", 0), 54: ("o_sums", 0), 55: ("mix_split", 0), 58: ("o_rows", 0), 59: ("mix_split", 1)})
        QUARTERS = 64

        def pass_bank(d):
            return 4 if d % 2 == 0 else 0

        def y_piece(g, t):
            return xT[:, 4 * g + 2 * t:4 * g + 2 * t + 2, :].rearrange("p a n -> p (a n)")

        PIECES = [(0, 1, 1), (0, 0, 0), (1, 0, 1), (1, 1, 1), (2, 0, 0), (2, 1, 1), (3, 0, 0), (3, 1, 1)]

        block = ctx.enter_context(nc.Block())

        @block.sync
        def _(sp):
            for t in range(TT):
                sp.dma_start(xtok[:, t, :], x2[P * t:P * t + P, :]).then_inc(x_loaded[t], 16)
            for r, v, k in [(N1, norm1_w[0], 16), (N2, norm2_w[0], 16), (NF, final_norm_w, 16), (PSC, pool_scale[0], 8),
                            (ONW, out_norm_w[0], 1)]:
                sp.dma_start(staged[r:r + k, 0, :], v.rearrange("(t p) -> t p", p=P)).then_inc(norms_loaded, 16)

            def load(u, slot, src, first=False):
                if not first:
                    sp.wait_ge(lo_split, 2 * (u - 1))
                sp.dma_start(raw[:, slot, :].rearrange("p (k n) -> p k n", k=4),
                             src.rearrange("(k p) n -> p k n", p=P)).then_inc(raw_loaded[slot], 16)

            def load_block(b, w, c0, order=(0, 1, 2, 3)):
                for i, r in enumerate(order):
                    load(4 * b + i, i % 2, w[512 * r:512 * r + 512, bass.ds(c0, 512)])

            for i in range(2):
                load(i, i, w_in2[512 * i:512 * i + 512, 0:512], first=True)
            sp.dma_start(w_log, w_in2[:, 4 * DN:4 * DN + 2 * HEADS].rearrange("(k p) n -> p k n", p=P)).then_inc(par_loaded, 16)
            sp.dma_start(staged[0:88, 1, :], conv_ffn_b[0].rearrange("(t p) -> t p", p=P)).then_inc(par_loaded, 16)
            for t in range(3):
                sp.dma_start(staged[0:88, 2 + t, :], conv_ffn_w[0, t, :].rearrange("(t p) -> t p", p=P)).then_inc(par_loaded, 16)
            sp.dma_start(staged[0:96, 5, :], conv_qkv_w[0].rearrange("j (t p) -> (j t) p", p=P)).then_inc(par_loaded, 16)
            sp.dma_start(al8, a_log[0:1, :].to_broadcast([P, 8])).then_inc(par_loaded, 16)
            sp.dma_start(dt8, dt_bias[0:1, :].to_broadcast([P, 8])).then_inc(par_loaded, 16)
            sp.dma_start(cst[:, :], table[:, 0:C_IDENT]).then_inc(cst_loaded, 16)
            sp.dma_start(pw, pool_w[0].rearrange("g (k p) n -> p g k n", p=P)).then_inc(pool_w_loaded, 16)
            for i in range(2, 4):
                load(i, i % 2, w_in2[512 * i:512 * i + 512, 0:512])
            with sp.Fori(1, 6) as i:
                load_block(i, w_in2, i * 512)
            for b in range(6, 10):
                load_block(b, w_in2, IN_COLS[b])
            for i in range(4):
                load_block(OUT_B + i, w_out2, 512 * i, (2, 3, 0, 1))
            with sp.Fori(0, 11) as i:
                load_block(UP_B + 2 * i, w_up2, i * 512)
                load_block(UP_B + 1 + 2 * i, w_up2, i * 512 + FF)
            for d in range(PASSES):
                u, c = DOWN_U + DOWN_STEPS * d, slice(512 * d, 512 * d + 512)
                load(u, u % 2, w_down2[0:512, c])
                with sp.Fori(0, DOWN_STEPS // 2) as i:
                    for n in (1, 2):
                        load(u + n + 2 * i, (u + n) % 2, w_down2[bass.ds(i * 1024 + 512 * n, 512), c])
            done = [0, 0]
            for g, t, e in PIECES:
                done[e] += 1
                sp.wait_ge(y_scaled[e], done[e])
                sp.dma_start(out2[P * t:P * t + P, 512 * g:512 * g + 512], y_piece(g, t)).then_inc(stored, 16)
            sp.wait_ge(stored, 16 * 8)

        @block.gpsimd
        def _(pool):
            pool.memset(eps[:, :], EPS)
            pool.memset(vnew[:, :, :, :], 0.0)
            pool.memset(ub[:, :, 0:PAD], 0.0).then_inc(filled, 1)

            pool.wait_ge(cst_loaded, 16)
            pool.wait_ge(logits, 1)
            pool.wait_ge(act_hi, 4)
            pool.wait_ge(act_lo, 4)
            pool.memset(LT, 0.0).then_inc(zeroed, 1)
            pool.wait_ge(decay_summed, 1)
            pool.tensor_tensor(diag_g, times(cst[:, C_EYE2:C_EYE2 + 64], J), over(g_cum, 64), ALU.mult).then_inc(diag_ready, 1)
            pool.wait_ge(norm_cols, 1)
            pool.tensor_tensor(diag_b, times(cst[:, C_EYE2:C_EYE2 + 64], J), over(g_brk, 64), ALU.mult).then_inc(diag_ready, 1)
            pool.tensor_tensor(qkt[:, :, :], times(cst[:, C_CAUSAL:C_CAUSAL + 64], J), over(g_rk, 64), ALU.mult).then_inc(diag_ready, 1)
            pool.wait_ge(norm_cols, 2)
            pool.tensor_tensor(diag_q, times(cst[:, C_EYE2:C_EYE2 + 64], J), over(g_qs, 64), ALU.mult).then_inc(diag_ready, 1)
            pool.wait_ge(norm_cols, 3)
            pool.tensor_tensor(diag_eq, times(cst[:, C_EYE2:C_EYE2 + 64], J), over(g_eq, 64), ALU.mult).then_inc(diag_ready, 1)
            pool.wait_ge(qg_rows, PAIRS)
            for l in range(len(LEVELS)):
                for p in range(PAIRS):
                    if l == 0:
                        pool.wait_ge(lt_ready, p + 1)
                    else:
                        pool.wait_ge(lx, PAIRS * (l - 1) + p + 1)
                    pool.tensor_tensor(masked[:, js(p), :], LT[:, js(p), :], times(cst[:, C_NM + P * l:C_NM + P * l + P], CHUNKS),
                                       ALU.mult).then_inc(l_masked, 1)

            n = 0
            pool.wait_ge(lx, PAIRS * len(LEVELS))
            for g, w in enumerate(WINDOWS):
                u = uT[:, 2 * g:2 * g + 2, :]
                pool.wait_ge(evacuated, 24 + 2 * g + 2)
                src, b, s = u, 0, 1
                while s < w:
                    dst = win[:, b]
                    pool.tensor_tensor(dst[:, :, s:], src[:, :, s:], src[:, :, :SEQ - s], ALU.add)
                    pool.tensor_copy(dst[:, :, 0:s], src[:, :, 0:s]).then_inc(pool_chain, 1)
                    n += 1
                    pool.wait_ge(pool_chain, n)
                    src, b, s = dst, 1 - b, 2 * s
                mean = win[:, b]
                pool.tensor_tensor(mean[:, :, 0:16], src[:, :, 0:16],
                                   times(cst[:, C_COUNT + 16 * g:C_COUNT + 16 * g + 16], 2), ALU.mult)
                pool.tensor_scalar(mean[:, :, 16:], src[:, :, 16:], 1.0 / w, None, ALU.mult).then_inc(pool_chain, 1)
                n += 1
                pool.wait_ge(pool_chain, n)
                pool.tensor_tensor(u, mean, u, ALU.subtract).then_inc(pooled, 1)
                pool.wait_ge(pooled, g + 1)

            pool.wait_ge(rstd_ready, 1)
            with pool.Fori(0, DOWN_B - UP_B) as i:
                for f in range(4):
                    pool.wait_ge(evacuated, 4 * i + 4 * UP_B + f + 1)
                    pool.tensor_tensor(ub[:, f, PAD:], ub[:, f, PAD:], rstd[:, :], ALU.mult).then_inc(scaled, 1)

        @block.scalar
        def _(a):
            def copy(o, i):
                return a.activation(o, i, ACT.Copy)

            a.dma_start(ident[:, :], table[:, C_IDENT:C_IDENT + P]).then_inc(ident_loaded, 16)
            a.dma_start(ones[:, :], table[:, C_ONES:C_ONES + P]).then_inc(ones_loaded, 16)
            a.wait_ge(filled, 1)
            a.activation(y_rstd[:, 0:1], eps[:, 0:1], ACT.Sqrt)

            def hi_half(u, use, slot, h):
                if h == 0:
                    a.wait_ge(raw_loaded[slot], 16 * (use + 1))
                if not (isinstance(u, int) and u < 2):
                    a.wait_ge(slabs, 4 * (u - 2) + 2 * (h + 1))
                copy(halves(w_hi, slot, h), halves(raw, slot, h)).then_inc(hi_split, 1)

            def hi(b, i):
                for h in range(2):
                    hi_half(4 * b + i, 2 * b + i // 2, i % 2, h)

            def post_copy(t, slab, free=None, bank=0, n=None):
                for f in range(4):
                    a.wait_ge(slabs, slab + f + 1)
                    if free is not None:
                        a.wait_ge(free[0], free[1] + f)
                    copy(yb[:, f, :], ps[:, bank + f, 256:512]).then_inc(copied, 1)
                    if n is not None:
                        a.wait_ge(residual, n + f + 1)
                        a.activation(yb[:, f, :], xT[:, n - KD + f, :], ACT.Square).then_inc(squared, 1)

            def post_tap(ready, t, weight, bias):
                for f in range(4):
                    a.wait_ge(ready, t + f + 1)
                    a.activation(yb[:, f, :], ub[:, f, PAD:], ACT.Identity, scale=cols[:, bass.ds(weight + f, 1)],
                                 bias=0.0 if bias is None else cols[:, bass.ds(bias + f, 1)]).then_inc(tapped, 1)

            def post_square(t, n):
                for f in range(4):
                    a.wait_ge(residual, n + f + 1)
                    a.activation(yb[:, f, :], xT[:, bass.ds(t + f, 1), :].rearrange("p a n -> p (a n)"), ACT.Square).then_inc(squared, 1)

            def split_hi(group, g, n):
                a.wait_ge(normed, n + 4 * g + 4)
                copy(act[:, 4 * g:4 * g + 4, 0:SEQ], group).then_inc(act_hi, 1)

            for t in range(TT):
                a.wait_ge(x_loaded[t], 16)
                if t:
                    a.wait_ge(x_squared, t)
                a.activation(sqx, xtok[:, t, :], ACT.Square, accum_out=sq_acc[:, t:t + 1]).then_inc(x_squared, 1)
            a.wait_ge(x_squared, 2)
            a.wait_ge(filled, 1)
            a.activation(sq_acc[:, :], sq_acc[:, :], ACT.Sqrt, scale=1.0 / D, bias=eps[:, 0:1]).then_inc(x_root, 1)
            def copy_x(i):
                a.wait_ge(x_turned, i + 3)
                copy(xT[:, 2 * i:2 * i + 2, :], ps[:, i, :].rearrange("p (t n) -> p t n", n=SEQ)).then_inc(x_copied_act, 1)

            copy_x(0)
            copy_x(1)
            hi(0, 0)
            split_hi(h32[:, 0:4, :], 0, 0)
            copy_x(3)
            copy_x(4)
            copy_x(5)
            hi(0, 1)
            split_hi(h32[:, 4:8, :], 1, 0)
            hi(0, 2)
            split_hi(h32[:, 8:12, :], 2, 0)
            hi(0, 3)
            split_hi(h32[:, 12:16, :], 3, 0)

            def logits_act():
                a.wait_ge(logits, 1)
                copy(lg, ps[0:16, 4, 0:SEQ]).then_inc(logits_copied, 1)
                a.wait_ge(logits_copied, 1)
                for d in range(2):
                    last = copy(lgd[:, :, d, :], lg.rearrange("p (c n) -> p c n", n=64))
                last.then_inc(logits_twice, 1)

            def gates_act():
                a.wait_ge(par_loaded, 16 * 8)
                a.activation(al8, al8, ACT.Exp).then_inc(gate_exp, 1)
                a.wait_ge(minus_abs, 1)
                a.activation(g_t1, g_in[:, 0:16], ACT.Exp, scale=-1.0).then_inc(gate_exp, 1)
                a.activation(g_t2, g_t2, ACT.Exp).then_inc(gate_exp, 1)
                a.wait_ge(gate_exp, 3)
                a.activation(g_t2, g_t2, ACT.Ln, bias=1.0).then_inc(gate_log, 1)

            def qkv_silu(pair, f):
                a.activation(by_problem[:, bass.ds(pair, 1), :, f % 2, :].rearrange("p a c n -> p (a c) n"),
                             yb[:, f, :].rearrange("p (c n) -> p c n", n=64), ACT.Silu).then_inc(silu_done, 1)

            def token_squares(k):
                for j in range(J):
                    a.wait_ge(qk_turned, PAIRS * k + j // CHUNKS + 1)
                    a.activation((sq_q, sq_k)[k][:, P * j:P * j + P], pbank(j // CHUNKS, P)[:, j % CHUNKS, :], ACT.Square,
                                 accum_out=g_norm[:, J * k + j:J * k + j + 1]).then_inc(qk_sq, 1)

            def decay_exps_act():
                a.wait_ge(decay_summed, 1)
                a.activation(g_eg, g_cum, ACT.Exp).then_inc(decay_exps, 1)
                a.activation(g_kt, g_kt, ACT.Exp).then_inc(decay_exps, 1)
                a.activation(g_sum[:, 32:64], g_sum[:, 32:64], ACT.Exp).then_inc(decay_exps, 1)

            def act_qkv_block(i, gates=False, norms=None):
                hi(i, 0)
                post_copy(4 * i - 4, 16 * i - 4)
                if gates:
                    logits_act()
                hi(i, 1)
                post_tap(evacuated, 4 * i - 4, QW + 72 + 4 * i - 4, None)
                if gates:
                    gates_act()
                hi(i, 2)
                for f in range(4):
                    a.wait_ge(convolved, 4 * i - 4 + f + 1)
                    qkv_silu(2 * i - 2 + f // 2, f)
                if norms == 1:
                    decay_exps_act()
                hi(i, 3)
                if norms is not None:
                    token_squares(norms)

            act_qkv_block(1, gates=True)
            with a.Fori(2, 4) as i:
                act_qkv_block(i)
            act_qkv_block(4, norms=0)
            act_qkv_block(5, norms=1)

            def late_half(c):
                hi_half(24 + c // 2, 12 + c // 4, (c // 2) % 2, c % 2)

            late_half(0)
            post_copy(20, 92)
            late_half(1)
            a.wait_ge(qk_sq, 2 * J)
            a.activation(g_norm, g_norm, ACT.Sqrt, bias=eps[:, 0:1]).then_inc(qk_root, 1)

            def act_step(step, k):
                for p in range(PAIRS):
                    n = PAIRS * k + p
                    if step == "decay_rows":
                        a.wait_ge(decay_bound, p + 1)
                        a.activation(decay[:, js(p), :], decay[:, js(p), :], ACT.Exp).then_inc(decay_exp, 1)
                    elif step == "first":
                        a.wait_ge(t_turned, p + 1)
                        copy(Tm[:, js(p), :], pbank(p, P)).then_inc(t_first, 1)
                    elif step == "lx":
                        a.wait_ge(lx, n + 1)
                        copy(X_[:, js(p), :], pbank(p, P)).then_inc(lx_copied, 1)
                    elif step == "turn":
                        a.wait_ge(t_back, n + 1)
                        copy(TT_[:, js(p), :], pbank(p, P)).then_inc(tt_copied, 1)
                    elif step == "k_tok":
                        a.wait_ge(k_scaled, p + 1)
                        for j in range(CHUNKS * p, CHUNKS * p + CHUNKS):
                            last = a.activation(ktail[:, j, :], pbank(p, P)[:, j % CHUNKS, :], ACT.Copy, scale=g_kt[:, j:j + 1])
                        last.then_inc(k_decayed, 1)
                    elif step == "w":
                        a.wait_ge(w_prod, p + 1)
                        copy(W[:, js(p)].rearrange("p j h c -> p (j h c)"), ps[:, 4 + p, :]).then_inc(w_copied, 1)
                    elif step == "values":
                        a.wait_ge(v_prod, n + 1)
                        for h in range(2):
                            last = copy(vnew[HALF[h], p, h, :], ps[HALF[h], 4 + p, 0:P])
                        last.then_inc(v_copied, 1)
                    elif step == "outputs":
                        a.wait_ge(so_prod, n + 1)
                        if k < CHUNKS - 1:
                            a.wait_ge(s_ready, n + 1)
                        copy(oT[:, hs(p), 64 * k:64 * k + 64],
                             ps[:, 4 + p, P:2 * P].rearrange("p (h n) -> p h n", h=2)).then_inc(o_copied, 1)
                    elif step == "mixer":
                        for f in range(2):
                            a.wait_ge(pool_prod, p + 1)
                            a.activation(uT[:, 2 * p + f, :], ps[:, 4 + p, SEQ * f:SEQ * f + SEQ], ACT.Identity,
                                         scale=cols[:, PSC + 2 * p + f:PSC + 2 * p + f + 1]).then_inc(pool_out, 1)
                if step == "o_sums":
                    for p in range(PAIRS):
                        a.wait_ge(o_turned, p + 1)
                        for c in range(4 * p, 4 * p + 4):
                            a.activation(sq_o[:, c, :], pbank(p, P)[:, c % 4, :], ACT.Square, accum_out=g_ro[:, c:c + 1]).then_inc(o_sq, 1)
                    a.wait_ge(o_sq, 4 * PAIRS)
                    a.activation(g_ro, g_ro, ACT.Sqrt, scale=1.0 / P, bias=eps[:, 0:1]).then_inc(o_root, 1)
                    z_silu(0)
                elif step == "mix_split":
                    a.wait_ge(pool_out, 4 * k + 4)
                    a.wait_ge(slabs, 4 * 36 + 4 * (k + 1))
                    copy(act[:, 4 * k:4 * k + 4, 0:SEQ], uT[:, 4 * k:4 * k + 4, :]).then_inc(pool_hi, 1)

            def z_silu(n):
                for f in range(4):
                    a.wait_ge(evacuated, 32 + n + f + 1)
                    a.activation(zT[:, n + f, :], ub[:, f, PAD:], ACT.Silu).then_inc(silu_done, 1)

            late_half(2)
            post_tap(evacuated, 20, QW + 72 + 20, None)
            for f in range(4):
                a.wait_ge(convolved, 20 + f + 1)
                qkv_silu(10 + f // 2, f)
            for q in range(QUARTERS):
                if q in (16, 32, 48):
                    post_copy(20 + q // 4, 92 + q)
                if q in SCHEDULE:
                    act_step(*SCHEDULE[q])
                if q % 2:
                    if q // 2 + 3 < QUARTERS // 2 + 2:
                        late_half(q // 2 + 3)

            def heads_hi(p):
                a.wait_ge(o_gated, p + 1)
                a.wait_ge(slabs, 4 * 38 + 4 * (p // 2 + 1))
                copy(act[:, 8 + 2 * p:10 + 2 * p, 0:SEQ], oT[:, hs(p), :]).then_inc(o_hi, 1)

            post_copy(36, 156)
            hi(10, 1)
            z_silu(4)
            heads_hi(0)
            heads_hi(1)
            hi(10, 2)
            heads_hi(2)
            heads_hi(3)
            hi(10, 3)

            def act_out_block(b, i, first=False):
                hi(b, 0)
                post_copy(4 * b - 4, 16 * b - 4, None if first else (summed, 4 * i - 7))
                hi(b, 1)
                hi(b, 2)
                post_square(4 * i - 4, 4 * i - 4)
                hi(b, 3)

            def weighted_hi(g):
                a.wait_ge(residual, 4 * g + 4)
                a.wait_ge(slabs, 4 * (UP_B * 4 - 4) + 4 * g + 4)
                for t in range(4 * g, 4 * g + 4):
                    last = a.activation(act[:, t, 0:SEQ], xT[:, t, :], ACT.Identity, scale=cols[:, N2 + t:N2 + t + 1])
                last.then_inc(act_hi, 1)

            act_out_block(11, 1, first=True)
            act_out_block(12, 2)
            hi(13, 0)
            post_copy(48, 204, (summed, 5))
            hi(13, 1)
            hi(13, 2)
            weighted_hi(0)
            post_square(8, 8)
            hi(13, 3)
            weighted_hi(1)
            hi(14, 0)
            weighted_hi(2)
            post_copy(52, 220, (summed, 9))
            hi(14, 1)
            weighted_hi(3)
            post_square(12, 12)
            hi(14, 2)
            hi(14, 3)
            a.wait_ge(sums_ready, 1)
            a.activation(rstd[:, :], ps[:, 4, 0:SEQ], ACT.Sqrt, scale=1.0 / D, bias=eps[:, 0:1]).then_inc(root_ready, 1)

            def act_up_block(b, i, prev, first=False):
                hi(b, 0)
                if prev is not None:
                    free = (product_lo, 4 * i - 3) if prev == "gate" and not first else None
                    post_copy(4 * b - 4, 16 * b - 4, free)
                hi(b, 1)
                if prev is not None:
                    t = 4 * i + (44 if prev == "value" else 0)
                    post_tap(scaled, 8 * i + (4 if prev == "value" else 0), CW + 176 + t, CB + t)
                hi(b, 2)
                if prev == "gate":
                    for f in range(4):
                        a.wait_ge(convolved, 24 + 8 * i + f + 1)
                        if not first:
                            a.wait_ge(product, 4 * i - 3 + f)
                        a.activation(gb[:, f, :], yb[:, f, :], ACT.Silu).then_inc(silu_done, 1)
                hi(b, 3)
                if prev == "value":
                    product_split_hi(i)

            def product_split_hi(i):
                for f in range(4):
                    a.wait_ge(product, 4 * i + f + 1)
                    copy(fact[:, bass.ds(4 * i + f, 1), 0:SEQ], yb[:, f:f + 1, :]).then_inc(product_hi, 1)

            act_up_block(UP_B + 1, 0, "gate", first=True)
            with a.Fori(0, 10) as i:
                act_up_block(UP_B + 2 + 2 * i, i, "value")
                act_up_block(UP_B + 3 + 2 * i, i + 1, "gate")

            def hi_down(d, n, i=0):
                u = DOWN_U + DOWN_STEPS * d + n
                for h in range(2):
                    hi_half(u + 2 * i, u // 2 + i, u % 2, h)

            for d in range(PASSES):
                t = 4 * (d - 1)
                hi_down(d, 0)
                if d == 0:
                    post_copy(4 * DOWN_B - 4, 16 * DOWN_B - 4)
                else:
                    post_copy(DOWN_T + t, 4 * (DOWN_U + DOWN_STEPS * d) - 4, (product_lo, 41) if d == 1 else (summed, 16 + t - 3),
                              bank=pass_bank(d - 1))
                hi_down(d, 1)
                if d == 0:
                    post_tap(scaled, 84, CW + 176 + 84, CB + 84)
                else:
                    post_square(t, 16 + t)
                hi_down(d, 2)
                with a.Fori(0, 3) as i:
                    hi_down(d, 3, i)
                    hi_down(d, 4, i)
                if d == 0:
                    product_split_hi(10)
                hi_down(d, 9)
                hi_down(d, 10)
                if d:
                    a.wait_ge(y_turned, 2 * d)
                    copy(y_piece(d - 1, 0), ps[:, pass_bank(d - 1), :]).then_inc(y_kept[0], 1)
            post_copy(DOWN_T + 12, 4 * (DOWN_U + DOWN_STEPS * PASSES) - 4, (summed, 16 + 9), bank=pass_bank(3), n=28)
            a.wait_ge(sums_ready, 2)
            a.activation(y_rstd[:, :], ps[:, 6, 0:TT], ACT.Sqrt, scale=1.0 / D, bias=eps[:, 0:1]).then_inc(root_ready, 1)
            a.wait_ge(rstd_ready, 2)
            for g, t, e in PIECES:
                if e == 0:
                    a.wait_ge(y_kept[t] if g < 3 else y_turned, g + 1 if g < 3 else 8)
                    a.activation(y_piece(g, t), y_piece(g, t) if g < 3 else ps[:, pass_bank(3) + t, :], ACT.Copy,
                                 scale=y_rstd[:, t:t + 1]).then_inc(y_scaled[0], 1)

        @block.vector
        def _(v):
            def lo_half(u2, slot, h):
                v.wait_ge(hi_split, u2 + 1)
                v.tensor_tensor(halves(w_lo, slot, h), halves(raw, slot, h),
                                halves(w_hi, slot, h).bitcast(F32), ALU.subtract).then_inc(lo_split, 1)

            def lo(b, i):
                for h in range(2):
                    lo_half(8 * b + 2 * i + h, i % 2, h)

            def post_add(t, used=None, bank=0, tiles=range(4)):
                for f in tiles:
                    v.wait_ge(copied, t + f + 1)
                    if used is not None:
                        v.wait_ge(used[0], used[1] + f)
                    v.tensor_tensor(ub[:, f, PAD:], ps[:, bank + f, 0:256], yb[:, f, :], ALU.add).then_inc(evacuated, 1)

            def tap(f, back, weight, done, n):
                v.scalar_tensor_tensor(out=yb[:, f, :], in0=ub[:, f, PAD - back:PAD - back + SEQ],
                                       scalar=cols[:, bass.ds(weight + f, 1)], in1=yb[:, f, :],
                                       op0=ALU.mult, op1=ALU.add).then_inc(done, 1)

            def conv_qkv(t):
                for f in range(4):
                    v.wait_ge(tapped, t + f + 1)
                    tap(f, 1, QW + 48 + t, tap1, t)
                for f in range(4):
                    v.wait_ge(tap1, t + f + 1)
                    tap(f, 2, QW + 24 + t, tap2, t)
                for f in range(4):
                    v.wait_ge(tap2, t + f + 1)
                    tap(f, 3, QW + t, convolved, t)

            def conv_ffn(n, t):
                for f in range(4):
                    v.wait_ge(tapped, 24 + n + f + 1)
                    tap(f, 1, CW + 88 + t, tap1, t)
                for f in range(4):
                    v.wait_ge(tap1, 24 + n + f + 1)
                    tap(f, 2, CW + t, convolved, t)

            def post_residual(t, n, evac, tiles=range(4)):
                for f in tiles:
                    v.wait_ge(evacuated, evac + f + 1)
                    x_t = xT[:, bass.ds(t + f, 1), :]
                    v.tensor_tensor(x_t, x_t, ub[:, f:f + 1, PAD:], ALU.add).then_inc(residual, 1)

            def post_sum(n, first=False, tiles=range(4)):
                for f in tiles:
                    v.wait_ge(squared, n + f + 1)
                    if first and f == 0:
                        v.tensor_copy(sumsq[:, :], yb[:, f, :]).then_inc(summed, 1)
                    else:
                        v.wait_ge(summed, n + f)
                        v.tensor_tensor(sumsq[:, :], sumsq[:, :], yb[:, f, :], ALU.add).then_inc(summed, 1)

            def split_lo(group, g, n):
                v.wait_ge(act_hi, n + g + 1)
                v.tensor_tensor(act[:, 4 * g:4 * g + 4, SEQ:], group, act[:, 4 * g:4 * g + 4, 0:SEQ].bitcast(F32),
                                ALU.subtract).then_inc(act_lo, 1)

            def copy_x(i):
                v.wait_ge(x_turned, (i - 6) % 8 + 1)
                v.tensor_copy(xT[:, 2 * i:2 * i + 2, :], ps[:, i, :].rearrange("p (t n) -> p t n", n=SEQ)).then_inc(x_copied_dve, 1)

            copy_x(6)
            copy_x(7)
            v.wait_ge(x_root, 1)
            v.reciprocal(sq_acc[:, :], sq_acc[:, :]).then_inc(x_rstd, 1)
            v.wait_ge(x_rstd, 1)
            v.wait_ge(ident_loaded, 16)
            for t in range(TT):
                v.tensor_scalar(rdiag[:, t, :], ident[:, :], sq_acc[:, t:t + 1], None, ALU.mult).then_inc(x_diag, 1)
            copy_x(2)
            v.wait_ge(par_turned, 1)
            v.tensor_copy(cols[:, 0:57], ps[:, 6, 0:57]).then_inc(cols_ready, 1)
            v.wait_ge(cols_ready, 1)
            v.wait_ge(rstd_rows, 1)
            v.wait_ge(x_squared, 2)
            v.wait_ge(x_copied_dve, 3)
            v.wait_ge(x_copied_act, 2)
            for g in range(4):
                if g:
                    v.wait_ge(x_copied_act, 3 if g == 1 else 5)
                for t in range(4 * g, 4 * g + 4):
                    v.scalar_tensor_tensor(out=h32[:, t, :], in0=xT[:, t, :], scalar=cols[:, N1 + t:N1 + t + 1],
                                           in1=ps[:, 7, 0:SEQ], op0=ALU.mult, op1=ALU.mult).then_inc(normed, 1)
                lo_half(2 * g, g % 2, 0)
                split_lo(h32[:, 4 * g:4 * g + 4, :], g, 0)
                lo_half(2 * g + 1, g % 2, 1)
            v.wait_ge(par_turned, 2)
            v.tensor_copy(cols[:, 57:505], ps[:, 6, 57:505]).then_inc(cols_ready, 1)
            v.wait_ge(cols_ready, 2)

            chained = [0]

            def link(ins):
                chained[0] += 1
                ins.then_inc(gate_chain, 1)
                v.wait_ge(gate_chain, chained[0])

            def gates_in():
                heads = g_in.rearrange("p (k j c) -> p k j c", k=2, c=CHUNKS)
                v.wait_ge(logits_turned, 1)
                for h in range(2):
                    last = v.tensor_copy(heads[HALF[h]], ps[HALF[h], 5, 0:64].rearrange(
                        "p (c k j h) -> p h k j c", c=CHUNKS, k=2, h=2)[:, h])
                link(last)
                v.wait_ge(par_loaded, 16 * 8)
                for h in range(2):
                    bias = dt8[HALF[h]].rearrange("p (j h) -> p h j", h=2)[:, h]
                    last = v.tensor_tensor(heads[HALF[h], 1], heads[HALF[h], 1], over(bias, CHUNKS), ALU.add)
                link(last)
                y = g_in[:, 16:32]
                v.scalar_tensor_tensor(out=g_t2, in0=y, scalar=-1.0, in1=y, op0=ALU.mult, op1=ALU.min).then_inc(minus_abs, 1)

            def gates_out():
                y = g_in[:, 16:32]
                v.wait_ge(gate_log, 1)
                link(v.tensor_scalar(g_t1, g_t1, 1.0, None, ALU.add))
                link(v.reciprocal(g_beta, g_t1))
                link(v.scalar_tensor_tensor(out=g_t3, in0=y, scalar=0.0, in1=g_t2, op0=ALU.max, op1=ALU.add))
                for h in range(2):
                    ea = al8[HALF[h]].rearrange("p (j h) -> p h j", h=2)[:, h]
                    sp_h = g_t3[HALF[h]].rearrange("p (j c) -> p j c", c=CHUNKS)
                    last = v.scalar_tensor_tensor(out=g_g[HALF[h]].rearrange("p (j c) -> p j c", c=CHUNKS), in0=sp_h, scalar=-1.0,
                                                  in1=over(ea, CHUNKS), op0=ALU.mult, op1=ALU.mult)
                last.then_inc(log_decay, 1)

            def dve_qkv_block(i, gates=False, first=False, sums=False):
                lo(i, 0)
                post_add(4 * i - 4, None if first else (convolved, 4 * i - 7))
                if sums:
                    v.wait_ge(decay_sums, 1)
                    link(v.tensor_copy(g_sum, ps[:, 5, 64:128]))
                    v.tensor_tensor(g_kt, g_tot, g_cum, ALU.subtract).then_inc(decay_summed, 1)
                lo(i, 1)
                if gates:
                    gates_in()
                conv_qkv(4 * i - 4)
                lo(i, 2)
                if gates:
                    gates_out()
                lo(i, 3)

            v.wait_ge(filled, 1)
            dve_qkv_block(1, gates=True, first=True)
            with v.Fori(2, 5) as i:
                dve_qkv_block(i)
            dve_qkv_block(5, sums=True)

            def late_half(c):
                lo_half(48 + c, (c // 2) % 2, c % 2)

            late_half(0)
            post_add(20, (convolved, 17))
            late_half(1)
            v.wait_ge(qk_root, 1)
            v.reciprocal(g_norm, g_norm).then_inc(qk_inv, 1)
            v.wait_ge(qk_inv, 1)
            v.tensor_tensor(g_brk, g_beta, g_rk, ALU.mult).then_inc(norm_cols, 1)
            v.tensor_scalar(g_qs, g_rq, QSCALE, None, ALU.mult).then_inc(norm_cols, 1)
            v.wait_ge(norm_cols, 2)
            v.wait_ge(decay_exps, 3)
            v.tensor_tensor(g_eq, g_eg, g_qs, ALU.mult).then_inc(norm_cols, 1)
            v.scalar_tensor_tensor(out=g_nbeg, in0=g_brk, scalar=-1.0, in1=g_eg, op0=ALU.mult, op1=ALU.mult)
            v.tensor_tensor(g_kt, g_kt, g_rk, ALU.mult).then_inc(gates_ready, 1)

            def dve_step(step, k):
                if step == "decay_rows":
                    for p in range(PAIRS):
                        v.wait_ge(decay_rows, p + 1)
                        v.tensor_tensor(decay[:, js(p), :], ps[:, 4 + p, 0:SEQ].rearrange("p (j n) -> p j n", n=64),
                                        over(g_cum[:, js(p)], 64), ALU.subtract).then_inc(decay_diff, 1)
                    for p in range(PAIRS):
                        v.wait_ge(decay_diff, p + 1)
                        v.tensor_scalar(decay[:, js(p), :], decay[:, js(p), :], 0.0, None, ALU.min).then_inc(decay_bound, 1)
                    v.wait_ge(diag_ready, 3)
                    for p in range(PAIRS):
                        v.wait_ge(decay_exp, p + 1)
                        v.tensor_tensor(decay[:, js(p), :], decay[:, js(p), :], qkt[:, js(p), :], ALU.mult).then_inc(decay_ready, 1)
                    for p in range(PAIRS):
                        v.wait_ge(decay_ready, p + 1)
                        v.tensor_tensor(bdec[:, js(p), :], ps[:, 4 + p, SEQ:].rearrange("p (j n) -> p j n", n=64),
                                        decay[:, js(p), :], ALU.mult).then_inc(beta_decay, 1)
                if step == "q_row":
                    for p in range(PAIRS):
                        v.wait_ge(q_row, p + 1)
                        v.tensor_tensor(qkt[:, js(p), :], ps[:, 4 + p, 0:SEQ].rearrange("p (j n) -> p j n", n=64),
                                        decay[:, js(p), :], ALU.mult).then_inc(q_decay, 1)
                if step == "kq":
                    v.wait_ge(zeroed, 1)
                    for p in range(PAIRS):
                        v.wait_ge(kq, p + 1)
                        v.wait_ge(beta_decay, p + 1)
                        for h in range(2):
                            last = v.tensor_tensor(LT[HALF[h], js(p), 64 * h:64 * h + 64], pbank(p, P)[HALF[h], :, 64:128],
                                                   bdec[HALF[h], js(p), :], ALU.mult)
                        last.then_inc(lt_ready, 1)
                        v.wait_ge(q_decay, p + 1)
                        v.tensor_tensor(qkt[:, js(p), :], pbank(p, P)[:, :, 0:64], qkt[:, js(p), :], ALU.mult).then_inc(qkt_ready, 1)
                    for p in range(PAIRS):
                        v.wait_ge(lt_ready, p + 1)
                        v.tensor_tensor(TT_[:, js(p), :], LT[:, js(p), :], times(cst[:, C_NM + 5 * P:C_NM + 6 * P], CHUNKS),
                                        ALU.mult).then_inc(tt_part, 1)
                    for p in range(PAIRS):
                        v.wait_ge(tt_part, p + 1)
                        v.tensor_tensor(TT_[:, js(p), :], TT_[:, js(p), :], times(ident[:, :], CHUNKS), ALU.add).then_inc(tt_first, 1)
                if step == "qg_rows":
                    for p in range(PAIRS):
                        v.wait_ge(qg_rows, p + 1)
                        q = by_problem[:, p]
                        for h in range(2):
                            last = v.tensor_tensor(q[:, :, h, :], ps[:, 4 + p, SEQ * h:SEQ * h + SEQ].rearrange("p (c n) -> p c n", n=64),
                                                   q[:, :, h, :], ALU.mult)
                        last.then_inc(qg_ready, 1)
                if step == "join":
                    for p in range(PAIRS):
                        v.wait_ge(tlt, PAIRS * k + p + 1)
                        t_ = (Tm, TT_)[k == len(LEVELS) - 1][:, js(p), :]
                        v.tensor_tensor(t_, t_, pbank(p, P), ALU.add).then_inc(t_joined, 1)
                if step == "k_tok":
                    v.wait_ge(gates_ready, 1)
                    for p in range(PAIRS):
                        v.wait_ge(k_tok, p + 1)
                        v.tensor_tensor(kg[:, js(p), :], pbank(p, P), over(g_nbeg[:, js(p)], P), ALU.mult).then_inc(k_scaled, 1)
                if step == "v_tok":
                    for p in range(PAIRS):
                        v.wait_ge(v_tok, p + 1)
                        v.tensor_tensor(vb[:, js(p), :], pbank(p, P), over(g_beta[:, js(p)], P), ALU.mult).then_inc(v_scaled, 1)
                if step == "outputs" and k < CHUNKS - 1:
                    for p in range(PAIRS):
                        v.wait_ge(so_prod, PAIRS * k + p + 1)
                        for h in range(2):
                            new = ps[:, 4 + p, 256 + P * h:256 + P * h + P]
                            j = CHUNKS * p + k
                            if k == 0:
                                last = v.tensor_copy(S[:, 2 * p + h, :], new)
                            else:
                                v.wait_ge(s_ready, PAIRS * k - PAIRS + p + 1)
                                last = v.scalar_tensor_tensor(out=S[:, 2 * p + h, :], in0=S[:, 2 * p + h, :], scalar=g_last[:, h, j:j + 1],
                                                              in1=new, op0=ALU.mult, op1=ALU.add)
                        last.then_inc(s_ready, 1)
                if step == "mix_split":
                    v.wait_ge(pool_hi, k + 1)
                    v.tensor_tensor(act[:, 4 * k:4 * k + 4, SEQ:], uT[:, 4 * k:4 * k + 4, :],
                                    act[:, 4 * k:4 * k + 4, 0:SEQ].bitcast(F32), ALU.subtract).then_inc(pool_lo, 1)
                if step == "o_sums":
                    v.wait_ge(o_root, 1)
                    v.reciprocal(g_ro, g_ro).then_inc(o_inv, 1)
                    v.wait_ge(o_inv, 1)
                    for p in range(PAIRS):
                        v.tensor_tensor(diag_o[:, 4 * p:4 * p + 4, :], times(ident[:, :], 4), over(g_ro[:, 4 * p:4 * p + 4], P),
                                        ALU.mult).then_inc(o_diag, 1)
                if step == "o_rows":
                    for p in range(PAIRS):
                        v.wait_ge(o_row, p + 1)
                        v.tensor_tensor(oT[:, hs(p), :], oT[:, hs(p), :], pbank(p, SEQ), ALU.mult).then_inc(o_normed, 1)

            def gate_heads(g):
                v.wait_ge(silu_done, 28 + 4 * g)
                for p in (2 * g, 2 * g + 1):
                    v.wait_ge(o_normed, p + 1)
                    v.scalar_tensor_tensor(out=oT[:, hs(p), :], in0=oT[:, hs(p), :], scalar=cols[:, ONW:ONW + 1], in1=zT[:, hs(p), :],
                                           op0=ALU.mult, op1=ALU.mult).then_inc(o_gated, 1)

            late_half(2)
            conv_qkv(20)
            for q in range(QUARTERS):
                if q in (16, 32):
                    for f in range(4):
                        t = 20 + q // 4 + f
                        v.wait_ge(copied, t + 1)
                        v.tensor_tensor(uT[:, t - 24, :], ps[:, f, 0:256], yb[:, f, :], ALU.add).then_inc(evacuated, 1)
                if q == 48:
                    post_add(32)
                if q in SCHEDULE:
                    dve_step(*SCHEDULE[q])
                if q % 2:
                    if q // 2 + 3 < QUARTERS // 2 + 2:
                        late_half(q // 2 + 3)

            def heads_lo(p):
                v.wait_ge(o_hi, p + 1)
                v.tensor_tensor(act[:, 8 + 2 * p:10 + 2 * p, SEQ:], oT[:, hs(p), :], act[:, 8 + 2 * p:10 + 2 * p, 0:SEQ].bitcast(F32),
                                ALU.subtract).then_inc(o_lo, 1)

            post_add(36, (silu_done, 25))
            lo(10, 1)
            gate_heads(0)
            heads_lo(0)
            heads_lo(1)
            gate_heads(1)
            lo(10, 2)
            heads_lo(2)
            heads_lo(3)
            lo(10, 3)

            def dve_out_block(b, i, first=False):
                lo(b, 0)
                post_add(4 * b - 4, (silu_done, 29) if first else (residual, 4 * i - 7))
                lo(b, 1)
                post_residual(4 * i - 4, 4 * i - 4, 4 * b - 4)
                lo(b, 2)
                lo(b, 3)
                post_sum(4 * i - 4, first)

            def weighted_lo(g):
                v.wait_ge(act_hi, 4 + g + 1)
                for t in range(4 * g, 4 * g + 4):
                    last = v.scalar_tensor_tensor(out=act[:, t, SEQ:], in0=xT[:, t, :], scalar=cols[:, N2 + t:N2 + t + 1],
                                                  in1=act[:, t, 0:SEQ].bitcast(F32), op0=ALU.mult, op1=ALU.subtract)
                last.then_inc(act_lo, 1)

            dve_out_block(11, 1, first=True)
            dve_out_block(12, 2)
            lo(13, 0)
            post_add(48, (residual, 5))
            lo(13, 1)
            post_residual(8, 8, 48)
            lo(13, 2)
            weighted_lo(0)
            lo(13, 3)
            weighted_lo(1)
            post_sum(8)
            lo(14, 0)
            weighted_lo(2)
            post_add(52, (residual, 9))
            post_residual(12, 12, 52)
            lo(14, 1)
            weighted_lo(3)
            post_sum(12)
            lo(14, 2)
            lo(14, 3)
            v.wait_ge(root_ready, 1)
            v.reciprocal(rstd[:, :], rstd[:, :]).then_inc(rstd_ready, 1)

            def dve_up_block(b, i, prev, first=False):
                lo(b, 0)
                if prev is not None:
                    post_add(4 * b - 4, (residual, 13) if first else (convolved, 24 + 8 * i + (1 if prev == "value" else -3)))
                lo(b, 1)
                if prev is not None:
                    conv_ffn(8 * i + (4 if prev == "value" else 0), 4 * i + (44 if prev == "value" else 0))
                lo(b, 2)
                if prev == "value":
                    products(i)
                lo(b, 3)
                if prev == "value":
                    product_split_lo(i)

            def products(i):
                for f in range(4):
                    v.wait_ge(convolved, 24 + 8 * i + 4 + f + 1)
                    v.wait_ge(silu_done, 32 + 4 * i + f + 1)
                    v.tensor_tensor(yb[:, f, :], yb[:, f, :], gb[:, f, :], ALU.mult).then_inc(product, 1)

            def product_split_lo(i):
                for f in range(4):
                    v.wait_ge(product_hi, 4 * i + f + 1)
                    k = bass.ds(4 * i + f, 1)
                    v.tensor_tensor(fact[:, k, SEQ:], yb[:, f:f + 1, :], fact[:, k, 0:SEQ].bitcast(F32),
                                    ALU.subtract).then_inc(product_lo, 1)

            dve_up_block(UP_B + 1, 0, "gate", first=True)
            with v.Fori(0, 10) as i:
                dve_up_block(UP_B + 2 + 2 * i, i, "value")
                dve_up_block(UP_B + 3 + 2 * i, i + 1, "gate")

            def lo_down(d, n, i=0):
                u = DOWN_U + DOWN_STEPS * d + n
                for h in range(2):
                    lo_half(2 * u + h + 4 * i, u % 2, h)

            def post_weight(g):
                for t in range(4 * g, 4 * g + 4):
                    v.wait_ge(squared, 16 + t + 1)
                    v.tensor_scalar(xT[:, t, :], xT[:, t, :], cols[:, NF + t:NF + t + 1], None, ALU.mult).then_inc(y_weighted, 1)

            for d in range(PASSES):
                t = 4 * (d - 1)
                lo_down(d, 0)
                if d == 0:
                    post_add(4 * DOWN_B - 4, (convolved, 24 + 81))
                else:
                    post_add(DOWN_T + t, (convolved, 24 + 85) if d == 1 else (residual, 16 + t - 3), bank=pass_bank(d - 1))
                lo_down(d, 1)
                if d == 0:
                    conv_ffn(84, 84)
                    products(10)
                else:
                    post_residual(t, 16 + t, DOWN_T + t)
                lo_down(d, 2)
                if d:
                    post_sum(16 + t, d == 1)
                    post_weight(d - 1)
                with v.Fori(0, 3) as i:
                    lo_down(d, 3, i)
                    lo_down(d, 4, i)
                if d == 0:
                    product_split_lo(10)
                lo_down(d, 9)
                lo_down(d, 10)
                if d:
                    v.wait_ge(y_turned, 2 * d)
                    v.tensor_copy(y_piece(d - 1, 1), ps[:, pass_bank(d - 1) + 1, :]).then_inc(y_kept[1], 1)
            for f in range(4):
                post_add(DOWN_T + 12, (residual, 16 + 9), bank=pass_bank(3), tiles=(f,))
                post_residual(12, 28, DOWN_T + 12, tiles=(f,))
                post_sum(28, tiles=(f,))
            post_weight(3)
            v.wait_ge(root_ready, 2)
            v.reciprocal(y_rstd[:, :], y_rstd[:, :]).then_inc(rstd_ready, 1)
            v.wait_ge(rstd_ready, 2)
            for g, t, e in PIECES:
                if e == 1:
                    v.wait_ge(y_kept[t] if g < 3 else y_turned, g + 1 if g < 3 else 8)
                    v.tensor_scalar(y_piece(g, t), y_piece(g, t) if g < 3 else ps[:, pass_bank(3) + t, :], y_rstd[:, t:t + 1], None,
                                    ALU.mult).then_inc(y_scaled[1], 1)

        @block.tensor
        def _(t_e):
            t = t_e

            def slab(slot, f, x, start, stop, bank):
                wh, wl = (w[:, slot, :].rearrange("p (k n) -> p k n", k=4)[:, :, P * f:P * f + P] for w in (w_hi, w_lo))
                for n in range(4):
                    t.matmul(ps[:, bank, :], wh[:, n, :], x[n], start=start and n == 0, stop=False)
                    last = t.matmul(ps[:, bank, 0:SEQ], wl[:, n, :], x[n][:, 0:SEQ], start=False, stop=stop and n == 3)
                return last

            def quarter(b, i, f):
                if f % 2 == 0:
                    t.wait_ge(lo_split, 8 * b + 2 * i + f // 2 + 1)
                if i == 0 and not (isinstance(b, int) and b == 0):
                    t.wait_ge(evacuated, 4 * b + f - 3)
                slab(i % 2, f, [act[:, 4 * i + n, :] for n in range(4)], i == 0, i == 3, f).then_inc(slabs, 1)

            def unit(b, i):
                for f in range(4):
                    quarter(b, i, f)

            t.wait_ge(ident_loaded, 16)
            for n in range(TT):
                t.wait_ge(x_loaded[n], 16)
                for i in (6, 7, 0, 1, 2, 3, 4, 5) if n else range(8):
                    for k in range(2):
                        last = t.transpose(ps[:, i, SEQ * k + P * n:SEQ * k + P * n + P], xtok[:, n, P * (2 * i + k):P * (2 * i + k) + P],
                                           ident[:, :])
                    if n:
                        last.then_inc(x_turned, 1)
            t.wait_ge(norms_loaded, 16 * 5)
            t.wait_ge(x_copied_dve, 2)
            t.transpose(ps[:, 6, 0:57], staged[0:57, 0, :], ident[0:57, 0:57]).then_inc(par_turned, 1)
            t.wait_ge(ones_loaded, 16)
            for n in range(TT):
                t.wait_ge(x_diag, n + 1)
                last = t.matmul(ps[:, 7, P * n:P * n + P], ones[:, :], rdiag[:, n, :], start=True, stop=True)
            last.then_inc(rstd_rows, 1)
            t.wait_ge(x_copied_dve, 3)
            t.wait_ge(x_copied_act, 3)
            for i in range(4):
                t.wait_ge(act_lo, i + 1)
                unit(0, i)
                if i == 2:
                    t.wait_ge(par_loaded, 16 * 8)
                    at = CB
                    for tile, rows in ((1, 88), (2, 88), (3, 88), (4, 88), (5, 96)):
                        last = t.transpose(ps[:, 6, at:at + rows], staged[0:rows, tile, :], ident[0:rows, 0:rows])
                        at += rows
                    last.then_inc(par_turned, 1)
            t.wait_ge(normed, KD)
            t.wait_ge(x_copied_act, 5)
            for k in range(KD):
                last = t.matmul(ps[0:16, 4, 0:SEQ], w_log[:, k, :], h32[:, k, :], start=k == 0, stop=k == KD - 1)
            last.then_inc(logits, 1)
            unit(1, 0)
            t.wait_ge(logits_twice, 1)
            for c in range(CHUNKS):
                last = t.matmul(ps[:, 5, 16 * c:16 * c + 16], lgd[:, c].rearrange("p d n -> p (d n)"), ident[0:16, 0:16],
                                start=True, stop=True)
            last.then_inc(logits_turned, 1)
            for i in range(1, 4):
                unit(1, i)
            with t.Fori(2, 4) as b:
                for i in range(4):
                    unit(b, i)

            def turn_tokens(k):
                t.wait_ge(silu_done, 8 * k + 8)
                for p in range(PAIRS):
                    if k:
                        t.wait_ge(qk_sq, CHUNKS * p + CHUNKS)
                    for c in range(CHUNKS):
                        last = t.transpose(ps[:, 4 + p, P * c:P * c + P],
                                           by_problem[:, PAIRS * k + p, c].rearrange("p h n -> p (h n)"), ident[:, :])
                    last.then_inc(qk_turned, 1)

            for i in range(4):
                unit(4, i)
                if i == 1:
                    turn_tokens(0)
            t.wait_ge(qk_sq, J)
            t.wait_ge(log_decay, 1)
            t.wait_ge(cst_loaded, 16)
            t.matmul(ps[:, 5, 64:80], cst[:, C_TRI:C_TRI + P], g_g, start=True, stop=True)
            t.matmul(ps[:, 5, 80:96], cst[:, C_BLOCK:C_BLOCK + P], g_g, start=True, stop=True)
            for h in range(2):
                last = t.matmul(ps[:, 5, 96 + 16 * h:112 + 16 * h], cst[:, C_HALF + P * h:C_HALF + P * h + P], g_g, start=True, stop=True)
            last.then_inc(decay_sums, 1)
            for i in range(4):
                unit(5, i)
                if i == 1:
                    t.wait_ge(decay_summed, 1)
                    turn_tokens(1)

            def broadcast(out, lhsT, diag, p):
                return t.matmul(out, lhsT, diag[:, js(p), :].rearrange("p j n -> p (j n)"), start=True, stop=True)

            def pe_step(step, k):
                for p in range(PAIRS):
                    bank = 4 + p
                    n = PAIRS * k + p
                    if step == "decay_rows":
                        t.wait_ge(diag_ready, 2)
                        t.wait_ge(gates_ready, 1)
                        broadcast(ps[:, bank, 0:SEQ], cst[:, C_BLOCK:C_BLOCK + P], diag_g, p)
                        broadcast(ps[:, bank, SEQ:], cst[:, C_BLOCK:C_BLOCK + P], diag_b, p).then_inc(decay_rows, 1)
                    elif step == "q_row":
                        t.wait_ge(diag_ready, 4)
                        t.wait_ge(beta_decay, p + 1)
                        broadcast(ps[:, bank, 0:SEQ], cst[:, C_BLOCK:C_BLOCK + P], diag_q, p).then_inc(q_row, 1)
                    elif step == "kq":
                        t.wait_ge(silu_done, 16)
                        t.wait_ge(q_decay, p + 1)
                        for c in range(CHUNKS):
                            for h in range(2):
                                last = t.matmul(ps[HALF[h], bank, P * c:P * c + P].rearrange("p (a n) -> p a n", a=2),
                                                by_problem[:, PAIRS + p, c, h, :], by_problem[:, p:PAIRS + p + 1:PAIRS, c, h, :],
                                                start=True, stop=True)
                        last.then_inc(kq, 1)
                    elif step == "qg_rows":
                        t.wait_ge(diag_ready, 5)
                        t.wait_ge(qkt_ready, p + 1)
                        for h in range(2):
                            last = broadcast(ps[:, bank, SEQ * h:SEQ * h + SEQ], cst[:, C_HALF + P * h:C_HALF + P * h + P], diag_eq, p)
                        last.then_inc(qg_rows, 1)
                    elif step == "first":
                        t.wait_ge(tt_first, p + 1)
                        t.wait_ge(qg_ready, p + 1)
                        for c in range(CHUNKS):
                            last = t.transpose(ps[:, bank, P * c:P * c + P], TT_[:, CHUNKS * p + c, :], ident[:, :])
                        last.then_inc(t_turned, 1)
                    elif step in ("lx", "join", "turn"):
                        if step == "lx":
                            t.wait_ge(l_masked, n + 1)
                            t.wait_ge(tt_copied if k else t_first, n - PAIRS + 1 if k else p + 1)
                        elif step == "join":
                            t.wait_ge(lx_copied, n + 1)
                        else:
                            t.wait_ge(t_joined, n + 1)
                        for c in range(CHUNKS):
                            j = CHUNKS * p + c
                            o = ps[:, bank, P * c:P * c + P]
                            if step == "lx":
                                last = t.matmul(o, masked[:, j, :], Tm[:, j, :], start=True, stop=True)
                            elif step == "turn":
                                last = t.transpose(o, Tm[:, j, :], ident[:, :])
                            elif k < len(LEVELS) - 1:
                                last = t.matmul(o, TT_[:, j, :], X_[:, j, :], start=True, stop=True)
                            else:
                                last = t.matmul(o, X_[:, j, :], TT_[:, j, :], start=True, stop=True)
                        last.then_inc({"lx": lx, "join": tlt, "turn": t_back}[step], 1)
                    elif step in ("k_tok", "v_tok"):
                        if step == "k_tok":
                            t.wait_ge(t_joined, PAIRS * (len(LEVELS) - 1) + p + 1)
                        else:
                            t.wait_ge(k_decayed, p + 1)
                            t.wait_ge(silu_done, 24)
                        for c in range(CHUNKS):
                            tokens = by_problem[:, (PAIRS if step == "k_tok" else 2 * PAIRS) + p, c]
                            last = t.transpose(ps[:, bank, P * c:P * c + P], tokens.rearrange("p h n -> p (h n)"), ident[:, :])
                        last.then_inc(k_tok if step == "k_tok" else v_tok, 1)
                    elif step == "w":
                        t.wait_ge(v_scaled, p + 1)
                        for c in range(CHUNKS):
                            last = t.matmul(ps[:, bank, P * c:P * c + P], kg[:, CHUNKS * p + c, :], TT_[:, CHUNKS * p + c, :],
                                            start=True, stop=True)
                        last.then_inc(w_prod, 1)
                    elif step == "values":
                        j = CHUNKS * p + k
                        t.wait_ge(o_copied if k else w_copied, n - PAIRS + 1 if k else p + 1)
                        last = t.matmul(ps[:, bank, 0:P], TT_[:, j, :], vb[:, j, :], start=True, stop=k == 0)
                        if k:
                            t.wait_ge(s_ready, n - PAIRS + 1)
                            for h in range(2):
                                last = t.matmul(ps[HALF[h], bank, 0:P], W[:, j, h, :], S[:, 2 * p + h, :], start=False, stop=True)
                        last.then_inc(v_prod, 1)
                    elif step == "outputs":
                        j = CHUNKS * p + k
                        t.wait_ge(v_copied, n + 1)
                        for h in range(2):
                            o = ps[:, bank, P + 64 * h:P + 64 * h + 64]
                            if k:
                                t.matmul(o, S[:, 2 * p + h, :], by_problem[:, p, k, h, :], start=True, stop=False)
                            last = t.matmul(o, vnew[:, p, h, :], qkt[:, j, :], start=k == 0, stop=True)
                        if k < CHUNKS - 1:
                            last = t.matmul(ps[:, bank, 256:512], ktail[:, j, :], vnew[:, p, :, :].rearrange("p h n -> p (h n)"),
                                            start=True, stop=True)
                        last.then_inc(so_prod, 1)
                    elif step == "mixer":
                        t.wait_ge(pooled, p + 1)
                        t.wait_ge(pool_w_loaded, 16)
                        t.wait_ge(o_copied, PAIRS * (CHUNKS - 1) + p + 1)
                        for f in range(2):
                            for c in range(2):
                                last = t.matmul(ps[:, bank, SEQ * f:SEQ * f + SEQ], pw[:, p, c, P * f:P * f + P], uT[:, 2 * p + c, :],
                                                start=c == 0, stop=c == 1)
                        last.then_inc(pool_prod, 1)
                    elif step == "o_sums":
                        t.wait_ge(pool_out, 2 * p + 2)
                        for c in range(4):
                            last = t.transpose(ps[:, bank, P * c:P * c + P], oT[:, 2 * p + c // TT, P * (c % TT):P * (c % TT) + P],
                                               ident[:, :])
                        last.then_inc(o_turned, 1)
                    elif step == "o_rows":
                        t.wait_ge(o_diag, p + 1)
                        t.matmul(ps[:, bank, :], ones[:, :], diag_o[:, 4 * p:4 * p + 4, :].rearrange("p i n -> p (i n)"),
                                 start=True, stop=True).then_inc(o_row, 1)

            for q in range(QUARTERS):
                if q in SCHEDULE:
                    pe_step(*SCHEDULE[q])
                quarter(6 + q // 16, q // 4 % 4, q % 4)

            for i, (ready, n) in enumerate(((pool_lo, 1), (pool_lo, 2), (o_lo, 2), (o_lo, 4))):
                t.wait_ge(ready, n)
                unit(OUT_B, i)
            with t.Fori(OUT_B + 1, OUT_B + 4) as b:
                for i in range(4):
                    unit(b, i)

            for i in range(4):
                t.wait_ge(act_lo, 4 + i + 1)
                unit(UP_B, i)
                if i == 2:
                    t.wait_ge(summed, KD)
                    t.wait_ge(o_normed, PAIRS)
                    t.matmul(ps[:, 4, 0:SEQ], ones[:, :], sumsq[:, :], start=True, stop=True).then_inc(sums_ready, 1)
            with t.Fori(UP_B + 1, UP_B + 22) as b:
                for i in range(4):
                    unit(b, i)

            def down_unit(d, n, i=0):
                u = DOWN_U + DOWN_STEPS * d + n
                for f in range(4):
                    if f % 2 == 0:
                        t.wait_ge(lo_split, 2 * u + f // 2 + 1 + 4 * i)
                    if n == 0 and d:
                        t.wait_ge(evacuated, DOWN_T + 4 * (d - 2) + f + 1)
                    x = [fact[:, bass.ds(8 * i + 4 * n + k, 1), :].rearrange("p a n -> p (a n)") for k in range(4)]
                    slab(u % 2, f, x, n == 0, n == DOWN_STEPS - 1, pass_bank(d) + f).then_inc(slabs, 1)

            def turn(g):
                t.wait_ge(y_weighted, 4 * g + 4)
                for n in range(TT):
                    for k in range(4):
                        last = t.transpose(ps[:, pass_bank(g) + n, P * k:P * k + P], xT[:, 4 * g + k, P * n:P * n + P], ident[:, :])
                    last.then_inc(y_turned, 1)

            t.wait_ge(root_ready, 1)
            t.wait_ge(product_lo, KF - 4)
            for d in range(PASSES):
                if d >= 2:
                    t.wait_ge(y_kept[0], d - 1)
                    t.wait_ge(y_kept[1], d - 1)
                for n in range(3):
                    down_unit(d, n)
                with t.Fori(0, 3) as i:
                    down_unit(d, 3, i)
                    down_unit(d, 4, i)
                if d:
                    turn(d - 1)
                down_unit(d, 9)
                if d == 0:
                    t.wait_ge(product_lo, KF)
                down_unit(d, 10)
            t.wait_ge(summed, 2 * KD)
            for n in range(TT):
                last = t.matmul(ps[:, 6, n:n + 1], sumsq[:, P * n:P * n + P], ones[:, 0:1], start=True, stop=True)
            last.then_inc(sums_ready, 1)
            turn(3)


_INS = ["x", "norm1_w", "w_in", "conv_qkv_w", "a_log", "dt_bias", "out_norm_w", "pool_w", "pool_scale",
        "w_out", "norm2_w", "w_up", "conv_ffn_w", "conv_ffn_b", "w_down", "final_norm_w"]


def kernel(**inputs):
    import numpy as np
    import concourse.bacc as bacc
    from concourse.bass_utils import run_bass_kernel_spmd

    nc = bacc.Bacc("TRN2", target_bir_lowering=False, num_devices=1)
    arrays, args = {}, []
    for name in _INS:
        arrays[f"in_{name}"] = np.ascontiguousarray(inputs[name])
    arrays["in_table"] = constants()
    for name, a in arrays.items():
        args.append(nc.dram_tensor(name, a.shape, mybir.dt.from_np(a.dtype), kind="ExternalInput").ap())
    shape = arrays["in_x"].shape
    args.append(nc.dram_tensor("out_y", shape, F32, kind="ExternalOutput").ap())
    hybrid_layer(nc, *args)
    r = run_bass_kernel_spmd(nc, [arrays], core_ids=[0])
    return r.results[0]["out_y"]
```
